# Optimizing a Trainium2 kernel written in Bass

```python
import jax
import jax.numpy as jnp
from jax import lax
import numpy as np
import jax, jax.numpy as jnp

D_MODEL = 1024
BATCH = 1
SEQ = 512
DEPTH = 2

CTX_LEN = 256
GRID_W = 64
N_MOD = 6
RMS_EPS = 1e-6
NEG_INF = -1e30
D_POOL = D_MODEL // 2
POOL_WINDOWS = (2, 4, 8, 16)
D_POOL_GROUP = D_POOL // len(POOL_WINDOWS)
NA_HEAD_DIM = 64
D_NA = D_MODEL - D_POOL
NA_HEADS = D_NA // NA_HEAD_DIM
WIN_R = 8
WIN_C = 16
D_IN_EVEN = D_POOL + 3 * D_NA
RW_HEAD = 64
RW_HEADS = D_MODEL // RW_HEAD
DECAY_LORA = 64
AAA_LORA = 64
GATE_LORA = 128
GN_EPS = 64e-5
D_FF = 4 * D_MODEL


def rms_norm(x, g):
    xf = x.astype(jnp.float32)
    y = xf * lax.rsqrt(jnp.mean(xf * xf, axis=-1, keepdims=True) + RMS_EPS)
    return (y * g.astype(jnp.float32)).astype(x.dtype)

def modulate(h, shift, scale):
    return h * (1 + scale) + shift

def squared_relu_mlp(h, w1, w2):
    return jnp.square(jax.nn.relu(h @ w1)) @ w2

def split_heads(t, n_heads, head_dim):
    return t.reshape(t.shape[0], t.shape[1], n_heads, head_dim)

def pool_mixer(u, pool_w, pool_scale):
    L = u.shape[1]
    uf = u.astype(jnp.float32)
    cs = jnp.concatenate([jnp.zeros_like(uf[:, :1]), jnp.cumsum(uf, axis=1)], axis=1)
    t = jnp.arange(L)
    outs = []
    for gi, w in enumerate(POOL_WINDOWS):
        lo = jnp.clip(t - w // 2, 0, L)
        hi = jnp.clip(t + w // 2, 0, L)
        sl = slice(gi * D_POOL_GROUP, (gi + 1) * D_POOL_GROUP)
        csg = cs[..., sl]
        mean = (jnp.take(csg, hi, axis=1) - jnp.take(csg, lo, axis=1)) / (hi - lo).astype(jnp.float32)[None, :, None]
        outs.append((mean - uf[..., sl]).astype(u.dtype) @ pool_w[gi])
    return jnp.concatenate(outs, axis=-1) * pool_scale

def context_attention(q, k, v):
    B, L = q.shape[:2]
    s = jnp.einsum('bqhd,bkhd->bhqk', q, k).astype(jnp.float32) * (NA_HEAD_DIM ** -0.5)
    p = jax.nn.softmax(s, axis=-1).astype(v.dtype)
    return jnp.einsum('bhqk,bkhd->bqhd', p, v).reshape(B, L, D_NA)

def neighbourhood_attention(q, k, v, k_ctx, v_ctx, rpb):
    B, L = q.shape[:2]
    rows = L // GRID_W
    kr = min(WIN_R, rows)
    scale = NA_HEAD_DIM ** -0.5
    grid = lambda t: t.reshape(B, rows, GRID_W, NA_HEADS, NA_HEAD_DIM)
    qg, kg, vg = grid(q), grid(k), grid(v)
    col = jnp.arange(GRID_W)
    c_start = jnp.clip(col - WIN_C // 2, 0, GRID_W - WIN_C)
    col_ok = (col[None, :] >= c_start[:, None]) & (col[None, :] < c_start[:, None] + WIN_C)
    dc_idx = jnp.clip(col[None, :] - col[:, None], -(WIN_C - 1), WIN_C - 1) + WIN_C - 1
    rpb_c = rpb.astype(jnp.float32)[:, :, dc_idx]

    def row_block(args):
        q_row, r = args
        start = jnp.clip(r - kr // 2, 0, rows - kr)
        k_band = lax.dynamic_slice_in_dim(kg, start, kr, axis=1)
        v_band = lax.dynamic_slice_in_dim(vg, start, kr, axis=1)
        s_lat = jnp.einsum('bqhd,brkhd->bhqrk', q_row, k_band).astype(jnp.float32) * scale
        dr_idx = start + jnp.arange(kr) - r + WIN_R - 1
        bias = jnp.take(rpb_c, dr_idx, axis=1).transpose(0, 2, 1, 3)
        s_lat = jnp.where(col_ok[:, None, :], s_lat + bias, NEG_INF)
        s_ctx = jnp.einsum('bqhd,bchd->bhqc', q_row, k_ctx).astype(jnp.float32) * scale
        s = jnp.concatenate([s_lat.reshape(B, NA_HEADS, GRID_W, kr * GRID_W), s_ctx], axis=-1)
        p = jax.nn.softmax(s, axis=-1).astype(v.dtype)
        p_lat = p[..., :kr * GRID_W].reshape(B, NA_HEADS, GRID_W, kr, GRID_W)
        p_ctx = p[..., kr * GRID_W:]
        return (jnp.einsum('bhqrk,brkhd->bqhd', p_lat, v_band)
                + jnp.einsum('bhqc,bchd->bqhd', p_ctx, v_ctx))

    out = lax.map(row_block, (jnp.moveaxis(qg, 1, 0), jnp.arange(rows)))
    return jnp.moveaxis(out, 0, 1).reshape(B, L, D_NA)

def even_mixer(h, hc, w_in, w_out, pool_w, pool_scale, rpb, with_ctx):
    heads = lambda t: split_heads(t, NA_HEADS, NA_HEAD_DIM)
    u = h @ w_in
    q = heads(u[..., D_POOL:D_POOL + D_NA])
    k = heads(u[..., D_POOL + D_NA:D_POOL + 2 * D_NA])
    v = heads(u[..., D_POOL + 2 * D_NA:])
    if with_ctx:
        uc = hc @ w_in
        kv_c = uc[..., D_POOL + D_NA:]
    else:
        kv_c = hc @ w_in[:, D_POOL + D_NA:]
    k_c, v_c = heads(kv_c[..., :D_NA]), heads(kv_c[..., D_NA:])
    y = jnp.concatenate([pool_mixer(u[..., :D_POOL], pool_w, pool_scale),
                         neighbourhood_attention(q, k, v, k_c, v_c, rpb)], axis=-1) @ w_out
    if with_ctx:
        yc = jnp.concatenate([pool_mixer(uc[..., :D_POOL], pool_w, pool_scale),
                              context_attention(heads(uc[..., D_POOL:D_POOL + D_NA]), k_c, v_c)], axis=-1) @ w_out
    else:
        yc = None
    return y, yc

def centred_shift(x):
    prev = jnp.pad(x[:, :-1], ((0, 0), (1, 0), (0, 0)))
    nxt = jnp.pad(x[:, 1:], ((0, 0), (0, 1), (0, 0)))
    return 0.5 * (prev + nxt) - x

def rwkv_features(h, mu, wr, wk, wv, w0, w1, w2, a0, a1, a2, g1, g2, k_k, k_a, with_rg):
    B, L, _ = h.shape
    heads = lambda t: split_heads(t, RW_HEADS, RW_HEAD).astype(jnp.float32)
    xx = centred_shift(h)
    mix = lambda j: h + xx * mu[j]
    xw, xk, xv, xa = mix(1), mix(2), mix(3), mix(4)
    k = xk @ wk
    v = heads(xv @ wv)
    kk = heads(k * k_k)
    kk = kk * lax.rsqrt(jnp.maximum(jnp.sum(kk * kk, axis=-1, keepdims=True), 1e-24))
    kh = heads(k)
    k_a_h = k_a.reshape(RW_HEADS, RW_HEAD).astype(jnp.float32)
    dirs = []
    for d in range(2):
        w_raw = heads(w0[d] + jnp.tanh(xw @ w1[d]) @ w2[d])
        decay = jnp.exp(-jnp.exp(-jax.nn.softplus(-w_raw) - 0.5))
        a = jax.nn.sigmoid(heads(a0[d] + (xa @ a1[d]) @ a2[d]))
        k_d = kh * (1 + (a - 1) * k_a_h)
        dirs.append((decay, k_d, a))
    if with_rg:
        r = heads(mix(0) @ wr)
        g = jax.nn.sigmoid(mix(5) @ g1) @ g2
    else:
        r, g = None, None
    return v, kk, dirs, r, g

def wkv_scan(s0, decay, k, v, kk, a, r, reverse):
    tm = lambda t: jnp.moveaxis(t.astype(jnp.float32), 1, 0)
    emit = r is not None
    xs = (tm(decay), tm(k), tm(v), tm(kk), tm(kk * a)) + ((tm(r),) if emit else ())

    def step(S, inp):
        w_t, k_t, v_t, kk_t, kka_t = inp[:5]
        S = (S * w_t[:, :, None, :]
             - jnp.einsum('bhij,bhj->bhi', S, kk_t)[..., None] * kka_t[:, :, None, :]
             + v_t[..., None] * k_t[:, :, None, :])
        y = jnp.einsum('bhij,bhj->bhi', S, inp[5]) if emit else None
        return S, y

    S, ys = lax.scan(step, s0, xs, reverse=reverse)
    return S, (jnp.moveaxis(ys, 0, 1) if emit else None)

def rwkv_readout(y, r, k_sum, v, g, r_k, ln_g, ln_b, wo, dtype):
    B, L = y.shape[:2]
    mean = jnp.mean(y, axis=-1, keepdims=True)
    var = jnp.mean(jnp.square(y - mean), axis=-1, keepdims=True)
    yn = ((y - mean) * lax.rsqrt(var + GN_EPS)).reshape(B, L, D_MODEL) * ln_g + ln_b
    bonus = (jnp.sum(r * k_sum * r_k.astype(jnp.float32), axis=-1, keepdims=True) * v).reshape(B, L, D_MODEL)
    return ((yn + bonus) * g).astype(dtype) @ wo

def odd_mixer(h, hc, mu, wr, wk, wv, wo, w0, w1, w2, a0, a1, a2, g1, g2, k_k, k_a, r_k, ln_g, ln_b, with_ctx):
    feat = lambda t, rg: rwkv_features(t, mu, wr, wk, wv, w0, w1, w2, a0, a1, a2, g1, g2, k_k, k_a, rg)
    v, kk, dirs, r, g = feat(h, True)
    v_c, kk_c, dirs_c, r_c, g_c = feat(hc, with_ctx)
    s0 = jnp.zeros((h.shape[0], RW_HEADS, RW_HEAD, RW_HEAD), jnp.float32)
    ys, ys_c = [], []
    for d, reverse in enumerate((False, True)):
        decay_c, k_dc, a_c = dirs_c[d]
        s_ctx, y_c = wkv_scan(s0, decay_c, k_dc, v_c, kk_c, a_c, r_c, reverse)
        decay, k_d, a = dirs[d]
        _, y_d = wkv_scan(s_ctx, decay, k_d, v, kk, a, r, reverse)
        ys.append(y_d)
        ys_c.append(y_c)
    y = rwkv_readout(ys[0] + ys[1], r, dirs[0][1] + dirs[1][1], v, g, r_k, ln_g, ln_b, wo, h.dtype)
    if with_ctx:
        yc = rwkv_readout(ys_c[0] + ys_c[1], r_c, dirs_c[0][1] + dirs_c[1][1], v_c, g_c, r_k, ln_g, ln_b, wo, hc.dtype)
    else:
        yc = None
    return y, yc

def first_inputs(seed: int = 0) -> dict:
    key = jax.random.key(seed)
    ks = iter(jax.random.split(key, 40))
    n_even = (DEPTH + 1) // 2
    n_odd = DEPTH // 2
    D = D_MODEL
    nrm = lambda shape, s: jax.random.normal(next(ks), shape, jnp.float32) * s
    return {
        "x": nrm((BATCH, SEQ, D), 1.0),
        "c": nrm((BATCH, D), 1.0),
        "ctx": nrm((BATCH, CTX_LEN, D), 1.0),
        "c_ctx": nrm((D,), 1.0),
        "ada_w": nrm((DEPTH, D, N_MOD * D), 0.5 * D ** -0.5),
        "ada_b": nrm((DEPTH, N_MOD * D), 0.02),
        "norm_g": 1.0 + nrm((DEPTH, 4, D), 0.1),
        "mlp_w1": nrm((DEPTH, D, D_FF), D ** -0.5),
        "mlp_w2": nrm((DEPTH, D_FF, D), D_FF ** -0.5),
        "ev_w_in": nrm((n_even, D, D_IN_EVEN), D ** -0.5),
        "ev_w_out": nrm((n_even, D, D), D ** -0.5),
        "ev_pool_w": nrm((n_even, len(POOL_WINDOWS), D_POOL_GROUP, D_POOL_GROUP), D_POOL_GROUP ** -0.5),
        "ev_pool_scale": 1.0 + nrm((n_even, D_POOL), 0.1),
        "ev_rpb": nrm((n_even, NA_HEADS, 2 * WIN_R - 1, 2 * WIN_C - 1), 0.1),
        "rw_mu": jax.random.uniform(next(ks), (n_odd, 6, D), jnp.float32),
        "rw_wr": nrm((n_odd, D, D), D ** -0.5),
        "rw_wk": nrm((n_odd, D, D), D ** -0.5),
        "rw_wv": nrm((n_odd, D, D), D ** -0.5),
        "rw_wo": nrm((n_odd, D, D), D ** -0.5),
        "rw_w0": -2.0 + nrm((n_odd, 2, D), 0.5),
        "rw_w1": nrm((n_odd, 2, D, DECAY_LORA), D ** -0.5),
        "rw_w2": nrm((n_odd, 2, DECAY_LORA, D), 0.1 * DECAY_LORA ** -0.5),
        "rw_a0": nrm((n_odd, 2, D), 0.1),
        "rw_a1": nrm((n_odd, 2, D, AAA_LORA), D ** -0.5),
        "rw_a2": nrm((n_odd, 2, AAA_LORA, D), 0.1 * AAA_LORA ** -0.5),
        "rw_g1": nrm((n_odd, D, GATE_LORA), D ** -0.5),
        "rw_g2": nrm((n_odd, GATE_LORA, D), GATE_LORA ** -0.5),
        "rw_kk": 0.85 + nrm((n_odd, D), 0.05),
        "rw_ka": 1.0 + nrm((n_odd, D), 0.05),
        "rw_rk": nrm((n_odd, RW_HEADS, RW_HEAD), 0.1),
        "rw_lng": 1.0 + nrm((n_odd, D), 0.1),
        "rw_lnb": nrm((n_odd, D), 0.01),
    }

def first_block(x, c, ctx, c_ctx, ada_w, ada_b, norm_g, mlp_w1, mlp_w2,
              ev_w_in, ev_w_out, ev_pool_w, ev_pool_scale, ev_rpb,
              rw_mu, rw_wr, rw_wk, rw_wv, rw_wo, rw_w0, rw_w1, rw_w2,
              rw_a0, rw_a1, rw_a2, rw_g1, rw_g2, rw_kk, rw_ka, rw_rk, rw_lng, rw_lnb):
    silu_c = jax.nn.silu(c)
    silu_cc = jax.nn.silu(c_ctx)
    for i in range(DEPTH):
        j = i // 2
        with_ctx = i < DEPTH - 1
        mod = (silu_c @ ada_w[i] + ada_b[i])[:, None, :]
        mod_c = silu_cc @ ada_w[i] + ada_b[i]
        sh1, sc1, gt1, sh2, sc2, gt2 = jnp.split(mod, N_MOD, axis=-1)
        sh1c, sc1c, gt1c, sh2c, sc2c, gt2c = jnp.split(mod_c, N_MOD, axis=-1)
        h = modulate(rms_norm(x, norm_g[i, 0]), sh1, sc1)
        hc = modulate(rms_norm(ctx, norm_g[i, 0]), sh1c, sc1c)
        if i % 2 == 0:
            y, yc = even_mixer(h, hc, ev_w_in[j], ev_w_out[j], ev_pool_w[j], ev_pool_scale[j], ev_rpb[j], with_ctx)
        else:
            y, yc = odd_mixer(h, hc, rw_mu[j], rw_wr[j], rw_wk[j], rw_wv[j], rw_wo[j],
                              rw_w0[j], rw_w1[j], rw_w2[j], rw_a0[j], rw_a1[j], rw_a2[j],
                              rw_g1[j], rw_g2[j], rw_kk[j], rw_ka[j], rw_rk[j], rw_lng[j], rw_lnb[j], with_ctx)
        x = x + gt1 * rms_norm(y, norm_g[i, 1])
        h = modulate(rms_norm(x, norm_g[i, 2]), sh2, sc2)
        x = x + gt2 * rms_norm(squared_relu_mlp(h, mlp_w1[i], mlp_w2[i]), norm_g[i, 3])
        if with_ctx:
            ctx = ctx + gt1c * rms_norm(yc, norm_g[i, 1])
            hc = modulate(rms_norm(ctx, norm_g[i, 2]), sh2c, sc2c)
            ctx = ctx + gt2c * rms_norm(squared_relu_mlp(hc, mlp_w1[i], mlp_w2[i]), norm_g[i, 3])
    return x


DEPTH_2 = 1

MLA_HEADS = 8
MLA_NOPE = 64
MLA_ROPE = 32
MLA_V = 64
MLA_Q_LORA = 512
MLA_KV_LORA = 256
DIL_HEADS = 8
DIL_HEAD_DIM = 64
DIL_PATTERNS = ((128, 1), (512, 4), (2048, 16))
DIL_WIDTH = DIL_HEADS * DIL_HEAD_DIM
MIX_WIDTH = MLA_HEADS * MLA_V + DIL_WIDTH
IN_COLS = MLA_Q_LORA + MLA_KV_LORA + MLA_ROPE + 3 * DIL_WIDTH
SPLITS = (MLA_Q_LORA,
          MLA_Q_LORA + MLA_KV_LORA,
          MLA_Q_LORA + MLA_KV_LORA + MLA_ROPE,
          MLA_Q_LORA + MLA_KV_LORA + MLA_ROPE + DIL_WIDTH,
          MLA_Q_LORA + MLA_KV_LORA + MLA_ROPE + 2 * DIL_WIDTH)
D_FF_2 = 2816
CONV_WIDTH = 3
ROPE_THETA = 10000.0
EPS = 1e-6
Q_BLOCK = 128
NEG_INF_2 = -1e30


def rms_norm_2(x, g):
    xf = x.astype(jnp.float32)
    y = xf * lax.rsqrt(jnp.mean(xf * xf, axis=-1, keepdims=True) + EPS)
    return (y * g.astype(jnp.float32)).astype(x.dtype)

def rope(x, positions):
    d = x.shape[-1]
    half = d // 2
    inv_freq = jnp.power(ROPE_THETA, -2.0 * jnp.arange(half, dtype=jnp.float32) / d)
    ang = positions.astype(jnp.float32)[:, :, None, None] * inv_freq
    cos, sin = jnp.cos(ang), jnp.sin(ang)
    xf = x.astype(jnp.float32)
    x1, x2 = xf[..., :half], xf[..., half:]
    return jnp.concatenate([x1 * cos - x2 * sin, x1 * sin + x2 * cos], axis=-1).astype(x.dtype)

def causal_dense_attention(q, k, v, scale):
    B, S, H, Dk = q.shape
    Dv = v.shape[-1]
    nb = S // Q_BLOCK
    qb = q.reshape(B, nb, Q_BLOCK, H, Dk).transpose(1, 0, 2, 3, 4)
    kpos = jnp.arange(S)

    def one_block(args):
        qi, i = args
        s = jnp.einsum('bqhd,bkhd->bhqk', qi, k).astype(jnp.float32) * scale
        qpos = i * Q_BLOCK + jnp.arange(Q_BLOCK)
        mask = kpos[None, :] <= qpos[:, None]
        s = jnp.where(mask, s, NEG_INF_2)
        p = jax.nn.softmax(s, axis=-1).astype(v.dtype)
        return jnp.einsum('bhqk,bkhd->bqhd', p, v)

    out = lax.map(one_block, (qb, jnp.arange(nb)))
    return out.transpose(1, 0, 2, 3, 4).reshape(B, S, H, Dv)

def banded_causal_attention(q, k, v, span):
    N, L, H, D = q.shape
    blk = span
    nb = -(-L // blk)
    Lp = nb * blk
    pad = ((0, 0), (0, Lp - L), (0, 0), (0, 0))
    q, k, v = jnp.pad(q, pad), jnp.pad(k, pad), jnp.pad(v, pad)
    qb = q.reshape(N, nb, blk, H, D)

    def two_blocks(t):
        tb = jnp.pad(t, ((0, 0), (blk, 0), (0, 0), (0, 0))).reshape(N, nb + 1, blk, H, D)
        return jnp.concatenate([tb[:, :-1], tb[:, 1:]], axis=2)

    kb, vb = two_blocks(k), two_blocks(v)
    s = jnp.einsum('nbqhd,nbkhd->nbhqk', qb, kb).astype(jnp.float32) * (D ** -0.5)
    blk_idx = jnp.arange(nb)[:, None, None]
    qry_pos = blk_idx * blk + jnp.arange(blk)[None, :, None]
    key_pos = (blk_idx - 1) * blk + jnp.arange(2 * blk)[None, None, :]
    dist = qry_pos - key_pos
    mask = (dist >= 0) & (dist <= span) & (key_pos >= 0)
    s = jnp.where(mask[None, :, None], s, NEG_INF_2)
    m = jnp.max(s, axis=-1, keepdims=True)
    e = jnp.exp(s - m)
    denom = jnp.sum(e, axis=-1, keepdims=True)
    p = (e / denom).astype(v.dtype)
    o = jnp.einsum('nbhqk,nbkhd->nbqhd', p, vb).reshape(N, Lp, H, D)[:, :L]
    lse = (m + jnp.log(denom))[..., 0]
    lse = lse.transpose(0, 1, 3, 2).reshape(N, Lp, H)[:, :L]
    return o, lse

def to_strided(t, dil):
    B, S, H, D = t.shape
    return t.reshape(B, S // dil, dil, H, D).transpose(0, 2, 1, 3, 4).reshape(B * dil, S // dil, H, D)

def dilated_attention(q, k, v):
    B, S, H, D = q.shape
    outs, lses = [], []
    for window, dil in DIL_PATTERNS:
        L = S // dil
        o, lse = banded_causal_attention(to_strided(q, dil), to_strided(k, dil),
                                         to_strided(v, dil), window // dil)
        outs.append(o.reshape(B, dil, L, H, D).transpose(0, 2, 1, 3, 4).reshape(B, S, H, D))
        lses.append(lse.reshape(B, dil, L, H).transpose(0, 2, 1, 3).reshape(B, S, H))
    w = jax.nn.softmax(jnp.stack(lses, axis=0), axis=0)
    out = jnp.sum(w[..., None] * jnp.stack(outs, axis=0).astype(jnp.float32), axis=0)
    return out.astype(q.dtype)

def causal_depthwise_conv(u, w, b):
    K = w.shape[0]
    S = u.shape[1]
    up = jnp.pad(u, ((0, 0), (K - 1, 0), (0, 0)))
    y = b
    for kk in range(K):
        y = y + up[:, kk:kk + S] * w[kk]
    return y

def second_inputs(seed: int = 0) -> dict:
    key = jax.random.key(seed)
    ks = jax.random.split(key, 24)
    nrm = jax.random.normal
    L = DEPTH_2

    def gain(k, n):
        return 1.0 + 0.05 * nrm(k, (L, n), jnp.float32)

    x = nrm(ks[0], (BATCH, SEQ, D_MODEL), jnp.float32)
    c = nrm(ks[1], (BATCH, D_MODEL), jnp.float32)
    positions = (jnp.arange(SEQ, dtype=jnp.int32)[None, :]
                 + jax.random.randint(ks[2], (BATCH, 1), 0, 4096, dtype=jnp.int32))
    return {
        "x": x,
        "c": c,
        "positions": positions,
        "w_ada": nrm(ks[3], (L, D_MODEL, 6 * D_MODEL), jnp.float32) * (0.5 * D_MODEL ** -0.5),
        "b_ada": 0.02 * nrm(ks[4], (L, 6 * D_MODEL), jnp.float32),
        "g_mix_norm": gain(ks[5], D_MODEL),
        "w_in": nrm(ks[6], (L, D_MODEL, IN_COLS), jnp.float32) * D_MODEL ** -0.5,
        "g_q_lat": gain(ks[7], MLA_Q_LORA),
        "w_q_b": nrm(ks[8], (L, MLA_Q_LORA, MLA_HEADS * (MLA_NOPE + MLA_ROPE)), jnp.float32) * MLA_Q_LORA ** -0.5,
        "g_kv_lat": gain(ks[9], MLA_KV_LORA),
        "w_kv_b": nrm(ks[10], (L, MLA_KV_LORA, MLA_HEADS * (MLA_NOPE + MLA_V)), jnp.float32) * MLA_KV_LORA ** -0.5,
        "g_mla_q_nope": gain(ks[11], MLA_NOPE),
        "g_mla_q_pe": gain(ks[12], MLA_ROPE),
        "g_mla_k_nope": gain(ks[13], MLA_NOPE),
        "g_mla_k_pe": gain(ks[14], MLA_ROPE),
        "g_dil_q": gain(ks[15], DIL_HEAD_DIM),
        "g_dil_k": gain(ks[16], DIL_HEAD_DIM),
        "w_o": nrm(ks[17], (L, MIX_WIDTH, D_MODEL), jnp.float32) * MIX_WIDTH ** -0.5,
        "g_ffn_norm": gain(ks[18], D_MODEL),
        "w_up": nrm(ks[19], (L, D_MODEL, 2 * D_FF_2), jnp.float32) * D_MODEL ** -0.5,
        "w_conv": nrm(ks[20], (L, CONV_WIDTH, 2 * D_FF_2), jnp.float32) * CONV_WIDTH ** -0.5,
        "b_conv": 0.02 * nrm(ks[21], (L, 2 * D_FF_2), jnp.float32),
        "w_down": nrm(ks[22], (L, D_FF_2, D_MODEL), jnp.float32) * D_FF_2 ** -0.5,
    }

def second_block(x, c, positions, w_ada, b_ada, g_mix_norm, w_in, g_q_lat, w_q_b, g_kv_lat, w_kv_b,
              g_mla_q_nope, g_mla_q_pe, g_mla_k_nope, g_mla_k_pe, g_dil_q, g_dil_k, w_o,
              g_ffn_norm, w_up, w_conv, b_conv, w_down):
    B, S, _ = x.shape
    for l in range(DEPTH_2):
        mod = jax.nn.silu(c) @ w_ada[l] + b_ada[l]
        sh1, sc1, g1, sh2, sc2, g2 = jnp.split(mod, 6, axis=-1)

        h = rms_norm_2(x, g_mix_norm[l]) * (1.0 + sc1[:, None]) + sh1[:, None]
        proj = h @ w_in[l]
        q_lat, kv_lat, k_pe, qd, kd, vd = jnp.split(proj, SPLITS, axis=-1)

        q = (rms_norm_2(q_lat, g_q_lat[l]) @ w_q_b[l]).reshape(B, S, MLA_HEADS, MLA_NOPE + MLA_ROPE)
        q_nope = rms_norm_2(q[..., :MLA_NOPE], g_mla_q_nope[l])
        q_pe = rope(rms_norm_2(q[..., MLA_NOPE:], g_mla_q_pe[l]), positions)
        kv = (rms_norm_2(kv_lat, g_kv_lat[l]) @ w_kv_b[l]).reshape(B, S, MLA_HEADS, MLA_NOPE + MLA_V)
        k_nope = rms_norm_2(kv[..., :MLA_NOPE], g_mla_k_nope[l])
        v_mla = kv[..., MLA_NOPE:]
        k_pe = rope(rms_norm_2(k_pe, g_mla_k_pe[l])[:, :, None, :], positions)
        k_mla = jnp.concatenate([k_nope, jnp.broadcast_to(k_pe, (B, S, MLA_HEADS, MLA_ROPE))], axis=-1)
        q_mla = jnp.concatenate([q_nope, q_pe], axis=-1)
        o_mla = causal_dense_attention(q_mla, k_mla, v_mla, (MLA_NOPE + MLA_ROPE) ** -0.5)

        qd = rope(rms_norm_2(qd.reshape(B, S, DIL_HEADS, DIL_HEAD_DIM), g_dil_q[l]), positions)
        kd = rope(rms_norm_2(kd.reshape(B, S, DIL_HEADS, DIL_HEAD_DIM), g_dil_k[l]), positions)
        vd = vd.reshape(B, S, DIL_HEADS, DIL_HEAD_DIM)
        o_dil = dilated_attention(qd, kd, vd)

        mix = jnp.concatenate([o_mla.reshape(B, S, MLA_HEADS * MLA_V),
                               o_dil.reshape(B, S, DIL_WIDTH)], axis=-1) @ w_o[l]
        x = x + g1[:, None] * mix

        h2 = rms_norm_2(x, g_ffn_norm[l]) * (1.0 + sc2[:, None]) + sh2[:, None]
        u = causal_depthwise_conv(h2 @ w_up[l], w_conv[l], b_conv[l])
        gate, val = jnp.split(u, 2, axis=-1)
        x = x + g2[:, None] * ((jax.nn.silu(gate) * val) @ w_down[l])
    return x


def setup_inputs(seed=0):
    out = dict(first_inputs(seed))
    for name, value in second_inputs(seed + 1).items():
        if name != "x":
            out[name + "_2"] = value
    return out


def reference(
    x, c, ctx, c_ctx, ada_w, ada_b, norm_g, mlp_w1, mlp_w2, ev_w_in, ev_w_out, ev_pool_w,
    ev_pool_scale, ev_rpb, rw_mu, rw_wr, rw_wk, rw_wv, rw_wo, rw_w0, rw_w1, rw_w2, rw_a0, rw_a1,
    rw_a2, rw_g1, rw_g2, rw_kk, rw_ka, rw_rk, rw_lng, rw_lnb, c_2, positions_2, w_ada_2,
    b_ada_2, g_mix_norm_2, w_in_2, g_q_lat_2, w_q_b_2, g_kv_lat_2, w_kv_b_2, g_mla_q_nope_2,
    g_mla_q_pe_2, g_mla_k_nope_2, g_mla_k_pe_2, g_dil_q_2, g_dil_k_2, w_o_2, g_ffn_norm_2,
    w_up_2, w_conv_2, b_conv_2, w_down_2,
):
    x = first_block(
        x, c, ctx, c_ctx, ada_w, ada_b, norm_g, mlp_w1, mlp_w2, ev_w_in, ev_w_out, ev_pool_w,
        ev_pool_scale, ev_rpb, rw_mu, rw_wr, rw_wk, rw_wv, rw_wo, rw_w0, rw_w1, rw_w2, rw_a0,
        rw_a1, rw_a2, rw_g1, rw_g2, rw_kk, rw_ka, rw_rk, rw_lng, rw_lnb,
    )
    return second_block(
        x, c_2, positions_2, w_ada_2, b_ada_2, g_mix_norm_2, w_in_2, g_q_lat_2, w_q_b_2,
        g_kv_lat_2, w_kv_b_2, g_mla_q_nope_2, g_mla_q_pe_2, g_mla_k_nope_2, g_mla_k_pe_2,
        g_dil_q_2, g_dil_k_2, w_o_2, g_ffn_norm_2, w_up_2, w_conv_2, b_conv_2, w_down_2,
    )


_drawn_inputs = setup_inputs


def setup_inputs(seed=0):
    import zlib

    import numpy as np

    out = dict(_drawn_inputs(seed))
    spreads = {}
    factors = {'ev_rpb': 8.0,
     'rw_w1': 8.0,
     'rw_w2': 8.0,
     'rw_a0': 4.463,
     'rw_a1': 5.624,
     'rw_a2': 5.61,
     'rw_kk': 3.672,
     'rw_lnb': 8.0,
     'b_ada_2': 3.474,
     'g_mix_norm_2': 8.0,
     'g_q_lat_2': 8.0,
     'g_kv_lat_2': 8.0,
     'g_mla_q_nope_2': 8.0,
     'g_mla_q_pe_2': 8.0,
     'g_mla_k_nope_2': 8.0,
     'g_mla_k_pe_2': 8.0,
     'g_dil_q_2': 8.0,
     'g_dil_k_2': 8.0,
     'g_ffn_norm_2': 4.488,
     'b_conv_2': 8.0}
    for name, (base, spread) in spreads.items():
        noise = np.random.default_rng([zlib.crc32(name.encode()), seed]).standard_normal(out[name].shape)
        drawn = base * np.exp(spread * noise) if base else spread * noise
        out[name] = jnp.asarray(drawn.astype(out[name].dtype))
    for name, factor in factors.items():
        out[name] = (out[name] * factor).astype(out[name].dtype)
    return out
```

```python
from contextlib import ExitStack

import numpy as np

import concourse.bass as bass
from concourse import mybir

F32 = mybir.dt.float32
I32 = mybir.dt.int32
ALU = mybir.AluOpType
ACT = mybir.ActivationFunctionType
AX = mybir.AxisListType

P = 128
D = 1024
SEQ = 512
CTX = 256
T0 = SEQ + CTX
DT = D // P
N_MOD = 6
EPS = 1e-6
CREDIT = 16

POOL_WINDOWS = (2, 4, 8, 16)
D_FF = 4 * D
HEAD = 64
GRID_W = 64
WIN_R, WIN_C = 8, 16
ROWS = SEQ // GRID_W
NEG = -1e30

D_FF2 = 2816
FT2 = D_FF2 // P
MLA_HEADS, MLA_NOPE, MLA_ROPE = 8, 64, 32
MLA_QK = MLA_NOPE + MLA_ROPE
Q_LORA, KV_LORA = 512, 256
DIL_PATTERNS = ((128, 1), (512, 4), (2048, 16))
ROPE_THETA = 10000.0

RW_HEADS = D // HEAD
GN_EPS = 64e-5
CHUNK = 64
DECAY_SCALE = float(np.exp(-0.5))


class Signal:

    def __init__(self, nc, name):
        self.sem = nc.alloc_semaphore(name)
        self.base = 0


class Core:

    def __init__(self, nc):
        self.nc = nc
        self.counters = {}
        self.stages = 0
        self.psum = nc.alloc_psum_tensor("psum", [P, 8, 512], F32)

    def block(self):
        self.stages += 1
        return self.nc.Block(no_gpsimd_drain=True)

    def sb(self, scope, name, shape, dtype=F32):
        self.stages += 1
        return scope.enter_context(self.nc.sbuf_tensor(f"{name}_{self.stages}", shape, dtype))


def counter(core, name):
    if name not in core.counters:
        core.counters[name] = Signal(core.nc, name)
    return core.counters[name]


class Chain:

    def __init__(self, eng, signal, start):
        self.eng, self.counter, self.start, self.steps = eng, signal, start, 0

    def __call__(self, instruction):
        self.steps += 1
        instruction.then_inc(self.counter.sem, 1)
        self.eng.wait_ge(self.counter.sem, self.start + self.steps)


def tile(ap, n):
    if isinstance(n, int):
        return ap[:, n, :]
    return ap[:, bass.ds(n, 1), :].rearrange("p a t -> p (a t)")


def col(ap, n):
    return ap[:, n:n + 1] if isinstance(n, int) else ap[:, bass.ds(n, 1)]


def halves(ap):
    return ap.rearrange("p (a t) -> p a t", a=2)



def gemm(core, weights, kt, nt, act, tokens, act_evict=None, dve_evict=None, m=P, m0=0, kp=P, k0=0,
         dve_steps=0, ring=4, bufs=4):
    nc = core.nc
    wide = tokens > 512
    landed = [counter(core, f"panel_landed_{s}") for s in range(4)]
    done, evicted, first = counter(core, "panel_done"), counter(core, "panel_evicted"), counter(core, "panel_first_evict")
    steps = counter(core, "gemm_vector_step")
    looped = nt % 4 == 0 and nt > 4
    landed_base = [s.base for s in landed]

    def place(n):
        s = n % bufs
        if wide:
            return core.psum[m0:m0 + m, 2 * s:2 * s + 2, 0:tokens // 2]
        return core.psum[m0:m0 + m, s, 0:tokens]

    def panels(eng):
        if looped:
            with eng.Fori(0, nt // 4) as blk:
                for u in range(4):
                    yield blk * 4 + u, u, blk * (4 // ring) + u // ring
        else:
            for n in range(nt):
                yield n, n, n // ring

    with ExitStack() as scope:
        panel = core.sb(scope, "panels", [P, ring, kt * m])
        with core.block() as block:
            @block.sync
            def _(sp):
                for n, u, turn in panels(sp):
                    sp.wait_ge(done.sem, done.base + n + 1 - ring)
                    src = weights[n, :, :] if isinstance(n, int) else \
                        weights[bass.ds(n, 1), :, :].rearrange("a p k -> p (a k)")
                    sp.dma_start(panel[k0:k0 + kp, u % ring, :], src).then_inc(landed[u % ring].sem, 16)

            @block.tensor
            def _(pe):
                for n, u, turn in panels(pe):
                    pe.wait_ge(landed[u % ring].sem, landed_base[u % ring] + 16 * (turn + 1))
                    pe.wait_ge(evicted.sem, evicted.base + n + 1 - bufs)
                    out = place(u)
                    for k in range(kt):
                        w = panel[k0:k0 + kp, u % ring, k * m:(k + 1) * m]
                        if wide:
                            for a in range(2):
                                last = nc.tensor.matmul(out[:, a, :], w, act[:, k, a * tokens // 2:(a + 1) * tokens // 2],
                                                        start=k == 0, stop=k == kt - 1)
                        else:
                            last = nc.tensor.matmul(out, w, act[:, k, :], start=k == 0, stop=k == kt - 1)
                    last.then_inc(done.sem, 1)

            if act_evict is not None:
                @block.scalar
                def _(eng):
                    for n, u, turn in panels(eng):
                        eng.wait_ge(done.sem, done.base + n + 1)
                        act_evict(n, place(u)).then_inc(first.sem if dve_evict else evicted.sem, 1)

            if dve_evict is not None:
                @block.vector
                def _(dve):
                    for n, u, turn in panels(dve):
                        if act_evict is not None:
                            dve.wait_ge(first.sem, first.base + n + 1)
                        else:
                            dve.wait_ge(done.sem, done.base + n + 1)
                        chain = Chain(dve, steps, steps.base + n * dve_steps)
                        dve_evict(n, place(u), chain).then_inc(evicted.sem, 1)
                        assert chain.steps == dve_steps

    for s in range(ring):
        landed[s].base += 16 * len(range(s, nt, ring))
    done.base += nt
    evicted.base += nt
    if act_evict is not None and dve_evict is not None:
        first.base += nt
    steps.base += nt * dve_steps


def gemm_tokens(core, weights, kt, act, tiles, dst):
    nc = core.nc
    landed, done, out = counter(core, "value_weights_landed"), counter(core, "panel_done"), counter(core, "panel_evicted")
    with ExitStack() as scope:
        w = core.sb(scope, "value_weights", [P, kt * 512])
        with core.block() as block:
            @block.sync
            def _(sp):
                sp.dma_start(w[:, :], weights).then_inc(landed.sem, 16)

            @block.tensor
            def _(pe):
                pe.wait_ge(landed.sem, landed.base + 16)
                for t in range(tiles):
                    pe.wait_ge(out.sem, out.base + t + 1 - 8)
                    for k in range(kt):
                        last = nc.tensor.matmul(core.psum[:, t % 8, :], act[:, k, t * P:(t + 1) * P],
                                                w[:, k * 512:(k + 1) * 512], start=k == 0, stop=k == kt - 1)
                    last.then_inc(done.sem, 1)

            @block.scalar
            def _(eng):
                for t in range(tiles):
                    eng.wait_ge(done.sem, done.base + t + 1)
                    nc.scalar.activation(dst[:, t, :], core.psum[:, t % 8, :], ACT.Copy).then_inc(out.sem, 1)
    landed.base += 16
    done.base += tiles
    out.base += tiles



def rms_stage(core, src, kt, tokens, scales, shifts=None, dst=None, residual=None, eps=EPS):
    nc = core.nc
    squared, summed = counter(core, "norm_squared"), counter(core, "norm_summed")
    inverted, rooted = counter(core, "norm_inverted"), counter(core, "norm_rooted")
    scaled, finished = counter(core, "norm_scaled"), counter(core, "norm_finished")
    steps = counter(core, "norm_vector_step")
    nb = 2 if tokens > 512 else 1
    width = tokens // nb
    with ExitStack() as scope:
        sq = core.sb(scope, "norm_sq", [P, 2, tokens])
        var = core.sb(scope, "norm_var", [P, tokens])
        inv = core.sb(scope, "norm_inv", [P, tokens])
        rstd = core.sb(scope, "norm_rstd", [P, tokens])
        tmp = core.sb(scope, "norm_tmp", [P, 2, tokens])
        total = core.psum[:, 0:nb, 0:width]

        def by_bank(ap):
            return ap.rearrange("p (a t) -> p a t", a=nb)

        with core.block() as block:
            @block.scalar
            def _(eng):
                for k in range(kt):
                    if k >= 2:
                        eng.wait_ge(summed.sem, summed.base + k - 1)
                    nc.scalar.activation(sq[:, k % 2, :], src[:, k, 0:tokens], ACT.Square).then_inc(squared.sem, 1)
                eng.wait_ge(inverted.sem, inverted.base + 1)
                nc.scalar.activation(rstd[:, :], inv[:, :], ACT.Sqrt).then_inc(rooted.sem, 1)
                if shifts is not None:
                    for k in range(kt):
                        eng.wait_ge(scaled.sem, scaled.base + k + 1)
                        for t0, t1, c in shifts:
                            last = nc.scalar.activation(dst[:, k, t0:t1], tmp[:, k % 2, t0:t1], ACT.Identity,
                                                        bias=col(c, k))
                        last.then_inc(finished.sem, 1)

            @block.tensor
            def _(pe):
                for k in range(kt):
                    pe.wait_ge(squared.sem, squared.base + k + 1)
                    for a in range(nb):
                        last = nc.tensor.matmul(total[:, a, :], core.ones[:, :], sq[:, k % 2, a * width:(a + 1) * width],
                                                start=k == 0, stop=k == kt - 1)
                    last.then_inc(summed.sem, 1)

            @block.vector
            def _(dve):
                chain = Chain(dve, steps, steps.base)
                dve.wait_ge(summed.sem, summed.base + kt)
                chain(nc.vector.tensor_scalar(by_bank(var[:, :]), total, 1.0 / (kt * P), eps, ALU.mult, ALU.add))
                nc.vector.reciprocal(inv[:, :], var[:, :]).then_inc(inverted.sem, 1)
                dve.wait_ge(rooted.sem, rooted.base + 1)
                for k in range(kt):
                    if k >= 2 and (shifts is not None or residual is not None):
                        dve.wait_ge(finished.sem, finished.base + k - 1)
                    for t0, t1, c in scales:
                        o = dst[:, k, t0:t1] if shifts is None and residual is None else tmp[:, k % 2, t0:t1]
                        last = nc.vector.scalar_tensor_tensor(o, src[:, k, t0:t1], col(c, k), rstd[:, t0:t1],
                                                              ALU.mult, ALU.mult)
                    last.then_inc(scaled.sem, 1)

            if residual is not None:
                @block.gpsimd
                def _(pool):
                    for k in range(kt):
                        pool.wait_ge(scaled.sem, scaled.base + k + 1)
                        nc.gpsimd.tensor_tensor(residual[:, k, 0:tokens], residual[:, k, 0:tokens], tmp[:, k % 2, :],
                                                ALU.add).then_inc(finished.sem, 1)
                    pool.wait_ge(finished.sem, finished.base + kt)
    squared.base += kt
    summed.base += kt
    inverted.base += 1
    rooted.base += 1
    steps.base += 1
    scaled.base += kt
    if shifts is not None or residual is not None:
        finished.base += kt



def modulation(core, weights, biases, vectors, mods):
    nc = core.nc
    nt, ring = N_MOD * DT, 4
    landed = [counter(core, f"panel_landed_{s}") for s in range(4)]
    used, steps = counter(core, "mod_panel_used"), counter(core, "mod_vector_step")
    nv = len(vectors)
    per = (nv - 1) * ring + nv
    with ExitStack() as scope:
        w = core.sb(scope, "mod_weights", [P, ring, D])
        junk = core.sb(scope, "mod_products", [P, D])
        part = core.sb(scope, "mod_part", [P, nv, ring])
        with core.block() as block:
            @block.sync
            def _(sp):
                with sp.Fori(0, nt // ring) as blk:
                    for u in range(ring):
                        sp.wait_ge(used.sem, used.base + blk * ring + u + 1 - ring)
                        sp.dma_start(w[:, u, :], weights[bass.ds(blk * ring + u, 1), :, :].rearrange("a p k -> p (a k)"))\
                            .then_inc(landed[u].sem, 16)

            @block.vector
            def _(dve):
                with dve.Fori(0, nt // ring) as blk:
                    chain = Chain(dve, steps, steps.base + blk * per)
                    for u in range(ring):
                        dve.wait_ge(landed[u].sem, landed[u].base + 16 * (blk + 1))
                        for v in range(nv):
                            ins = nc.vector.tensor_tensor_reduce(
                                out=junk[:, :], in0=w[:, u, :], in1=vectors[v], scale=1.0, scalar=0.0,
                                op0=ALU.mult, op1=ALU.add, accum_out=part[:, v, u:u + 1])
                            if v == nv - 1:
                                ins.then_inc(used.sem, 1)
                                dve.wait_ge(used.sem, used.base + blk * ring + u + 1)
                            else:
                                chain(ins)
                    for v in range(nv):
                        chain(nc.vector.tensor_tensor(mods[v][:, bass.ds(blk * ring, ring)], part[:, v, :],
                                                      biases[:, bass.ds(blk * ring, ring)], ALU.add))
                    assert chain.steps == per
    for s in range(ring):
        landed[s].base += 16 * (nt // ring)
    used.base += nt
    steps.base += per * (nt // ring)



def pool_mixer(core, u, pool_weights, inv_count, scale_cols, dst):
    nc = core.nc
    pad = POOL_WINDOWS[-1] // 2
    x0, c0 = pad, pad + SEQ + pad
    total = c0 + CTX + pad
    groups = len(POOL_WINDOWS)
    landed, done, ready, out = (counter(core, "pool_weights_landed"), counter(core, "panel_done"),
                                counter(core, "pool_ready"), counter(core, "pool_out"))
    zeroed, steps = counter(core, "pool_zeroed"), counter(core, "pool_vector_step")
    n_steps = 0
    with ExitStack() as scope:
        w = core.sb(scope, "pool_w", [P, groups, P])
        padded = core.sb(scope, "pool_padded", [P, total])
        sums = core.sb(scope, "pool_sums", [P, 2, total])
        mean = core.sb(scope, "pool_mean", [P, T0])
        diff = core.sb(scope, "pool_diff", [P, groups, T0])
        with core.block() as block:
            @block.sync
            def _(sp):
                sp.dma_start(w[:, :, :], pool_weights.rearrange("g p k -> p g k")).then_inc(landed.sem, 16)

            @block.gpsimd
            def _(pool):
                nc.gpsimd.memset(padded[:, :], 0.0).then_inc(zeroed.sem, 1)

            @block.vector
            def _(dve):
                nonlocal n_steps
                chain = Chain(dve, steps, steps.base)
                dve.wait_ge(zeroed.sem, zeroed.base + 1)
                for g, window in enumerate(POOL_WINDOWS):
                    chain(nc.vector.tensor_copy(padded[:, x0:x0 + SEQ], u[:, g, 0:SEQ]))
                    chain(nc.vector.tensor_copy(padded[:, c0:c0 + CTX], u[:, g, SEQ:T0]))
                    have, src, slot = 1, padded[:, :], 0
                    while have < window:
                        n = total - 2 * have + 1
                        chain(nc.vector.tensor_tensor(sums[:, slot, 0:n], src[:, 0:n], src[:, have:have + n], ALU.add))
                        src, slot, have = sums[:, slot, :], 1 - slot, 2 * have
                    for t0, t1, at in ((0, SEQ, x0), (SEQ, T0, c0)):
                        lo = at - window // 2
                        chain(nc.vector.tensor_tensor(mean[:, t0:t1], src[:, lo:lo + t1 - t0], inv_count[:, g, t0:t1],
                                                      ALU.mult))
                    nc.vector.tensor_tensor(diff[:, g, :], mean[:, :], u[:, g, :], ALU.subtract).then_inc(ready.sem, 1)
                    dve.wait_ge(ready.sem, ready.base + g + 1)
                n_steps = chain.steps

            @block.tensor
            def _(pe):
                pe.wait_ge(landed.sem, landed.base + 16)
                for g in range(groups):
                    pe.wait_ge(ready.sem, ready.base + g + 1)
                    for a in range(2):
                        last = nc.tensor.matmul(core.psum[:, 2 * g + a, 0:T0 // 2], w[:, g, :],
                                                diff[:, g, a * T0 // 2:(a + 1) * T0 // 2], start=True, stop=True)
                    last.then_inc(done.sem, 1)

            @block.scalar
            def _(eng):
                for g in range(groups):
                    eng.wait_ge(done.sem, done.base + g + 1)
                    nc.scalar.activation(halves(dst[:, g, :]), core.psum[:, 2 * g:2 * g + 2, 0:T0 // 2], ACT.Identity,
                                         scale=col(scale_cols, g)).then_inc(out.sem, 1)
    landed.base += 16
    zeroed.base += 1
    ready.base += groups
    done.base += groups
    out.base += groups
    steps.base += n_steps



class Head:

    def __init__(self, q, queries, keys, values, out, scale, bias=None, causal=False, bias_load=None):
        self.q, self.queries, self.keys, self.values, self.out = q, queries, keys, values, out
        self.scale, self.bias, self.causal, self.bias_load = scale, bias, causal, bias_load
        self.tiles = queries // P
        self.total = sum(k.shape[-1] for k in keys)

    def seen(self, i):
        return (i + 1) * P if self.causal else self.total


def attention(core, heads, bias_tile=None, bias_mask=None):
    nc = core.nc
    ps = core.psum
    scored, biased, exped = counter(core, "att_scored"), counter(core, "att_biased"), counter(core, "att_exped")
    probs, turned, kept = counter(core, "att_probs"), counter(core, "att_turned"), counter(core, "att_kept")
    mixed, out = counter(core, "att_mixed"), counter(core, "att_out")
    steps, peaked = counter(core, "att_vector_step"), counter(core, "att_peaked")
    loaded = [counter(core, f"att_bias_landed_{s}") for s in range(2)]
    units = [(h, i) for h in range(len(heads)) for i in range(heads[h].tiles)]
    last_unit = {h: n for n, (h, i) in enumerate(units)}
    n_steps = 0
    widest = max(h.total for h in heads)
    with ExitStack() as scope:
        s = core.sb(scope, "att_scores", [P, 3, widest])
        pt = core.sb(scope, "att_turned_probs", [P, 2, widest // P, 512])
        peak = core.sb(scope, "att_peak", [P, 3])
        minus = core.sb(scope, "att_minus_peak", [P, 3])
        norm = core.sb(scope, "att_sum", [P, 3])
        recip = core.sb(scope, "att_recip", [P, 3])
        with core.block() as block:
            if bias_tile is not None:
                @block.sync
                def _(sp):
                    for h, head in enumerate(heads):
                        if h >= 2:
                            sp.wait_ge(biased.sem, biased.base + last_unit[h - 2] + 1)
                        sp.dma_start(bias_tile[:, h % 2, :], head.bias_load).then_inc(loaded[h % 2].sem, 16)

            @block.tensor
            def _(pe):
                def scores(n):
                    h, i = units[n]
                    head = heads[h]
                    if n >= 2:
                        pe.wait_ge(biased.sem, biased.base + n - 1)
                    at, seen = 0, head.seen(i)
                    for b, keys in enumerate(head.keys):
                        width = min(keys.shape[-1], seen - at)
                        if width <= 0:
                            break
                        last = nc.tensor.matmul(ps[:, 2 * (n % 2) + b, 0:width], head.q[:, i * P:(i + 1) * P],
                                                keys[:, 0:width], start=True, stop=True)
                        at += width
                    last.then_inc(scored.sem, 1)

                def transposes(n):
                    h, i = units[n]
                    seen = heads[h].seen(i) // P
                    pe.wait_ge(probs.sem, probs.base + n + 1)
                    if n >= 1:
                        pe.wait_ge(kept.sem, kept.base + n)
                    for kt in range(seen):
                        last = nc.tensor.transpose(ps[:, 4 + kt // 4, (kt % 4) * P:(kt % 4 + 1) * P],
                                                   s[:, n % 3, kt * P:(kt + 1) * P], core.ident[:, :])
                    last.then_inc(turned.sem, 1)

                def values(h, n):
                    head = heads[h]
                    pe.wait_ge(kept.sem, kept.base + n + 1)
                    if h >= 2:
                        pe.wait_ge(out.sem, out.base + h - 1)
                    o = head.out.base_row
                    for kt in range(head.total // P):
                        q0 = kt * P if head.causal else 0
                        last = nc.tensor.matmul(ps[o:o + HEAD, 6 + h % 2, q0:head.queries], head.values(kt),
                                                pt[:, h % 2, kt, q0:head.queries], start=kt == 0,
                                                stop=kt == head.total // P - 1)
                    last.then_inc(mixed.sem, 1)

                for n in range(len(units) + 1):
                    if n < len(units):
                        scores(n)
                    if n >= 1:
                        transposes(n - 1)
                        h, i = units[n - 1]
                        if i == heads[h].tiles - 1:
                            values(h, n - 1)

            @block.vector
            def _(dve):
                nonlocal n_steps
                chain = Chain(dve, steps, steps.base)

                def shift(n):
                    h, i = units[n]
                    head = heads[h]
                    seen = head.seen(i)
                    if bias_tile is not None and i == 0:
                        dve.wait_ge(loaded[h % 2].sem, loaded[h % 2].base + 16 * (h // 2 + 1))
                        b = bias_tile[:, h % 2, :].rearrange("p (r c) -> p r c", c=GRID_W)
                        chain(nc.vector.tensor_tensor(b, b, bias_mask, ALU.add))
                    dve.wait_ge(scored.sem, scored.base + n + 1)
                    row = s[:, n % 3, :]
                    if n >= 3:
                        dve.wait_ge(turned.sem, turned.base + n - 2)
                    at, banks, bias = 0, 2 * (n % 2), head.bias(i) if head.bias else None
                    if bias is not None:
                        last = nc.vector.scalar_tensor_tensor(row[:, 0:bias.shape[-1]], ps[:, banks, 0:bias.shape[-1]],
                                                              head.scale, bias, ALU.mult, ALU.add)
                        at, banks = bias.shape[-1], banks + 1
                    if at < seen:
                        if at:
                            chain(last)
                        last = nc.vector.tensor_scalar(row[:, at:seen], ps[:, banks, 0:seen - at], head.scale, None,
                                                       ALU.mult)
                    last.then_inc(biased.sem, 1)
                    dve.wait_ge(biased.sem, biased.base + n + 1)
                    chain(nc.vector.reduce_max(peak[:, n % 3:n % 3 + 1], row[:, 0:seen], AX.X))
                    nc.vector.tensor_scalar(minus[:, n % 3:n % 3 + 1], peak[:, n % 3:n % 3 + 1], -1.0, None,
                                            ALU.mult).then_inc(peaked.sem, 1)

                def normalise(n):
                    h, i = units[n]
                    seen = heads[h].seen(i)
                    dve.wait_ge(exped.sem, exped.base + n + 1)
                    c = slice(n % 3, n % 3 + 1)
                    chain(nc.vector.reciprocal(recip[:, c], norm[:, c]))
                    nc.vector.tensor_scalar(s[:, n % 3, 0:seen], s[:, n % 3, 0:seen], recip[:, c], None, ALU.mult)\
                        .then_inc(probs.sem, 1)

                for n in range(len(units) + 1):
                    if n < len(units):
                        shift(n)
                    if n >= 1:
                        normalise(n - 1)
                n_steps = chain.steps

            @block.scalar
            def _(eng):
                def exps(n):
                    h, i = units[n]
                    seen = heads[h].seen(i)
                    c = slice(n % 3, n % 3 + 1)
                    eng.wait_ge(peaked.sem, peaked.base + n + 1)
                    nc.scalar.activation(s[:, n % 3, 0:seen], s[:, n % 3, 0:seen], ACT.Exp, bias=minus[:, c],
                                         accum_out=norm[:, c]).then_inc(exped.sem, 1)

                def keep(n):
                    h, i = units[n]
                    seen = heads[h].seen(i) // P
                    eng.wait_ge(turned.sem, turned.base + n + 1)
                    if i == 0 and h >= 2:
                        eng.wait_ge(mixed.sem, mixed.base + h - 1)
                    for b in range(0, seen, 4):
                        m = min(4, seen - b)
                        last = nc.scalar.activation(
                            pt[:, h % 2, b:b + m, i * P:(i + 1) * P],
                            ps[:, 4 + b // 4, 0:m * P].rearrange("p (k q) -> p k q", q=P), ACT.Copy)
                    last.then_inc(kept.sem, 1)

                def finish(h):
                    head = heads[h]
                    o = head.out.base_row
                    eng.wait_ge(mixed.sem, mixed.base + h + 1)
                    nc.scalar.activation(head.out.ap, ps[o:o + HEAD, 6 + h % 2, 0:head.queries], ACT.Copy)\
                        .then_inc(out.sem, 1)

                for n in range(len(units) + 1):
                    if n < len(units):
                        exps(n)
                    if n >= 1:
                        keep(n - 1)
                        h, i = units[n - 1]
                        if i == heads[h].tiles - 1:
                            finish(h)
    nu, nh = len(units), len(heads)
    for sig in (scored, biased, peaked, exped, probs, turned, kept):
        sig.base += nu
    mixed.base += nh
    out.base += nh
    steps.base += n_steps
    if bias_tile is not None:
        for slot in range(2):
            loaded[slot].base += 16 * len(range(slot, nh, 2))


class Rows:

    def __init__(self, ap, base_row):
        self.ap, self.base_row = ap, base_row



def head_norm(core, x, rows, tiles, mean_of, gain, rotate=None, cos=None, sin=None):
    nc, ps = core.nc, core.psum
    squared, summed = counter(core, "norm_squared"), counter(core, "norm_summed")
    inverted, rooted = counter(core, "norm_inverted"), counter(core, "norm_rooted")
    scaled, turned, finished = counter(core, "norm_scaled"), counter(core, "norm_turned"), counter(core, "norm_finished")
    steps = counter(core, "norm_vector_step")
    per = 1 + (2 if rotate is not None else 0)
    with ExitStack() as scope:
        sq = core.sb(scope, "head_sq", [P, 2, SEQ])
        var = core.sb(scope, "head_var", [P, 2, SEQ])
        rstd = core.sb(scope, "head_rstd", [P, 2, SEQ])
        part = core.sb(scope, "head_part", [P, SEQ])
        with core.block() as block:
            @block.scalar
            def _(eng):
                def square(n):
                    if n >= 2:
                        eng.wait_ge(summed.sem, summed.base + n - 1)
                    nc.scalar.activation(sq[0:rows, n % 2, :], x[0:rows, n, :], ACT.Square).then_inc(squared.sem, 1)

                square(0)
                for n in range(tiles):
                    if n + 1 < tiles:
                        square(n + 1)
                    eng.wait_ge(inverted.sem, inverted.base + n + 1)
                    nc.scalar.activation(rstd[0:rows, n % 2, :], var[0:rows, n % 2, :], ACT.Sqrt).then_inc(rooted.sem, 1)

            @block.tensor
            def _(pe):
                def mean(n):
                    pe.wait_ge(squared.sem, squared.base + n + 1)
                    if n >= 2:
                        pe.wait_ge(inverted.sem, inverted.base + n - 1)
                    nc.tensor.matmul(ps[0:rows, n % 2, :], mean_of, sq[0:rows, n % 2, :], start=True, stop=True)\
                        .then_inc(summed.sem, 1)

                mean(0)
                for n in range(tiles):
                    if n + 1 < tiles:
                        mean(n + 1)
                    if rotate is not None:
                        pe.wait_ge(scaled.sem, scaled.base + n + 1)
                        if n >= 2:
                            pe.wait_ge(finished.sem, finished.base + n - 1)
                        nc.tensor.matmul(ps[0:rows, 2 + n % 2, :], rotate, x[0:rows, n, :], start=True, stop=True)\
                            .then_inc(turned.sem, 1)

            @block.vector
            def _(dve):
                chain = Chain(dve, steps, steps.base)
                for n in range(tiles):
                    dve.wait_ge(summed.sem, summed.base + n + 1)
                    v = var[0:rows, n % 2, :]
                    chain(nc.vector.tensor_scalar(v, ps[0:rows, n % 2, :], EPS, None, ALU.add))
                    nc.vector.reciprocal(v, v).then_inc(inverted.sem, 1)
                    dve.wait_ge(rooted.sem, rooted.base + n + 1)
                    nc.vector.scalar_tensor_tensor(x[0:rows, n, :], x[0:rows, n, :], gain, rstd[0:rows, n % 2, :],
                                                   ALU.mult, ALU.mult).then_inc(scaled.sem, 1)
                    if rotate is not None:
                        dve.wait_ge(turned.sem, turned.base + n + 1)
                        chain(nc.vector.tensor_tensor(part[0:rows, :], ps[0:rows, 2 + n % 2, :], sin, ALU.mult))
                        chain(nc.vector.tensor_tensor(x[0:rows, n, :], x[0:rows, n, :], cos, ALU.mult))
                        nc.vector.tensor_tensor(x[0:rows, n, :], x[0:rows, n, :], part[0:rows, :], ALU.add)\
                            .then_inc(finished.sem, 1)
                        dve.wait_ge(finished.sem, finished.base + n + 1)
    for sig in (squared, summed, inverted, rooted, scaled):
        sig.base += tiles
    if rotate is not None:
        turned.base += tiles
        finished.base += tiles
    steps.base += per * tiles


def rotation_tables(core, positions, freqs, tables):
    nc = core.nc
    landed, reduced, waved = counter(core, "positions_landed"), counter(core, "angle_reduced"), counter(core, "angle_waved")
    steps = counter(core, "rope_vector_step")
    c1 = 6.28125
    c2 = float(np.float32(np.floor((2 * np.pi - c1) * 2.0 ** 20) / 2.0 ** 20))
    c3 = float(2 * np.pi - c1 - c2)
    magic = 1.5 * 2.0 ** 23
    pi = float(np.nextafter(np.float32(np.pi), np.float32(0)))
    n_steps = 0
    with ExitStack() as scope:
        raw = core.sb(scope, "rope_positions", [P, SEQ], I32)
        pos = core.sb(scope, "rope_pos", [P, SEQ])
        ang = core.sb(scope, "rope_angle", [P, SEQ])
        turns = core.sb(scope, "rope_turns", [P, SEQ])
        red = core.sb(scope, "rope_reduced", [P, 4, SEQ])
        with core.block() as block:
            @block.sync
            def _(sp):
                sp.dma_start(raw[:, :], positions.to_broadcast([P, SEQ])).then_inc(landed.sem, 16)

            @block.vector
            def _(dve):
                nonlocal n_steps
                chain = Chain(dve, steps, steps.base)
                dve.wait_ge(landed.sem, landed.base + 16)
                chain(nc.vector.tensor_copy(pos[:, :], raw[:, :]))
                for n in range(len(tables)):
                    for j, quarter in enumerate((0.25, 0.0)):
                        r = red[:, 2 * n + j, :]
                        chain(nc.vector.tensor_scalar(ang[:, :], pos[:, :], col(freqs, n), None, ALU.mult))
                        chain(nc.vector.tensor_scalar(turns[:, :], ang[:, :], float(1 / (2 * np.pi)), quarter,
                                                      ALU.mult, ALU.add))
                        chain(nc.vector.tensor_scalar(turns[:, :], turns[:, :], magic, None, ALU.add))
                        chain(nc.vector.tensor_scalar(turns[:, :], turns[:, :], -magic, None, ALU.add))
                        src = ang[:, :]
                        for c in (c1, c2, c3):
                            chain(nc.vector.scalar_tensor_tensor(r, turns[:, :], -c, src, ALU.mult, ALU.add))
                            src = r
                        chain(nc.vector.tensor_scalar(r, r, quarter * 2 * float(np.pi), pi, ALU.add, ALU.min))
                        nc.vector.tensor_scalar(r, r, -pi, None, ALU.max).then_inc(reduced.sem, 1)
                n_steps = chain.steps

            @block.scalar
            def _(eng):
                for n, pair in enumerate(tables):
                    for j in range(2):
                        eng.wait_ge(reduced.sem, reduced.base + 2 * n + j + 1)
                        nc.scalar.activation(pair[j], red[:, 2 * n + j, :], ACT.Sin).then_inc(waved.sem, 1)
    landed.base += 16
    reduced.base += 2 * len(tables)
    waved.base += 2 * len(tables)
    steps.base += n_steps



def conv_mlp(core, weights, act, taps, bias, dst):
    nc, ps = core.nc, core.psum
    nt, ring = 2 * FT2, 4
    landed = [counter(core, f"panel_landed_{s}") for s in range(4)]
    done, first, evicted = counter(core, "panel_done"), counter(core, "panel_first_evict"), counter(core, "panel_evicted")
    conv, gated, steps = counter(core, "conv_done"), counter(core, "gate_done"), counter(core, "gemm_vector_step")
    blocks = nt // ring
    per = 2 * 2 + 2 * 2 - 1 + 1
    with ExitStack() as scope:
        w = core.sb(scope, "up_panels", [P, ring, D])
        y = core.sb(scope, "conv_out", [P, ring, SEQ])
        gate = core.sb(scope, "gate_out", [P, 2, SEQ])
        with core.block() as block:
            @block.sync
            def _(sp):
                with sp.Fori(0, blocks) as blk:
                    for u in range(ring):
                        sp.wait_ge(done.sem, done.base + blk * ring + u + 1 - ring)
                        sp.dma_start(w[:, u, :], weights[bass.ds(blk * ring + u, 1), :, :].rearrange("a p k -> p (a k)"))\
                            .then_inc(landed[u].sem, 16)

            @block.tensor
            def _(pe):
                with pe.Fori(0, blocks) as blk:
                    for u in range(ring):
                        pe.wait_ge(landed[u].sem, landed[u].base + 16 * (blk + 1))
                        pe.wait_ge(evicted.sem, evicted.base + blk * ring + u + 1 - ring)
                        for k in range(DT):
                            last = nc.tensor.matmul(ps[:, u, :], w[:, u, k * P:(k + 1) * P], act[:, k, 0:SEQ],
                                                    start=k == 0, stop=k == DT - 1)
                        last.then_inc(done.sem, 1)

            @block.scalar
            def _(eng):
                with eng.Fori(0, blocks) as blk:
                    for u in range(ring):
                        n = blk * ring + u
                        eng.wait_ge(done.sem, done.base + n + 1)
                        eng.wait_ge(gated.sem, gated.base + blk * 2 + u // 2 - 1)
                        nc.scalar.activation(y[:, u, :], ps[:, u, :], ACT.Identity, bias=col(bias, n),
                                             scale=col(taps[:, 2, :], n)).then_inc(first.sem, 1)
                        if u % 2 == 1:
                            eng.wait_ge(evicted.sem, evicted.base + n)
                            nc.scalar.activation(gate[:, u // 2, :], y[:, u - 1, :], ACT.Sigmoid).then_inc(conv.sem, 1)

            @block.vector
            def _(dve):
                with dve.Fori(0, blocks) as blk:
                    chain = Chain(dve, steps, steps.base + blk * 6)
                    for u in range(ring):
                        n = blk * ring + u
                        dve.wait_ge(first.sem, first.base + n + 1)
                        chain(nc.vector.scalar_tensor_tensor(y[:, u, 1:SEQ], ps[:, u, 0:SEQ - 1], col(taps[:, 1, :], n),
                                                             y[:, u, 1:SEQ], ALU.mult, ALU.add))
                        nc.vector.scalar_tensor_tensor(y[:, u, 2:SEQ], ps[:, u, 0:SEQ - 2], col(taps[:, 0, :], n),
                                                       y[:, u, 2:SEQ], ALU.mult, ALU.add).then_inc(evicted.sem, 1)
                        if u % 2 == 1:
                            dve.wait_ge(evicted.sem, evicted.base + n + 1)
                            dve.wait_ge(conv.sem, conv.base + blk * 2 + u // 2 + 1)
                            chain(nc.vector.tensor_tensor(gate[:, u // 2, :], gate[:, u // 2, :], y[:, u - 1, :], ALU.mult))
                            nc.vector.tensor_tensor(tile(dst, blk * 2 + u // 2), gate[:, u // 2, :], y[:, u, :],
                                                    ALU.mult).then_inc(gated.sem, 1)
                    assert chain.steps == 6
    for s in range(ring):
        landed[s].base += 16 * blocks
    done.base += nt
    first.base += nt
    evicted.base += nt
    conv.base += FT2
    gated.base += FT2
    steps.base += 6 * blocks



def token_mix(core, h, segments, mu, dst, tokens):
    nc = core.nc
    shifted, mixed, steps = counter(core, "mix_shifted"), counter(core, "mix_done"), counter(core, "mix_vector_step")
    per = 2 * len(segments) + 1
    with ExitStack() as scope:
        pair = core.sb(scope, "mix_pair", [P, T0])
        with core.block() as block:
            @block.vector
            def _(dve):
                chain = Chain(dve, steps, steps.base)
                for k in range(DT):
                    for t0, t1 in segments:
                        chain(nc.vector.tensor_tensor(pair[:, t0 + 1:t1 - 1], h[:, k, t0:t1 - 2], h[:, k, t0 + 2:t1],
                                                      ALU.add))
                        nc.vector.tensor_copy(pair[:, t0:t0 + 1], h[:, k, t0 + 1:t0 + 2])
                        chain(nc.vector.tensor_copy(pair[:, t1 - 1:t1], h[:, k, t1 - 2:t1 - 1]))
                    chain(nc.vector.scalar_tensor_tensor(pair[:, 0:tokens], pair[:, 0:tokens], 0.5, h[:, k, 0:tokens],
                                                         ALU.mult, ALU.subtract))
                    nc.vector.scalar_tensor_tensor(dst[:, k, 0:tokens], pair[:, 0:tokens], col(mu, k), h[:, k, 0:tokens],
                                                   ALU.mult, ALU.add).then_inc(mixed.sem, 1)
                    dve.wait_ge(mixed.sem, mixed.base + k + 1)
    mixed.base += DT
    steps.base += per * DT


def spill(core, src, dst):
    stored = counter(core, "spill_stored")
    with core.block() as block:
        @block.sync
        def _(sp):
            sp.dma_start(dst.rearrange("k p t -> p k t"), src).then_inc(stored.sem, 16)
            sp.wait_ge(stored.sem, stored.base + 16)
    stored.base += 16


def fill(core, src, dst):
    spill_back = counter(core, "spill_fetched")
    with core.block() as block:
        @block.sync
        def _(sp):
            sp.dma_start(dst, src.rearrange("k p t -> p k t")).then_inc(spill_back.sem, 16)
            sp.wait_ge(spill_back.sem, spill_back.base + 16)
    spill_back.base += 16


def wkv(core, lora_w, lora_a, up_panels, k_dram, v_dram, r_dram, g_dram, par, masks, dst):
    nc, ps = core.nc, core.psum
    chunks = T0 // CHUNK
    tiles = T0 // P
    xt = SEQ // P
    levels = []
    n = 2
    while n < CHUNK:
        levels.append(n)
        n *= 2
    def sig(name):
        return counter(core, name)

    loaded, lora, acted = sig("pair_loaded"), sig("lora_done"), sig("lora_activated")
    ps_kk, ps_inv, ps_root = sig("key_squared"), sig("key_inverted"), sig("key_rooted")
    ps_sum, normed = sig("key_summed"), sig("key_normed")
    expo, powers = sig("decay_exponent"), sig("decay_powers")
    tilde = sig("tilde_ready")
    turned, tok = sig("tilde_turned"), sig("token_major_kept")
    product = [sig(f"triangle_product_{h}") for h in range(2)]
    keptv = [sig(f"triangle_kept_{h}") for h in range(2)]
    acte = [sig(f"factor_kept_{h}") for h in range(2)]
    u_done, u_kept, s_done, s_kept = sig("u_product"), sig("u_kept"), sig("state_product"), sig("state_kept")
    y_done, y_kept, zeroed = sig("y_state_product"), sig("y_state_kept"), sig("state_zeroed")
    intra, summed = sig("y_intra_product"), sig("y_summed")
    mean, centred, csq, var = sig("gn_mean"), sig("gn_centred"), sig("gn_squared"), sig("gn_var")
    ginv, groot, bonus_in, bonus = sig("gn_inverted"), sig("gn_rooted"), sig("bonus_terms"), sig("bonus_product")
    pair_done, steps = sig("pair_done"), sig("wkv_vector_step")

    def exchanges(m):
        return ["gram"] + (["read"] if m < xt // 2 else []) + [f"{s}{n}" for n in levels for s in "zw"] + ["kx", "ux"]

    before = [sum(len(exchanges(i)) for i in range(m)) for m in range(tiles // 2 + 1)]
    per_pair = before[-1]
    before_kept = [b - m for m, b in enumerate(before)]
    kept_per_pair = before_kept[-1]
    order = [[(SEQ // CHUNK + c) for c in range(CTX // CHUNK)] + list(range(SEQ // CHUNK)),
             [chunks - 1 - c for c in range(CTX // CHUNK)] + list(range(SEQ // CHUNK - 1, -1, -1))]
    first_x = CTX // CHUNK
    VSTEPS = 67

    with ExitStack() as scope:
        def sb(name, shape):
            return core.sb(scope, name, shape)

        ups = sb("wkv_ups", [P, 2 * P])
        K, V = sb("wkv_k", [P, T0]), sb("wkv_v", [P, T0])
        R, G = sb("wkv_r", [P, SEQ]), sb("wkv_g", [P, SEQ])
        LW, A = sb("wkv_logw", [P, 2, T0]), sb("wkv_a", [P, 2, T0])
        KK, SQ, VAR = sb("wkv_kk", [P, T0]), sb("wkv_sq", [P, T0]), sb("wkv_var", [P, T0])
        INC, EXC = sb("wkv_inc", [P, 2, T0]), sb("wkv_exc", [P, 2, T0])
        PINC, PINV = sb("wkv_pinc", [P, 2, SEQ]), sb("wkv_pinv", [P, 2, T0])
        KD = sb("wkv_kd", [P, 2, T0])
        KSUM = sb("wkv_ksum", [P, SEQ])
        PC = sb("wkv_chunk_decay", [P, 2, chunks])
        TOK = sb("wkv_tok", [P, 7, T0])
        KX = INC
        UX, U = (t[:, :, :].rearrange("p d (n h i) -> p d n h i", h=2, i=HEAD) for t in (LW, PINV))
        GA, GK = sb("wkv_ga", [P, 2, xt, 2, P]), sb("wkv_gk", [P, 2, xt, 2, P])
        S, SP = sb("wkv_s", [P, 2, 2, P]), sb("wkv_sp", [P, 2, P])
        YS = sb("wkv_ys", [P, 2, SEQ])
        MT, MK = sb("wkv_mt", [P, 2, 512]), sb("wkv_mk", [P, 2, 512])
        X, XT, Z = sb("wkv_x", [P, 2, 512]), sb("wkv_xt", [P, 2, 512]), sb("wkv_z", [P, 2, 512])
        MKV = sb("wkv_mkv", [P, 2, 4 * HEAD])
        BON = sb("wkv_bonus", [P, SEQ])

        def group(j, d):
            return slice((2 * j + d) * P, (2 * j + d + 1) * P)

        def over_tiles(ap):
            return ap.rearrange("p (j c) -> p j c", j=2)

        def mask(n):
            return masks[n].unsqueeze(1).to_broadcast([P, 2, 2 * P])

        with core.block() as block:
            @block.sync
            def _(sp):
                with sp.Fori(0, DT) as ft:
                    sp.wait_ge(pair_done.sem, pair_done.base + ft)
                    for dst_, src in ((ups, up_panels), (K, k_dram), (V, v_dram), (R, r_dram), (G, g_dram)):
                        sp.dma_start(dst_[:, :], src[bass.ds(ft, 1), :, :].rearrange("a p t -> p (a t)"))\
                            .then_inc(loaded.sem, 16)

            @block.tensor
            def _(pe):
                with pe.Fori(0, DT) as ft:
                    pe.wait_ge(loaded.sem, loaded.base + 80 * (ft + 1))
                    pe.wait_ge(pair_done.sem, pair_done.base + ft)
                    for which, src in ((0, lora_w), (1, lora_a)):
                        for d in range(2):
                            rows = slice(d * HEAD, (d + 1) * HEAD)
                            for a in range(2):
                                last = nc.tensor.matmul(ps[:, 4 * which + 2 * d + a, 0:T0 // 2],
                                                        ups[rows, which * P:(which + 1) * P],
                                                        src[rows, a * T0 // 2:(a + 1) * T0 // 2], start=True, stop=True)
                            last.then_inc(lora.sem, 1)
                    pe.wait_ge(ps_kk.sem, ps_kk.base + ft + 1)
                    pe.wait_ge(acted.sem, acted.base + 4 * ft + 4)
                    for a in range(2):
                        last = nc.tensor.matmul(ps[:, a, 0:T0 // 2], core.head_sum[:, :],
                                                SQ[:, a * T0 // 2:(a + 1) * T0 // 2], start=True, stop=True)
                    last.then_inc(ps_sum.sem, 1)
                    for n, src in enumerate((EXC[:, 0, :], EXC[:, 1, :], A[:, 0, :], A[:, 1, :], KD[:, 0, :],
                                             KD[:, 1, :], V[:, :])):
                        if n == 0:
                            pe.wait_ge(tilde.sem, tilde.base + ft + 1)
                        if n >= 4:
                            pe.wait_ge(tok.sem, tok.base + 7 * ft + n - 3)
                        for t in range(tiles):
                            last = nc.tensor.transpose(ps[:, 2 * (n % 4) + t // 3, (t % 3) * P:(t % 3 + 1) * P],
                                                       src[:, t * P:(t + 1) * P], core.ident[:, :])
                        last.then_inc(turned.sem, 1)
                    pe.wait_ge(tok.sem, tok.base + 7 * ft + 7)

                    def products(name, h, m):
                        rows = slice(h * HEAD, (h + 1) * HEAD)
                        b = 4 * h
                        for j in range(2):
                            t = 2 * m + j
                            at = slice(t * P, (t + 1) * P)
                            for d in range(2):
                                g = group(j, d)
                                kkt, at_, kt_ = EXC[rows, d, at], A[rows, d, at], KD[rows, d, at]
                                if name == "gram":
                                    nc.tensor.matmul(ps[:, b, g], at_, kkt, start=True, stop=True)
                                    nc.tensor.matmul(ps[:, b + 1, g], kkt, at_, start=True, stop=True)
                                    last = nc.tensor.matmul(ps[:, b + 2, g], kt_, kkt, start=True, stop=True)
                                elif name == "read":
                                    rt = PINC[rows, d, at]
                                    nc.tensor.matmul(ps[:, b, g], at_, rt, start=True, stop=True)
                                    last = nc.tensor.matmul(ps[:, b + 3, g], kt_, rt, start=True, stop=True)
                                elif name[0] == "z":
                                    last = nc.tensor.matmul(ps[:, b + 1, g], MT[:, h, g], X[:, h, g], start=True, stop=True)
                                elif name[0] == "w":
                                    if int(name[1:]) != levels[-1]:
                                        nc.tensor.matmul(ps[:, b + 2, g], XT[:, h, g], Z[:, h, g], start=True, stop=True)
                                    last = nc.tensor.matmul(ps[:, b + 3, g], Z[:, h, g], XT[:, h, g], start=True, stop=True)
                                elif name == "kx":
                                    c = slice(t * P + h * HEAD, t * P + (h + 1) * HEAD)
                                    nc.tensor.matmul(ps[rows, b, g], TOK[:, d, c], XT[:, h, g], start=True, stop=True)
                                    last = nc.tensor.matmul(ps[:, b + 1, (2 * j + d) * HEAD:(2 * j + d + 1) * HEAD],
                                                            MK[:, h, g], TOK[:, 6, c], start=True, stop=True)
                                else:
                                    v = slice((2 * j + d) * HEAD, (2 * j + d + 1) * HEAD)
                                    last = nc.tensor.matmul(ps[:, b + 2, v], XT[:, h, g], MKV[:, h, v],
                                                            start=True, stop=True)
                        last.then_inc(product[h].sem, 1)

                    for m in range(tiles // 2):
                        for e, name in enumerate(exchanges(m)):
                            for h in range(2):
                                pe.wait_ge(keptv[h].sem, keptv[h].base + kept_per_pair * ft + before_kept[m] + e)
                                if e == 0:
                                    pe.wait_ge(acte[h].sem, acte[h].base + 3 * ft + m)
                                products(name, h, m)
                    for h in range(2):
                        pe.wait_ge(keptv[h].sem, keptv[h].base + kept_per_pair * (ft + 1))
                        pe.wait_ge(acte[h].sem, acte[h].base + 3 * ft + 3)
                    pe.wait_ge(zeroed.sem, zeroed.base + ft + 1)
                    for c in range(chunks):
                        if c:
                            pe.wait_ge(s_kept.sem, s_kept.base + (chunks - 1) * ft + c)
                        n = c - first_x
                        if n >= 2:
                            pe.wait_ge(y_kept.sem, y_kept.base + (chunks - first_x) * ft + n - 1)
                        for d in range(2):
                            t = order[d][c] // 2
                            last = nc.tensor.matmul(ps[:, c % 2, d * P:(d + 1) * P], KX[:, d, t * P:(t + 1) * P],
                                                    S[:, c % 2, d, :], start=True, stop=True)
                        last.then_inc(u_done.sem, 1)
                        if n >= 0:
                            for d in range(2):
                                ch = order[d][c]
                                last = nc.tensor.matmul(ps[:, 6 + c % 2, d * CHUNK:(d + 1) * CHUNK], S[:, c % 2, d, :],
                                                        PINC[:, d, ch * CHUNK:(ch + 1) * CHUNK], start=True, stop=True)
                            last.then_inc(y_done.sem, 1)
                        if c < chunks - 1:
                            pe.wait_ge(u_kept.sem, u_kept.base + chunks * ft + c + 1)
                            for d in range(2):
                                ch = order[d][c]
                                rows = slice(ch % 2 * HEAD, ch % 2 * HEAD + HEAD)
                                f = slice(ch // 2 * P, ch // 2 * P + P)
                                nc.tensor.matmul(ps[:, 4 + d, 0:P], TOK[rows, 2 + d, f],
                                                 U[rows, d, ch // 2, :, :].rearrange("p h i -> p (h i)"),
                                                 start=True, stop=False)
                                last = nc.tensor.matmul(ps[:, 4 + d, 0:P], TOK[rows, 4 + d, f],
                                                        TOK[rows, 6, f], start=False, stop=True)
                            last.then_inc(s_done.sem, 1)
                    pe.wait_ge(u_kept.sem, u_kept.base + chunks * (ft + 1))
                    for t in range(xt):
                        for h in range(2):
                            out = slice(h * HEAD, (h + 1) * HEAD)
                            for d in range(2):
                                nc.tensor.matmul(ps[out, 0, t * P:(t + 1) * P], U[:, d, t, h, :], GA[:, h, t, d, :],
                                                 start=d == 0, stop=False)
                                last = nc.tensor.matmul(ps[out, 0, t * P:(t + 1) * P],
                                                        TOK[:, 6, t * P + h * HEAD:t * P + (h + 1) * HEAD],
                                                        GK[:, h, t, d, :], start=False, stop=d == 1)
                    last.then_inc(intra.sem, 1)
                    pe.wait_ge(summed.sem, summed.base + ft + 1)
                    nc.tensor.matmul(ps[:, 1, :], core.head_mean[:, :], YS[:, 0, :], start=True, stop=True)\
                        .then_inc(mean.sem, 1)
                    pe.wait_ge(csq.sem, csq.base + ft + 1)
                    nc.tensor.matmul(ps[:, 2, :], core.head_mean[:, :], SQ[:, 0:SEQ], start=True, stop=True)\
                        .then_inc(var.sem, 1)
                    pe.wait_ge(bonus_in.sem, bonus_in.base + ft + 1)
                    nc.tensor.matmul(ps[:, 3, :], core.head_sum[:, :], BON[:, :], start=True, stop=True)\
                        .then_inc(bonus.sem, 1)

            @block.scalar
            def _(eng):
                with eng.Fori(0, DT) as ft:
                    eng.wait_ge(pair_done.sem, pair_done.base + ft)
                    for which, dst_, bias in ((0, LW, par["w0"]), (1, A, par["a0"])):
                        for d in range(2):
                            eng.wait_ge(lora.sem, lora.base + 4 * ft + 2 * which + d + 1)
                            b = 4 * which + 2 * d
                            nc.scalar.activation(halves(dst_[:, d, :]), ps[:, b:b + 2, 0:T0 // 2], ACT.Sigmoid,
                                                 bias=col(bias[d], ft)).then_inc(acted.sem, 1)
                    eng.wait_ge(normed.sem, normed.base + 2 * ft + 1)
                    nc.scalar.activation(SQ[:, :], KK[:, :], ACT.Square).then_inc(ps_kk.sem, 1)
                    eng.wait_ge(ps_inv.sem, ps_inv.base + ft + 1)
                    nc.scalar.activation(VAR[:, :], VAR[:, :], ACT.Sqrt).then_inc(ps_root.sem, 1)
                    for d in range(2):
                        eng.wait_ge(expo.sem, expo.base + 2 * ft + d + 1)
                        nc.scalar.activation(EXC[:, d, :], EXC[:, d, :], ACT.Exp)
                        nc.scalar.activation(PINC[:, d, :], INC[:, d, 0:SEQ], ACT.Exp)
                        end = CHUNK - 1 if d == 0 else 0
                        nc.scalar.activation(PC[:, d, :], INC[:, d, end::CHUNK], ACT.Exp)
                        nc.scalar.activation(PINV[:, d, :], INC[:, d, :], ACT.Exp, scale=-1.0).then_inc(powers.sem, 1)
                    for n in range(7):
                        eng.wait_ge(turned.sem, turned.base + 7 * ft + n + 1)
                        b = 2 * (n % 4)
                        nc.scalar.activation(halves(TOK[:, n, :]), ps[:, b:b + 2, 0:T0 // 2], ACT.Copy)\
                            .then_inc(tok.sem, 1)
                    for m in range(tiles // 2):
                        names = exchanges(m)
                        for h in range(2):
                            rows = slice(h * HEAD, (h + 1) * HEAD)
                            b = 4 * h
                            eng.wait_ge(product[h].sem, product[h].base + per_pair * ft + before[m] + len(names) - 1)
                            for d in range(2):
                                nc.scalar.activation(
                                    KX[rows, d, 2 * m * P:2 * (m + 1) * P].rearrange("p (j c) -> p j c", j=2),
                                    over_tiles(ps[rows, b, :])[:, :, d * P:(d + 1) * P], ACT.Copy, scale=-1.0)
                            eng.wait_ge(product[h].sem, product[h].base + per_pair * ft + before[m] + len(names))
                            for d in range(2):
                                last = nc.scalar.activation(
                                    UX[:, d, 2 * m:2 * m + 2, h, :],
                                    ps[:, b + 2, 0:4 * HEAD].rearrange("p (j c) -> p j c", j=2)[:, :, d * HEAD:(d + 1) * HEAD],
                                    ACT.Copy, scale=-1.0)
                            last.then_inc(acte[h].sem, 1)
                    for c in range(first_x, chunks):
                        eng.wait_ge(y_done.sem, y_done.base + (chunks - first_x) * ft + c - first_x + 1)
                        for d in range(2):
                            ch = order[d][c]
                            last = nc.scalar.activation(YS[:, d, ch * CHUNK:(ch + 1) * CHUNK],
                                                        ps[:, 6 + c % 2, d * CHUNK:(d + 1) * CHUNK], ACT.Copy)
                        last.then_inc(y_kept.sem, 1)
                    eng.wait_ge(centred.sem, centred.base + ft + 1)
                    nc.scalar.activation(SQ[:, 0:SEQ], YS[:, 1, :], ACT.Square).then_inc(csq.sem, 1)
                    eng.wait_ge(ginv.sem, ginv.base + ft + 1)
                    nc.scalar.activation(VAR[:, 0:SEQ], VAR[:, 0:SEQ], ACT.Sqrt).then_inc(groot.sem, 1)

            @block.vector
            def _(dve):
                with dve.Fori(0, DT) as ft:
                    chain = Chain(dve, steps, steps.base + VSTEPS * ft)
                    tt, ts, stt = nc.vector.tensor_tensor, nc.vector.tensor_scalar, nc.vector.scalar_tensor_tensor
                    dve.wait_ge(loaded.sem, loaded.base + 80 * (ft + 1))
                    ts(KK[:, :], K[:, :], col(par["kk"], ft), None, ALU.mult).then_inc(normed.sem, 1)
                    nc.vector.memset(S[:, :, :, :], 0.0).then_inc(zeroed.sem, 1)
                    for d in range(2):
                        dve.wait_ge(acted.sem, acted.base + 4 * ft + d + 1)
                        chain(ts(LW[:, d, :], LW[:, d, :], -DECAY_SCALE, None, ALU.mult))
                        chain(nc.vector.tensor_tensor_scan(INC[:, d, :], masks["resets"], LW[:, d, :], 0.0,
                                                           ALU.mult, ALU.add))
                        if d == 0:
                            tt(EXC[:, d, :], INC[:, d, :], LW[:, d, :], ALU.subtract).then_inc(expo.sem, 1)
                            dve.wait_ge(expo.sem, expo.base + 2 * ft + 1)
                        else:
                            by_chunk = INC[:, d, :].rearrange("p (c t) -> p c t", t=CHUNK)
                            whole = by_chunk[:, :, CHUNK - 1:CHUNK].to_broadcast([P, chunks, CHUNK])
                            chain(tt(EXC[:, d, :].rearrange("p (c t) -> p c t", t=CHUNK), whole, by_chunk, ALU.subtract))
                            tt(INC[:, d, :], EXC[:, d, :], LW[:, d, :], ALU.add).then_inc(expo.sem, 1)
                            dve.wait_ge(expo.sem, expo.base + 2 * ft + 2)
                    dve.wait_ge(ps_sum.sem, ps_sum.base + ft + 1)
                    chain(ts(halves(VAR[:, :]), ps[:, 0:2, 0:T0 // 2], 1e-24, None, ALU.max))
                    nc.vector.reciprocal(VAR[:, :], VAR[:, :]).then_inc(ps_inv.sem, 1)
                    dve.wait_ge(ps_root.sem, ps_root.base + ft + 1)
                    tt(KK[:, :], KK[:, :], VAR[:, :], ALU.mult).then_inc(normed.sem, 1)
                    dve.wait_ge(normed.sem, normed.base + 2 * ft + 2)
                    for d in range(2):
                        dve.wait_ge(acted.sem, acted.base + 4 * ft + 3 + d)
                        chain(ts(KD[:, d, :], A[:, d, :], -1.0, col(par["ka"], ft), ALU.add, ALU.mult))
                        chain(stt(KD[:, d, :], KD[:, d, :], 1.0, K[:, :], ALU.add, ALU.mult))
                        chain(tt(A[:, d, :], A[:, d, :], KK[:, :], ALU.mult))
                    chain(tt(KSUM[:, :], KD[:, 0, 0:SEQ], KD[:, 1, 0:SEQ], ALU.add))
                    for d in range(2):
                        dve.wait_ge(powers.sem, powers.base + 2 * ft + d + 1)
                        chain(tt(KD[:, d, :], KD[:, d, :], PINV[:, d, :], ALU.mult))
                        chain(tt(A[:, d, :], A[:, d, :], PINV[:, d, :], ALU.mult))
                        chain(tt(PINC[:, d, :], PINC[:, d, :], R[:, :], ALU.mult))
                        last = tt(EXC[:, d, :], EXC[:, d, :], KK[:, :], ALU.mult)
                        if d == 0:
                            chain(last)
                    last.then_inc(tilde.sem, 1)
                    chain(tt(KSUM[:, :], KSUM[:, :], R[:, :], ALU.mult))
                    ts(BON[:, :], KSUM[:, :], col(par["rk"], ft), None, ALU.mult).then_inc(bonus_in.sem, 1)

                    def keep(name, h, m):
                        b = 4 * h
                        if name == "gram":
                            chain(tt(over_tiles(MT[:, h, :]), over_tiles(ps[:, b, :]), mask("strict"), ALU.mult))
                            chain(tt(over_tiles(X[:, h, :]), over_tiles(ps[:, b + 1, :]), mask("minus_first"), ALU.mult))
                            chain(tt(over_tiles(XT[:, h, :]), over_tiles(MT[:, h, :]), mask("minus_first_t"), ALU.mult))
                            chain(tt(over_tiles(X[:, h, :]), over_tiles(X[:, h, :]), mask("ident"), ALU.add))
                            chain(tt(over_tiles(XT[:, h, :]), over_tiles(XT[:, h, :]), mask("ident"), ALU.add))
                            last = tt(over_tiles(MK[:, h, :]), over_tiles(ps[:, b + 2, :]), mask("strict"), ALU.mult)
                        elif name == "read":
                            for dst_, bank in ((GA, b), (GK, b + 3)):
                                last = tt(dst_[:, h, 2 * m:2 * m + 2, :, :].rearrange("p j d c -> p j (d c)"),
                                          over_tiles(ps[:, bank, :]), mask("inclusive"), ALU.mult)
                        elif name[0] == "z":
                            last = tt(over_tiles(Z[:, h, :]), over_tiles(ps[:, b + 1, :]), mask(int(name[1:])), ALU.mult)
                        elif name[0] == "w":
                            if int(name[1:]) != levels[-1]:
                                tt(X[:, h, :], X[:, h, :], ps[:, b + 2, :], ALU.subtract)
                            last = tt(XT[:, h, :], XT[:, h, :], ps[:, b + 3, :], ALU.subtract)
                        else:
                            last = nc.vector.tensor_copy(MKV[:, h, :], ps[:, b + 1, 0:4 * HEAD])
                        last.then_inc(keptv[h].sem, 1)

                    for m in range(tiles // 2):
                        for e, name in enumerate(exchanges(m)[:-1]):
                            for h in range(2):
                                dve.wait_ge(product[h].sem, product[h].base + per_pair * ft + before[m] + e + 1)
                                keep(name, h, m)
                    dve.wait_ge(zeroed.sem, zeroed.base + ft + 1)
                    for c in range(chunks):
                        if c < chunks - 1:
                            for d in range(2):
                                last = ts(SP[:, d, :], S[:, c % 2, d, :], PC[:, d, order[d][c]:order[d][c] + 1], None,
                                          ALU.mult)
                            chain(last)
                        dve.wait_ge(u_done.sem, u_done.base + chunks * ft + c + 1)
                        if c == 0:
                            for h in range(2):
                                dve.wait_ge(acte[h].sem, acte[h].base + 3 * ft + 3)
                        for d in range(2):
                            ch = order[d][c]
                            rows = slice(ch % 2 * HEAD, ch % 2 * HEAD + HEAD)
                            last = tt(U[rows, d, ch // 2, :, :].rearrange("p h i -> p (h i)"),
                                      ps[rows, c % 2, d * P:(d + 1) * P],
                                      UX[rows, d, ch // 2, :, :].rearrange("p h i -> p (h i)"), ALU.add)
                        last.then_inc(u_kept.sem, 1)
                        if c < chunks - 1:
                            dve.wait_ge(s_done.sem, s_done.base + (chunks - 1) * ft + c + 1)
                            for d in range(2):
                                for h in range(2):
                                    own = slice(h * HEAD, (h + 1) * HEAD)
                                    last = stt(S[own, 1 - c % 2, d, own], ps[own, 4 + d, own],
                                               PC[own, d, order[d][c]:order[d][c] + 1], SP[own, d, own],
                                               ALU.mult, ALU.add)
                            last.then_inc(s_kept.sem, 1)
                            dve.wait_ge(s_kept.sem, s_kept.base + (chunks - 1) * ft + c + 1)
                    dve.wait_ge(intra.sem, intra.base + ft + 1)
                    dve.wait_ge(y_kept.sem, y_kept.base + (chunks - first_x) * (ft + 1))
                    chain(tt(YS[:, 0, :], YS[:, 0, :], YS[:, 1, :], ALU.add))
                    tt(YS[:, 0, :], ps[:, 0, :], YS[:, 0, :], ALU.add).then_inc(summed.sem, 1)
                    dve.wait_ge(mean.sem, mean.base + ft + 1)
                    dve.wait_ge(summed.sem, summed.base + ft + 1)
                    tt(YS[:, 1, :], YS[:, 0, :], ps[:, 1, :], ALU.subtract).then_inc(centred.sem, 1)
                    dve.wait_ge(var.sem, var.base + ft + 1)
                    chain(ts(VAR[:, 0:SEQ], ps[:, 2, :], GN_EPS, None, ALU.add))
                    nc.vector.reciprocal(VAR[:, 0:SEQ], VAR[:, 0:SEQ]).then_inc(ginv.sem, 1)
                    dve.wait_ge(groot.sem, groot.base + ft + 1)
                    dve.wait_ge(centred.sem, centred.base + ft + 1)
                    chain(stt(YS[:, 0, :], YS[:, 1, :], col(par["lng"], ft), VAR[:, 0:SEQ], ALU.mult, ALU.mult))
                    dve.wait_ge(bonus.sem, bonus.base + ft + 1)
                    chain(tt(BON[:, :], ps[:, 3, :], V[:, 0:SEQ], ALU.mult))
                    chain(stt(YS[:, 0, :], YS[:, 0, :], col(par["lnb"], ft), BON[:, :], ALU.add, ALU.add))
                    tt(tile(dst, ft), YS[:, 0, :], G[:, :], ALU.mult).then_inc(pair_done.sem, 1)
                    assert chain.steps == VSTEPS, chain.steps



COLUMNS = (
    ("ada_b0", 48), ("ada_b1", 48), ("b_ada_2", 48), ("norm_g", 2 * 4 * DT), ("ev_pool_scale", 4),
    ("rw_mu", 6 * DT), ("rw_w0", 2 * DT), ("rw_a0", 2 * DT), ("rw_kk", DT), ("rw_ka", DT), ("rw_rk", DT),
    ("rw_lng", DT), ("rw_lnb", DT), ("g_mix", DT), ("g_q_lat", 4), ("g_kv_lat", 2), ("g_q_head", 1),
    ("g_k_head", 1), ("g_dil_q", 1), ("g_dil_k", 1), ("g_ffn", DT), ("taps", 3 * 2 * FT2), ("b_conv", 2 * FT2),
)
CONSTANTS = (
    ("ident", P), ("ones", P), ("head_sum", P), ("head_mean", P), ("mla_mean", MLA_QK), ("mla_rotate", MLA_QK),
    ("dil_rotate", P), ("freqs", 2),
)
LEVELS = tuple(2 ** i for i in range(1, CHUNK.bit_length() - 1))
WKV_MASKS = ("strict", "inclusive", "minus_first", "minus_first_t", "ident") + LEVELS


def offsets(table):
    at, out = 0, {}
    for name, n in table:
        out[name] = (at, at + n)
        at += n
    return out, at


def load_all(core, pairs):
    landed = counter(core, "input_landed")
    with core.block() as block:
        @block.sync
        def _(sp):
            for dst, src in pairs:
                sp.dma_start(dst, src).then_inc(landed.sem, 16)
            sp.wait_ge(landed.sem, landed.base + 16 * len(pairs))
    landed.base += 16 * len(pairs)


def silu_rows(core, rows):
    nc = core.nc
    sigmoid, done = counter(core, "silu_sigmoid"), counter(core, "silu_done")
    with ExitStack() as scope:
        s = core.sb(scope, "silu_s", [P, len(rows), D])
        with core.block() as block:
            @block.scalar
            def _(eng):
                for n, row in enumerate(rows):
                    nc.scalar.activation(s[:, n, :], row, ACT.Sigmoid).then_inc(sigmoid.sem, 1)

            @block.vector
            def _(dve):
                for n, row in enumerate(rows):
                    dve.wait_ge(sigmoid.sem, sigmoid.base + n + 1)
                    nc.vector.tensor_tensor(row, row, s[:, n, :], ALU.mult).then_inc(done.sem, 1)
    sigmoid.base += len(rows)
    done.base += len(rows)


def gains(core, jobs):
    nc = core.nc
    done = counter(core, "gain_done")
    with core.block() as block:
        @block.vector
        def _(dve):
            for out, scale, gain, plus in jobs:
                nc.vector.scalar_tensor_tensor(out, scale, plus, gain, ALU.add, ALU.mult).then_inc(done.sem, 1)
    done.base += len(jobs)


def even_heads(core, q, k, v, queries, q0, out, bias_tile=None, bias_dram=None):
    heads = []
    ctx_tile = SEQ // P
    for h in range(8):
        rows = slice(h % 2 * HEAD, h % 2 * HEAD + HEAD)
        t = h // 2
        ctx_keys = k[rows, t, SEQ:T0]
        cols = slice(h * HEAD, (h + 1) * HEAD)
        if bias_tile is None:
            heads.append(Head(q[rows, t, q0:q0 + queries], queries, [ctx_keys],
                              lambda kt, cols=cols: v[:, ctx_tile + kt, cols],
                              Rows(out[rows, t, q0:q0 + queries], rows.start), HEAD ** -0.5))
        else:
            heads.append(Head(q[rows, t, q0:q0 + queries], queries, [k[rows, t, 0:SEQ], ctx_keys],
                              lambda kt, cols=cols: v[:, kt, cols],
                              Rows(out[rows, t, q0:q0 + queries], rows.start), HEAD ** -0.5,
                              bias=lambda i, h=h: bias_tile[:, h % 2, (6 - 2 * i) * GRID_W:(14 - 2 * i) * GRID_W],
                              bias_load=bias_dram[h, :, :]))
    return heads


def build(nc, io, stop=None):
    core = Core(nc)
    col_at, n_cols = offsets(COLUMNS)
    con_at, n_cons = offsets(CONSTANTS)
    scope = ExitStack()
    with scope:
        cols = core.sb(scope, "columns", [P, n_cols])
        cons = core.sb(scope, "constants", [P, n_cons])
        X = core.sb(scope, "residual", [P, DT, T0])
        mods = {name: core.sb(scope, f"mod_{name}", [P, N_MOD * DT]) for name in ("0x", "0c", "1x", "1c", "2x")}
        derived = core.sb(scope, "derived_gains", [P, 14, DT])

        def column(name, a=0, n=None):
            lo, hi = col_at[name]
            return cols[:, lo + a:hi if n is None else lo + a + n]

        def const(name):
            lo, hi = con_at[name]
            return cons[:, lo:hi]

        core.ident, core.ones = const("ident"), const("ones")
        core.head_sum, core.head_mean = const("head_sum"), const("head_mean")

        credit = [counter(core, n) for n in ("panel_done", "panel_evicted", "mod_panel_used", "gate_done", "pair_done",
                                           "triangle_kept_0", "triangle_kept_1", "factor_kept_0", "factor_kept_1")]
        with core.block() as block:
            @block.vector
            def _(dve):
                for i, s in enumerate(credit):
                    nc.vector.memset(derived[:, i, :], 0.0).then_inc(s.sem, CREDIT)
        for s in credit:
            s.base += CREDIT

        load_all(core, [(cols[:, :], io["columns"]), (cons[:, :], io["constants"]),
                        (X[:, :, 0:SEQ], io["x"].rearrange("(k p) t -> p k t", p=P)),
                        (X[:, :, SEQ:T0], io["ctx"].rearrange("(k p) t -> p k t", p=P))])

        with ExitStack() as s:
            rows = core.sb(s, "conditions", [P, 3, D])
            load_all(core, [(rows[:, n, :], io[name].to_broadcast([P, D]))
                            for n, name in enumerate(("c", "c_ctx", "c_2"))])
            silu_rows(core, [rows[:, n, :] for n in range(3)])
            c, cc, c2 = (rows[:, n, :] for n in range(3))
            modulation(core, io["ada0"], column("ada_b0"), [c, cc], [mods["0x"], mods["0c"]])
            modulation(core, io["ada1"], column("ada_b1"), [c, cc], [mods["1x"], mods["1c"]])
            modulation(core, io["ada2"], column("b_ada_2"), [c2], [mods["2x"]])

        def mod(which, n):
            return mods[which][:, n * DT:(n + 1) * DT]

        def norm_g(layer, n):
            return column("norm_g", (4 * layer + n) * DT, DT)

        jobs, at = [], {}
        for key, which, n, gain, plus in (
                ("0x in", "0x", 1, norm_g(0, 0), 1.0), ("0c in", "0c", 1, norm_g(0, 0), 1.0),
                ("0x mix", "0x", 2, norm_g(0, 1), 0.0), ("0c mix", "0c", 2, norm_g(0, 1), 0.0),
                ("0x mlp", "0x", 4, norm_g(0, 2), 1.0), ("0c mlp", "0c", 4, norm_g(0, 2), 1.0),
                ("0x out", "0x", 5, norm_g(0, 3), 0.0), ("0c out", "0c", 5, norm_g(0, 3), 0.0),
                ("1x in", "1x", 1, norm_g(1, 0), 1.0), ("1c in", "1c", 1, norm_g(1, 0), 1.0),
                ("1x mix", "1x", 2, norm_g(1, 1), 0.0), ("1x mlp", "1x", 4, norm_g(1, 2), 1.0),
                ("1x out", "1x", 5, norm_g(1, 3), 0.0), ("2x in", "2x", 1, column("g_mix"), 1.0)):
            at[key] = derived[:, len(jobs), :]
            jobs.append((at[key], mod(which, n), gain, plus))
        gains(core, jobs)

        def both(key):
            return [(0, SEQ, at[f"0x {key}"]), (SEQ, T0, at[f"0c {key}"])]

        def evict_copy(dst):
            return lambda n, psum: nc.scalar.activation(
                halves(tile(dst, n)) if dst.shape[-1] == T0 else tile(dst, n), psum, ACT.Copy)

        def mlp(w1, w2, tokens, act, hidden_scope, out):
            hidden = core.sb(hidden_scope, "hidden", [P, D_FF // P, tokens])

            def shaped(ap):
                return halves(ap) if tokens > 512 else ap

            gemm(core, w1, DT, D_FF // P, act, tokens,
                 act_evict=lambda n, psum: nc.scalar.activation(shaped(tile(hidden, n)), psum, ACT.Relu),
                 dve_evict=lambda n, psum, chain: nc.vector.tensor_tensor(shaped(tile(hidden, n)), psum,
                                                                          shaped(tile(hidden, n)), ALU.mult))
            gemm(core, w2, D_FF // P, DT, hidden, tokens, ring=2,
                 act_evict=lambda n, psum: nc.scalar.activation(shaped(tile(out, n)), psum, ACT.Copy))

        def finished(name):
            if stop != name:
                return False
            store(core, X[:, :, 0:SEQ], io["out"])
            return True

        with ExitStack() as s:
            H = core.sb(s, "h", [P, DT, T0])
            rms_stage(core, X, DT, T0, both("in"), [(0, SEQ, mod("0x", 0)), (SEQ, T0, mod("0c", 0))], H)
            with ExitStack() as s2:
                U = core.sb(s2, "u", [P, 12, T0])
                V = core.sb(s2, "v", [P, T0 // P, 512])
                CAT = core.sb(s2, "mixed", [P, DT, T0])
                gemm(core, io["w_in"], DT, 12, H, T0, act_evict=evict_copy(U))
                gemm_tokens(core, io["w_in_v"], DT, H, T0 // P, V)
                with ExitStack() as s3:
                    inv = core.sb(s3, "inverse_counts", [P, len(POOL_WINDOWS), T0])
                    load_all(core, [(inv[:, :, :], io["inv_count"].unsqueeze(0).to_broadcast([P, len(POOL_WINDOWS), T0]))])
                    pool_mixer(core, U, io["pool_w"], inv, column("ev_pool_scale"), CAT)
                with ExitStack() as s3:
                    bias = core.sb(s3, "grid_bias", [P, 2, 14 * GRID_W])
                    grid_mask = core.sb(s3, "grid_mask", [P, GRID_W])
                    load_all(core, [(grid_mask[:, :], io["grid_mask"])])
                    q, k = U[:, 4:8, :], U[:, 8:12, :]
                    attention(core, even_heads(core, q, k, V, SEQ, 0, CAT[:, 4:8, :], bias, io["bias"]), bias,
                              grid_mask[:, :].unsqueeze(1).to_broadcast([P, 14, GRID_W]))
                    attention(core, even_heads(core, q, k, V, CTX, SEQ, CAT[:, 4:8, :]))
                gemm(core, io["w_out"], DT, DT, CAT, T0, act_evict=evict_copy(H))
            rms_stage(core, H, DT, T0, both("mix"), residual=X)
            if finished("mix0"):
                return
            rms_stage(core, X, DT, T0, both("mlp"), [(0, SEQ, mod("0x", 3)), (SEQ, T0, mod("0c", 3))], H)
            with ExitStack() as s2:
                mlp(io["mlp_w1_0"], io["mlp_w2_0"], T0, H, s2, H)
            rms_stage(core, H, DT, T0, both("out"), residual=X)
        if finished("layer0"):
            return

        names = ("k", "v", "r", "g")
        dram = {n: nc.dram_tensor(f"spilled_{n}", [DT, P, T0 if n in "kv" else SEQ], F32, kind="Internal").ap()
                for n in names + ("x",)}
        with ExitStack() as s0:
            LA = core.sb(s0, "lora_inputs", [P, 2, T0])
            ZT = core.sb(s0, "wkv_out", [P, DT, SEQ])
            segs = ((0, SEQ), (SEQ, T0))
            with ExitStack() as s:
                H = core.sb(s, "h", [P, DT, T0])
                M = core.sb(s, "mixed_tokens", [P, DT, T0])
                Y = core.sb(s, "projected", [P, DT, T0])
                rms_stage(core, X, DT, T0, [(0, SEQ, at["1x in"]), (SEQ, T0, at["1c in"])],
                          [(0, SEQ, mod("1x", 0)), (SEQ, T0, mod("1c", 0))], H)
                spill(core, X[:, :, 0:SEQ], dram["x"])
                for j, name, w in ((0, "r", "rw_wr"), (2, "k", "rw_wk"), (3, "v", "rw_wv")):
                    tokens = SEQ if name == "r" else T0
                    token_mix(core, H, segs, column("rw_mu", j * DT, DT), M, T0)
                    gemm(core, io[w], DT, DT, M[:, :, 0:tokens], tokens, act_evict=evict_copy(Y[:, :, 0:tokens]))
                    spill(core, Y[:, :, 0:tokens], dram[name])
                for j, w, n, func in ((1, "rw_w1", 0, ACT.Tanh), (4, "rw_a1", 1, ACT.Copy)):
                    token_mix(core, H, segs, column("rw_mu", j * DT, DT), M, T0)
                    gemm(core, io[w], DT, 1, M, T0, act_evict=lambda _, psum, n=n, func=func: nc.scalar.activation(
                        halves(LA[:, n, :]), psum, func))
                token_mix(core, H, segs, column("rw_mu", 5 * DT, DT), M, T0)
                gemm(core, io["rw_g1"], DT, 1, M[:, :, 0:SEQ], SEQ, act_evict=lambda n, psum: nc.scalar.activation(
                    Y[:, DT - 1, 0:SEQ], psum, ACT.Sigmoid))
                gemm(core, io["rw_g2"], 1, DT, Y[:, DT - 1:DT, 0:SEQ], SEQ, act_evict=evict_copy(M[:, :, 0:SEQ]))
                spill(core, M[:, :, 0:SEQ], dram["g"])
            with ExitStack() as s:
                tall = core.sb(s, "wkv_masks", [P, len(WKV_MASKS), 2 * P])
                resets = core.sb(s, "wkv_resets", [P, T0])
                load_all(core, [(tall[:, :, :], io["wkv_masks"]),
                                (resets[:, :], io["wkv_resets"].to_broadcast([P, T0]))])
                masks = {name: tall[:, i, :] for i, name in enumerate(WKV_MASKS)}
                masks["resets"] = resets[:, :]
                par = {"w0": [column("rw_w0", d * DT, DT) for d in range(2)],
                       "a0": [column("rw_a0", d * DT, DT) for d in range(2)],
                       "kk": column("rw_kk"), "ka": column("rw_ka"), "rk": column("rw_rk"),
                       "lng": column("rw_lng"), "lnb": column("rw_lnb")}
                wkv(core, LA[:, 0, :], LA[:, 1, :], io["lora_up"], dram["k"], dram["v"], dram["r"], dram["g"], par,
                    masks, ZT)
            with ExitStack() as s:
                H = core.sb(s, "h", [P, DT, SEQ])
                gemm(core, io["rw_wo"], DT, DT, ZT, SEQ, act_evict=evict_copy(H))
                if stop == "wo1":
                    store(core, H[:, :, 0:SEQ], io["out"])
                    return
                rms_stage(core, H, DT, SEQ, [(0, SEQ, at["1x mix"])], residual=X)
                if finished("mix1"):
                    return
                rms_stage(core, X, DT, SEQ, [(0, SEQ, at["1x mlp"])], [(0, SEQ, mod("1x", 3))], H)
                with ExitStack() as s2:
                    mlp(io["mlp_w1_1"], io["mlp_w2_1"], SEQ, H, s2, H)
                rms_stage(core, H, DT, SEQ, [(0, SEQ, at["1x out"])], residual=X)
        if finished("layer1"):
            return

        ffn_gain = derived[:, 0, :]
        gains(core, [(ffn_gain, mod("2x", 4), column("g_ffn"), 1.0)])
        with ExitStack() as s:
            H = core.sb(s, "h", [P, DT, SEQ])
            MIX = core.sb(s, "mix", [P, DT, SEQ])
            rms_stage(core, X, DT, SEQ, [(0, SEQ, at["2x in"])], [(0, SEQ, mod("2x", 0))], H)
            cs = core.sb(s, "rotation", [P, 2, 2, SEQ])
            rotation_tables(core, io["positions"], const("freqs"),
                            [(cs[:, 0, 0, :], cs[:, 0, 1, :]), (cs[:, 1, 0, :], cs[:, 1, 1, :])])
            with ExitStack() as s2:
                LAT = core.sb(s2, "latents", [P, 6, SEQ])
                QM, KM = core.sb(s2, "q_mla", [P, 8, SEQ]), core.sb(s2, "k_mla", [P, 8, SEQ])
                VM = core.sb(s2, "v_mla", [P, SEQ // P, 512])
                mask = core.sb(s2, "causal_bias", [P, 2, 512])
                load_all(core, [(mask[:, :, :], io["causal_bias"])])
                gemm(core, io["w_lat"], DT, 6, H, SEQ, act_evict=evict_copy(LAT))
                rows = slice(MLA_NOPE, MLA_QK)
                gemm(core, io["w_kpe"], DT, 1, H, SEQ, m=MLA_ROPE, m0=MLA_NOPE, act_evict=lambda n, psum:
                     nc.scalar.activation(KM[rows, :, :], psum.unsqueeze(1).to_broadcast([MLA_ROPE, 8, SEQ]), ACT.Copy))
                rms_stage(core, LAT[:, 0:4, :], 4, SEQ, [(0, SEQ, column("g_q_lat"))], dst=LAT[:, 0:4, :])
                rms_stage(core, LAT[:, 4:6, :], 2, SEQ, [(0, SEQ, column("g_kv_lat"))], dst=LAT[:, 4:6, :])
                gemm(core, io["w_q_b"], 4, 8, LAT[:, 0:4, :], SEQ, m=MLA_QK, act_evict=evict_copy(QM[0:MLA_QK, :, :]))
                gemm(core, io["w_kv_b"], 2, 8, LAT[:, 4:6, :], SEQ, m=MLA_NOPE,
                     act_evict=evict_copy(KM[0:MLA_NOPE, :, :]))
                gemm_tokens(core, io["w_kv_v"], 2, LAT[:, 4:6, :], SEQ // P, VM)
                q96 = slice(0, MLA_QK)
                for t, g in ((QM, "g_q_head"), (KM, "g_k_head")):
                    head_norm(core, t, MLA_QK, 8, const("mla_mean")[q96, :], column(g)[q96, :],
                              const("mla_rotate")[q96, :], cs[q96, 0, 0, :], cs[q96, 0, 1, :])
                attention(core, [Head(QM[0:MLA_QK, h, :], SEQ, [KM[0:MLA_QK, h, :]],
                                      lambda kt, h=h: VM[:, kt, h * HEAD:(h + 1) * HEAD],
                                      Rows(MIX[h % 2 * HEAD:h % 2 * HEAD + HEAD, h // 2, :], h % 2 * HEAD),
                                      MLA_QK ** -0.5, bias=lambda i: mask[:, 0, (3 - i) * P:512], causal=True)
                                 for h in range(8)])
                QD, KD = QM[:, 0:4, :], KM[:, 0:4, :]
                gemm(core, io["w_qd"], DT, 4, H, SEQ, act_evict=evict_copy(QD))
                gemm(core, io["w_kd"], DT, 4, H, SEQ, act_evict=evict_copy(KD))
                gemm_tokens(core, io["w_vd"], DT, H, SEQ // P, VM)
                for t, g in ((QD, "g_dil_q"), (KD, "g_dil_k")):
                    head_norm(core, t, P, 4, const("head_mean"), column(g), const("dil_rotate"),
                              cs[:, 1, 0, :], cs[:, 1, 1, :])
                attention(core, [Head(QD[h % 2 * HEAD:h % 2 * HEAD + HEAD, h // 2, :], SEQ,
                                      [KD[h % 2 * HEAD:h % 2 * HEAD + HEAD, h // 2, :]],
                                      lambda kt, h=h: VM[:, kt, h * HEAD:(h + 1) * HEAD],
                                      Rows(MIX[h % 2 * HEAD:h % 2 * HEAD + HEAD, 4 + h // 2, :], h % 2 * HEAD),
                                      HEAD ** -0.5, bias=lambda i: mask[:, 1, (3 - i) * P:512], causal=True)
                                 for h in range(8)])
            gate1, gate2 = mod("2x", 2), mod("2x", 5)
            gemm(core, io["w_o"], DT, DT, MIX, SEQ, dve_evict=lambda n, psum, chain: nc.vector.scalar_tensor_tensor(
                tile(X, n)[:, 0:SEQ], psum, col(gate1, n), tile(X, n)[:, 0:SEQ], ALU.mult, ALU.add))
            if finished("mix2"):
                return
            rms_stage(core, X, DT, SEQ, [(0, SEQ, ffn_gain)], [(0, SEQ, mod("2x", 3))], H)
            with ExitStack() as s2:
                G = core.sb(s2, "gated", [P, FT2, SEQ])
                taps = column("taps").rearrange("p (j n) -> p j n", j=3)
                conv_mlp(core, io["w_up"], H, taps, column("b_conv"), G)
                gemm(core, io["w_down"], FT2, DT, G, SEQ, ring=2,
                     dve_evict=lambda n, psum, chain: nc.vector.scalar_tensor_tensor(
                         tile(X, n)[:, 0:SEQ], psum, col(gate2, n), tile(X, n)[:, 0:SEQ], ALU.mult, ALU.add))
        store(core, X[:, :, 0:SEQ], io["out"])


def store(core, src, out):
    stored = counter(core, "output_stored")
    with core.block() as block:
        @block.sync
        def _(sp):
            sp.dma_start(out.rearrange("(k p) t -> p k t", p=P), src).then_inc(stored.sem, 16)
            sp.wait_ge(stored.sem, stored.base + 16)
    stored.base += 16



def panels(w, m=P):
    k, n = w.shape
    return w.reshape(k // P, P, n // m, m).transpose(2, 1, 0, 3).reshape(n // m, P, k // P * m)


def columns(v):
    return v.reshape(-1, P).T


def padded_column(v):
    out = np.zeros((P, 1), v.dtype)
    out[:len(v), 0] = v
    return out


def constants():
    f = np.float32
    out = {"ident": np.eye(P, dtype=f), "ones": np.ones((P, P), f)}
    head = np.kron(np.eye(2, dtype=f), np.ones((HEAD, HEAD), f))
    out["head_sum"], out["head_mean"] = head, head / f(HEAD)
    mean = np.zeros((P, MLA_QK), f)
    mean[:MLA_NOPE, :MLA_NOPE] = 1 / MLA_NOPE
    mean[MLA_NOPE:MLA_QK, MLA_NOPE:] = 1 / MLA_ROPE
    out["mla_mean"] = mean

    def rotate(size, start, n):
        m = np.zeros((P, n), f)
        for j in range(size // 2):
            m[start + j + size // 2, start + j] = -1
            m[start + j, start + j + size // 2] = 1
        return m

    out["mla_rotate"] = rotate(MLA_ROPE, MLA_NOPE, MLA_QK)
    out["dil_rotate"] = rotate(HEAD, 0, P) + rotate(HEAD, HEAD, P)

    def freqs(d):
        half = d // 2
        e = (f(-2.0) * np.arange(half, dtype=f)) / f(d)
        return np.tile(np.power(f(ROPE_THETA), e).astype(f), 2)

    fr = np.zeros((P, 2), f)
    fr[MLA_NOPE:MLA_QK, 0] = freqs(MLA_ROPE)
    fr[:, 1] = np.tile(freqs(HEAD), 2)
    out["freqs"] = fr
    return np.concatenate([out[n] for n, _ in CONSTANTS], axis=1)


def inverse_counts():
    out = np.zeros((len(POOL_WINDOWS), T0), np.float32)
    for g, w in enumerate(POOL_WINDOWS):
        for t0, n in ((0, SEQ), (SEQ, CTX)):
            t = np.arange(n)
            out[g, t0:t0 + n] = 1.0 / (np.clip(t + w // 2, 0, n) - np.clip(t - w // 2, 0, n))
    return out


def grid_columns():
    c = np.arange(GRID_W)
    start = np.clip(c - WIN_C // 2, 0, GRID_W - WIN_C)
    ok = (c[None, :] >= start[:, None]) & (c[None, :] < start[:, None] + WIN_C)
    return np.tile(np.where(ok, 0, NEG).astype(np.float32), (2, 1))


def grid_bias(rpb):
    c = np.arange(GRID_W)
    dc = np.clip(c[None, :] - c[:, None], -(WIN_C - 1), WIN_C - 1) + WIN_C - 1
    full = rpb[:, :, dc].transpose(0, 2, 1, 3)
    return np.concatenate([full[:, :, 1:15], full[:, :, 0:14]], axis=1).reshape(rpb.shape[0], P, 14 * GRID_W)


def causal_biases():
    q = np.arange(P)[:, None]
    k = np.arange(512)[None, :] - 3 * P
    dist = q - k
    causal = np.where(dist >= 0, 0.0, NEG)
    count = sum(((dist >= 0) & (dist % dil == 0) & (dist // dil <= window // dil)).astype(int)
                for window, dil in DIL_PATTERNS)
    dil = np.where(count > 0, np.log(np.maximum(count, 1)), NEG)
    return np.stack([causal, dil], axis=1).astype(np.float32)


def wkv_masks():
    i, j = np.arange(P)[:, None], np.arange(P)[None, :]
    same = i // CHUNK == j // CHUNK

    def level(n):
        return (i // (2 * n) == j // (2 * n)) & (i // n > j // n)

    both = {"strict": (same & (i < j), same & (i > j)), "inclusive": (same & (i <= j), same & (i >= j)),
            "minus_first": (-1.0 * level(1), -1.0 * level(1).T), "minus_first_t": (-1.0 * level(1).T, -1.0 * level(1)),
            "ident": (i == j, i == j)}
    for n in LEVELS:
        both[n] = (level(n), level(n).T)
    return np.stack([np.concatenate(both[n], axis=1) for n in WKV_MASKS], axis=1).astype(np.float32)


def lay_out(i):
    f = {k: np.asarray(v) for k, v in i.items()}
    win, win2 = f["ev_w_in"][0], f["w_in_2"][0]
    taps = f["w_conv_2"][0].reshape(3, 2, FT2, P).transpose(0, 2, 1, 3).reshape(-1)
    bconv = f["b_conv_2"][0].reshape(2, FT2, P).transpose(1, 0, 2).reshape(-1)
    col = {
        "ada_b0": f["ada_b"][0], "ada_b1": f["ada_b"][1], "b_ada_2": f["b_ada_2"][0], "norm_g": f["norm_g"],
        "ev_pool_scale": f["ev_pool_scale"], "rw_mu": f["rw_mu"], "rw_w0": f["rw_w0"], "rw_a0": f["rw_a0"],
        "rw_kk": f["rw_kk"], "rw_ka": f["rw_ka"], "rw_rk": f["rw_rk"], "rw_lng": f["rw_lng"], "rw_lnb": f["rw_lnb"],
        "g_mix": f["g_mix_norm_2"], "g_q_lat": f["g_q_lat_2"], "g_kv_lat": f["g_kv_lat_2"],
        "g_q_head": np.concatenate([f["g_mla_q_nope_2"][0], f["g_mla_q_pe_2"][0]]),
        "g_k_head": np.concatenate([f["g_mla_k_nope_2"][0], f["g_mla_k_pe_2"][0]]),
        "g_dil_q": np.tile(f["g_dil_q_2"][0], 2), "g_dil_k": np.tile(f["g_dil_k_2"][0], 2), "g_ffn": f["g_ffn_norm_2"],
        "taps": taps, "b_conv": bconv,
    }
    cols = [padded_column(col[n].reshape(-1)) if col[n].size < P else columns(col[n].reshape(-1)) for n, _ in COLUMNS]
    q0 = Q_LORA + KV_LORA
    d0 = q0 + MLA_ROPE
    qb = f["w_q_b_2"][0]
    kvb = f["w_kv_b_2"][0].reshape(KV_LORA, MLA_HEADS, 2 * HEAD)
    up = f["w_up_2"][0].reshape(D, 2, FT2, P).transpose(0, 2, 1, 3).reshape(D, 2 * D_FF2)
    lora_up = np.concatenate([f["rw_w2"][0].reshape(P, DT, P), f["rw_a2"][0].reshape(P, DT, P)], axis=2).transpose(1, 0, 2)
    token_weights = lambda w: w.reshape(-1, P, 512).transpose(1, 0, 2).reshape(P, -1)
    out = {
        "x": f["x"][0].T, "ctx": f["ctx"][0].T, "c": f["c"].reshape(1, D), "c_ctx": f["c_ctx"].reshape(1, D),
        "c_2": f["c_2"].reshape(1, D), "positions": f["positions_2"].reshape(1, SEQ),
        "columns": np.concatenate(cols, axis=1), "constants": constants(),
        "ada0": f["ada_w"][0].T.reshape(48, P, D), "ada1": f["ada_w"][1].T.reshape(48, P, D),
        "ada2": f["w_ada_2"][0].T.reshape(48, P, D),
        "w_in": panels(win[:, 0:1536]), "w_in_v": token_weights(win[:, 1536:]), "w_out": panels(f["ev_w_out"][0]),
        "pool_w": f["ev_pool_w"][0], "inv_count": inverse_counts(), "grid_mask": grid_columns(),
        "bias": grid_bias(f["ev_rpb"][0]),
        "mlp_w1_0": panels(f["mlp_w1"][0]), "mlp_w2_0": panels(f["mlp_w2"][0]),
        "mlp_w1_1": panels(f["mlp_w1"][1]), "mlp_w2_1": panels(f["mlp_w2"][1]),
        "rw_wr": panels(f["rw_wr"][0]), "rw_wk": panels(f["rw_wk"][0]), "rw_wv": panels(f["rw_wv"][0]),
        "rw_wo": panels(f["rw_wo"][0]),
        "rw_w1": panels(np.concatenate([f["rw_w1"][0, 0], f["rw_w1"][0, 1]], axis=1)),
        "rw_a1": panels(np.concatenate([f["rw_a1"][0, 0], f["rw_a1"][0, 1]], axis=1)),
        "rw_g1": panels(f["rw_g1"][0]), "rw_g2": panels(f["rw_g2"][0]), "lora_up": lora_up,
        "wkv_masks": wkv_masks(), "wkv_resets": (np.arange(T0) % CHUNK != 0).astype(np.float32).reshape(1, T0),
        "w_lat": panels(win2[:, 0:q0]), "w_kpe": panels(win2[:, q0:d0], MLA_ROPE),
        "w_q_b": panels(qb, MLA_QK), "w_kv_b": panels(kvb[:, :, :MLA_NOPE].reshape(KV_LORA, -1), MLA_NOPE),
        "w_kv_v": token_weights(kvb[:, :, MLA_NOPE:].reshape(KV_LORA, -1)),
        "w_qd": panels(win2[:, d0:d0 + 512]), "w_kd": panels(win2[:, d0 + 512:d0 + 1024]),
        "w_vd": token_weights(win2[:, d0 + 1024:]), "causal_bias": causal_biases(),
        "w_o": panels(f["w_o_2"][0]), "w_up": panels(up), "w_down": panels(f["w_down_2"][0]),
    }
    return {k: np.ascontiguousarray(v) for k, v in out.items()}


def kernel(**inputs):
    import concourse.bacc as bacc
    from concourse.bass_utils import run_bass_kernel_spmd

    arrays = lay_out(inputs)
    nc = bacc.Bacc("TRN2", target_bir_lowering=False, num_devices=1)
    io = {n: nc.dram_tensor(f"in_{n}", a.shape, mybir.dt.from_np(a.dtype), kind="ExternalInput").ap()
          for n, a in arrays.items()}
    io["out"] = nc.dram_tensor("out", (D, SEQ), F32, kind="ExternalOutput").ap()
    build(nc, io)
    result = run_bass_kernel_spmd(nc, [{f"in_{n}": a for n, a in arrays.items()}], core_ids=[0])
    return np.ascontiguousarray(result.results[0]["out"].T).reshape(1, SEQ, D)
```

```python
from contextlib import ExitStack

import numpy as np

import concourse.bass as bass
from concourse import mybir

F32 = mybir.dt.float32
I32 = mybir.dt.int32
ALU = mybir.AluOpType
ACT = mybir.ActivationFunctionType
AX = mybir.AxisListType

P = 128
D = 1024
SEQ = 512
CTX = 256
T0 = SEQ + CTX
DT = D // P
N_MOD = 6
EPS = 1e-6
CREDIT = 16

POOL_WINDOWS = (2, 4, 8, 16)
D_FF = 4 * D
HEAD = 64
GRID_W = 64
WIN_R, WIN_C = 8, 16
ROWS = SEQ // GRID_W
NEG = -1e30

D_FF2 = 2816
FT2 = D_FF2 // P
MLA_HEADS, MLA_NOPE, MLA_ROPE = 8, 64, 32
MLA_QK = MLA_NOPE + MLA_ROPE
Q_LORA, KV_LORA = 512, 256
DIL_PATTERNS = ((128, 1), (512, 4), (2048, 16))
ROPE_THETA = 10000.0

RW_HEADS = D // HEAD
GN_EPS = 64e-5
CHUNK = 64
DECAY_SCALE = float(np.exp(-0.5))
LEVELS = tuple(2 ** i for i in range(1, CHUNK.bit_length() - 1))


class Signal:

    def __init__(self, nc, name):
        self.sem = nc.alloc_semaphore(name)
        self.base = 0


class Core:

    def __init__(self, nc):
        self.nc = nc
        self.counters = {}
        self.stages = 0
        self.psum = nc.alloc_psum_tensor("psum", [P, 8, 512], F32)

    def block(self):
        self.stages += 1
        return self.nc.Block(no_gpsimd_drain=True)

    def sb(self, scope, name, shape, dtype=F32):
        self.stages += 1
        return scope.enter_context(self.nc.sbuf_tensor(f"{name}_{self.stages}", shape, dtype))


def counter(core, name):
    if name not in core.counters:
        core.counters[name] = Signal(core.nc, name)
    return core.counters[name]


class Chain:

    def __init__(self, eng, signal, start):
        self.eng, self.counter, self.start, self.steps = eng, signal, start, 0

    def __call__(self, instruction):
        self.steps += 1
        instruction.then_inc(self.counter.sem, 1)
        self.eng.wait_ge(self.counter.sem, self.start + self.steps)


def tile(ap, n):
    if isinstance(n, int):
        return ap[:, n, :]
    return ap[:, bass.ds(n, 1), :].rearrange("p a t -> p (a t)")


def col(ap, n):
    return ap[:, n:n + 1] if isinstance(n, int) else ap[:, bass.ds(n, 1)]


def halves(ap):
    return ap.rearrange("p (a t) -> p a t", a=2)



def gemm(core, weights, kt, nt, act, tokens, act_evict=None, dve_evict=None, m=P, m0=0, kp=P, k0=0,
         dve_steps=0, ring=4, bufs=4, store=None, load_also=None, vector_also=None):
    nc = core.nc
    wide = tokens > 512
    landed = [counter(core, f"panel_landed_{s}") for s in range(4)]
    done, evicted, first = counter(core, "panel_done"), counter(core, "panel_evicted"), counter(core, "panel_first_evict")
    steps = counter(core, "gemm_vector_step")
    looped = nt % 4 == 0 and nt > 4
    landed_base = [s.base for s in landed]
    stored = [counter(core, f"panel_stored_{s}") for s in range(2)]

    def place(n):
        s = n % bufs
        if wide:
            return core.psum[m0:m0 + m, 2 * s:2 * s + 2, 0:tokens // 2]
        return core.psum[m0:m0 + m, s, 0:tokens]

    def panels(eng, ring=ring):
        if looped:
            with eng.Fori(0, nt // 4) as blk:
                for u in range(4):
                    yield blk * 4 + u, u, blk * (4 // ring) + u // ring
        else:
            for n in range(nt):
                yield n, n, n // ring

    with ExitStack() as scope:
        panel = core.sb(scope, "panels", [P, ring, kt * m])
        staged = core.sb(scope, "staged", [P, 2, tokens]) if store is not None else None
        with core.block() as block:
            @block.sync
            def _(sp):
                for n, u, turn in panels(sp):
                    sp.wait_ge(done.sem, done.base + n + 1 - ring)
                    src = weights[n, :, :] if isinstance(n, int) else \
                        weights[bass.ds(n, 1), :, :].rearrange("a p k -> p (a k)")
                    sp.dma_start(panel[k0:k0 + kp, u % ring, :], src).then_inc(landed[u % ring].sem, 16)
                    if load_also is not None:
                        load_also(sp, n, u)

            @block.tensor
            def _(pe):
                for n, u, turn in panels(pe):
                    pe.wait_ge(landed[u % ring].sem, landed_base[u % ring] + 16 * (turn + 1))
                    pe.wait_ge(evicted.sem, evicted.base + n + 1 - bufs)
                    out = place(u)
                    for k in range(kt):
                        w = panel[k0:k0 + kp, u % ring, k * m:(k + 1) * m]
                        if wide:
                            for a in range(2):
                                last = nc.tensor.matmul(out[:, a, :], w, act[:, k, a * tokens // 2:(a + 1) * tokens // 2],
                                                        start=k == 0, stop=k == kt - 1)
                        else:
                            last = nc.tensor.matmul(out, w, act[:, k, :], start=k == 0, stop=k == kt - 1)
                    last.then_inc(done.sem, 1)

            if act_evict is not None:
                @block.scalar
                def _(eng):
                    for n, u, turn in panels(eng):
                        eng.wait_ge(done.sem, done.base + n + 1)
                        act_evict(n, place(u)).then_inc(first.sem if dve_evict else evicted.sem, 1)

            if store is not None:
                @block.scalar
                def _(eng):
                    for n, u, pair in panels(eng, 2):
                        eng.wait_ge(done.sem, done.base + n + 1)
                        eng.wait_ge(stored[u % 2].sem, stored[u % 2].base + 16 * pair)
                        o = staged[:, u % 2, :]
                        nc.scalar.activation(halves(o) if wide else o, place(u), ACT.Copy).then_inc(evicted.sem, 1)
                        eng.wait_ge(evicted.sem, evicted.base + n + 1)
                        eng.dma_start(store[n, :, :] if isinstance(n, int) else
                                      store[bass.ds(n, 1), :, :].rearrange("a p t -> p (a t)"), o)\
                            .then_inc(stored[u % 2].sem, 16)
                    for slot in range(2):
                        eng.wait_ge(stored[slot].sem, stored[slot].base + 16 * (nt // 2))

            if vector_also is not None:
                @block.vector
                def _(dve):
                    vector_also(dve)

            if dve_evict is not None:
                @block.vector
                def _(dve):
                    for n, u, turn in panels(dve):
                        if act_evict is not None:
                            dve.wait_ge(first.sem, first.base + n + 1)
                        else:
                            dve.wait_ge(done.sem, done.base + n + 1)
                        chain = Chain(dve, steps, steps.base + n * dve_steps)
                        dve_evict(n, place(u), chain).then_inc(evicted.sem, 1)
                        assert chain.steps == dve_steps

    for s in range(ring):
        landed[s].base += 16 * len(range(s, nt, ring))
    if store is not None:
        for slot in range(2):
            stored[slot].base += 16 * (nt // 2)
    done.base += nt
    evicted.base += nt
    if act_evict is not None and dve_evict is not None:
        first.base += nt
    steps.base += nt * dve_steps


def gemm_tokens(core, weights, kt, act, tiles, dst):
    nc = core.nc
    landed, done, out = counter(core, "value_weights_landed"), counter(core, "panel_done"), counter(core, "panel_evicted")
    with ExitStack() as scope:
        w = core.sb(scope, "value_weights", [P, kt * 512])
        with core.block() as block:
            @block.sync
            def _(sp):
                sp.dma_start(w[:, :], weights).then_inc(landed.sem, 16)

            @block.tensor
            def _(pe):
                pe.wait_ge(landed.sem, landed.base + 16)
                for t in range(tiles):
                    pe.wait_ge(out.sem, out.base + t + 1 - 8)
                    for k in range(kt):
                        last = nc.tensor.matmul(core.psum[:, t % 8, :], act[:, k, t * P:(t + 1) * P],
                                                w[:, k * 512:(k + 1) * 512], start=k == 0, stop=k == kt - 1)
                    last.then_inc(done.sem, 1)

            @block.scalar
            def _(eng):
                for t in range(tiles):
                    eng.wait_ge(done.sem, done.base + t + 1)
                    nc.scalar.activation(dst[:, t, :], core.psum[:, t % 8, :], ACT.Copy).then_inc(out.sem, 1)
    landed.base += 16
    done.base += tiles
    out.base += tiles



def rms_stage(core, src, kt, tokens, scales, shifts=None, dst=None, residual=None, eps=EPS):
    nc = core.nc
    squared, summed = counter(core, "norm_squared"), counter(core, "norm_summed")
    inverted, rooted = counter(core, "norm_inverted"), counter(core, "norm_rooted")
    scaled, finished = counter(core, "norm_scaled"), counter(core, "norm_finished")
    steps = counter(core, "norm_vector_step")
    nb = 2 if tokens > 512 else 1
    width = tokens // nb
    with ExitStack() as scope:
        sq = core.sb(scope, "norm_sq", [P, 2, tokens])
        var = core.sb(scope, "norm_var", [P, tokens])
        inv = core.sb(scope, "norm_inv", [P, tokens])
        rstd = core.sb(scope, "norm_rstd", [P, tokens])
        tmp = core.sb(scope, "norm_tmp", [P, 2, tokens])
        total = core.psum[:, 0:nb, 0:width]

        def by_bank(ap):
            return ap.rearrange("p (a t) -> p a t", a=nb)

        with core.block() as block:
            @block.scalar
            def _(eng):
                for k in range(kt):
                    if k >= 2:
                        eng.wait_ge(summed.sem, summed.base + k - 1)
                    nc.scalar.activation(sq[:, k % 2, :], src[:, k, 0:tokens], ACT.Square).then_inc(squared.sem, 1)
                eng.wait_ge(inverted.sem, inverted.base + 1)
                nc.scalar.activation(rstd[:, :], inv[:, :], ACT.Sqrt).then_inc(rooted.sem, 1)
                if shifts is not None:
                    for k in range(kt):
                        eng.wait_ge(scaled.sem, scaled.base + k + 1)
                        for t0, t1, c in shifts:
                            last = nc.scalar.activation(dst[:, k, t0:t1], tmp[:, k % 2, t0:t1], ACT.Identity,
                                                        bias=col(c, k))
                        last.then_inc(finished.sem, 1)

            @block.tensor
            def _(pe):
                for k in range(kt):
                    pe.wait_ge(squared.sem, squared.base + k + 1)
                    for a in range(nb):
                        last = nc.tensor.matmul(total[:, a, :], core.ones[:, :], sq[:, k % 2, a * width:(a + 1) * width],
                                                start=k == 0, stop=k == kt - 1)
                    last.then_inc(summed.sem, 1)

            @block.vector
            def _(dve):
                chain = Chain(dve, steps, steps.base)
                dve.wait_ge(summed.sem, summed.base + kt)
                chain(nc.vector.tensor_scalar(by_bank(var[:, :]), total, 1.0 / (kt * P), eps, ALU.mult, ALU.add))
                nc.vector.reciprocal(inv[:, :], var[:, :]).then_inc(inverted.sem, 1)
                dve.wait_ge(rooted.sem, rooted.base + 1)
                for k in range(kt):
                    if k >= 2 and (shifts is not None or residual is not None):
                        dve.wait_ge(finished.sem, finished.base + k - 1)
                    for t0, t1, c in scales:
                        o = dst[:, k, t0:t1] if shifts is None and residual is None else tmp[:, k % 2, t0:t1]
                        last = nc.vector.scalar_tensor_tensor(o, src[:, k, t0:t1], col(c, k), rstd[:, t0:t1],
                                                              ALU.mult, ALU.mult)
                    last.then_inc(scaled.sem, 1)

            if residual is not None:
                @block.gpsimd
                def _(pool):
                    for k in range(kt):
                        pool.wait_ge(scaled.sem, scaled.base + k + 1)
                        nc.gpsimd.tensor_tensor(residual[:, k, 0:tokens], residual[:, k, 0:tokens], tmp[:, k % 2, :],
                                                ALU.add).then_inc(finished.sem, 1)
                    pool.wait_ge(finished.sem, finished.base + kt)
    squared.base += kt
    summed.base += kt
    inverted.base += 1
    rooted.base += 1
    steps.base += 1
    scaled.base += kt
    if shifts is not None or residual is not None:
        finished.base += kt



class Modulation:

    def __init__(self, core, scope, weights, ring, junk=None):
        self.core, self.weights, self.ring = core, weights, ring
        self.w = core.sb(scope, "mod_weights", [P, ring, D])
        self.junk = core.sb(scope, "mod_products", [P, D])[:, :] if junk is None else junk
        self.part = core.sb(scope, "mod_part", [P, 2, ring])
        self.landed = [counter(core, f"mod_landed_{s}") for s in range(ring)]
        self.used, self.steps = counter(core, "mod_tile_used"), counter(core, "mod_vector_step")
        self.used_base = self.used.base

    def load(self, sp, tile_, at, slot):
        sp.wait_ge(self.used.sem, self.used_base + at + 1 - self.ring)
        sp.dma_start(self.w[:, slot, :], self.weights[bass.ds(tile_, 1), :, :].rearrange("a p k -> p (a k)"))\
            .then_inc(self.landed[slot].sem, 16)

    def vector(self, dve, first, count, biases, vectors, mods):
        nc, ring, nv = self.core.nc, self.ring, len(vectors)
        per = (nv - 1) * ring + nv
        used, landed, steps = self.used, self.landed, self.steps
        with dve.Fori(0, count // ring) as blk:
            chain = Chain(dve, steps, steps.base + blk * per)
            for u in range(ring):
                dve.wait_ge(landed[u].sem, landed[u].base + 16 * (blk + 1))
                for v in range(nv):
                    ins = nc.vector.tensor_tensor_reduce(
                        out=self.junk, in0=self.w[:, u, :], in1=vectors[v], scale=1.0, scalar=0.0,
                        op0=ALU.mult, op1=ALU.add, accum_out=self.part[:, v, u:u + 1])
                    if v == nv - 1:
                        ins.then_inc(used.sem, 1)
                        dve.wait_ge(used.sem, used.base + blk * ring + u + 1)
                    else:
                        chain(ins)
            for v in range(nv):
                at = bass.ds(blk * ring + first, ring)
                chain(nc.vector.tensor_tensor(mods[v][:, at], self.part[:, v, :], biases[:, at], ALU.add))
            assert chain.steps == per
        for s in range(ring):
            landed[s].base += 16 * (count // ring)
        used.base += count
        steps.base += per * (count // ring)


def modulation(core, weights, first, count, biases, vectors, mods):
    ring = 4
    with ExitStack() as scope:
        m = Modulation(core, scope, weights, ring)
        with core.block() as block:
            @block.sync
            def _(sp):
                with sp.Fori(0, count // ring) as blk:
                    for u in range(ring):
                        m.load(sp, blk * ring + u + first, blk * ring + u, u)

            @block.vector
            def _(dve):
                m.vector(dve, first, count, biases, vectors, mods)



def pool_mixer(core, u, pool_weights, inv_count, scale_cols, dst):
    nc = core.nc
    pad = POOL_WINDOWS[-1] // 2
    x0, c0 = pad, pad + SEQ + pad
    total = c0 + CTX + pad
    groups = len(POOL_WINDOWS)
    landed, done, ready, out = (counter(core, "pool_weights_landed"), counter(core, "panel_done"),
                                counter(core, "pool_ready"), counter(core, "pool_out"))
    zeroed, steps = counter(core, "pool_zeroed"), counter(core, "pool_vector_step")
    n_steps = 0
    with ExitStack() as scope:
        w = core.sb(scope, "pool_w", [P, groups, P])
        padded = core.sb(scope, "pool_padded", [P, total])
        sums = core.sb(scope, "pool_sums", [P, 2, total])
        mean = core.sb(scope, "pool_mean", [P, T0])
        diff = core.sb(scope, "pool_diff", [P, groups, T0])
        with core.block() as block:
            @block.sync
            def _(sp):
                sp.dma_start(w[:, :, :], pool_weights.rearrange("g p k -> p g k")).then_inc(landed.sem, 16)

            @block.gpsimd
            def _(pool):
                nc.gpsimd.memset(padded[:, :], 0.0).then_inc(zeroed.sem, 1)

            @block.vector
            def _(dve):
                nonlocal n_steps
                chain = Chain(dve, steps, steps.base)
                dve.wait_ge(zeroed.sem, zeroed.base + 1)
                for g, window in enumerate(POOL_WINDOWS):
                    chain(nc.vector.tensor_copy(padded[:, x0:x0 + SEQ], u[:, g, 0:SEQ]))
                    chain(nc.vector.tensor_copy(padded[:, c0:c0 + CTX], u[:, g, SEQ:T0]))
                    have, src, slot = 1, padded[:, :], 0
                    while have < window:
                        n = total - 2 * have + 1
                        chain(nc.vector.tensor_tensor(sums[:, slot, 0:n], src[:, 0:n], src[:, have:have + n], ALU.add))
                        src, slot, have = sums[:, slot, :], 1 - slot, 2 * have
                    for t0, t1, at in ((0, SEQ, x0), (SEQ, T0, c0)):
                        lo = at - window // 2
                        chain(nc.vector.tensor_tensor(mean[:, t0:t1], src[:, lo:lo + t1 - t0], inv_count[:, g, t0:t1],
                                                      ALU.mult))
                    nc.vector.tensor_tensor(diff[:, g, :], mean[:, :], u[:, g, :], ALU.subtract).then_inc(ready.sem, 1)
                    dve.wait_ge(ready.sem, ready.base + g + 1)
                n_steps = chain.steps

            @block.tensor
            def _(pe):
                pe.wait_ge(landed.sem, landed.base + 16)
                for g in range(groups):
                    pe.wait_ge(ready.sem, ready.base + g + 1)
                    for a in range(2):
                        last = nc.tensor.matmul(core.psum[:, 2 * g + a, 0:T0 // 2], w[:, g, :],
                                                diff[:, g, a * T0 // 2:(a + 1) * T0 // 2], start=True, stop=True)
                    last.then_inc(done.sem, 1)

            @block.scalar
            def _(eng):
                for g in range(groups):
                    eng.wait_ge(done.sem, done.base + g + 1)
                    nc.scalar.activation(halves(dst[:, g, :]), core.psum[:, 2 * g:2 * g + 2, 0:T0 // 2], ACT.Identity,
                                         scale=col(scale_cols, g)).then_inc(out.sem, 1)
    landed.base += 16
    zeroed.base += 1
    ready.base += groups
    done.base += groups
    out.base += groups
    steps.base += n_steps



class Head:

    def __init__(self, q, queries, keys, values, out, scale, bias=None, causal=False, bias_load=None):
        self.q, self.queries, self.keys, self.values, self.out = q, queries, keys, values, out
        self.scale, self.bias, self.causal, self.bias_load = scale, bias, causal, bias_load
        self.tiles = queries // P
        self.total = sum(k.shape[-1] for k in keys)

    def seen(self, i):
        return (i + 1) * P if self.causal else self.total


def attention(core, heads, bias_tile=None, bias_mask=None):
    nc = core.nc
    ps = core.psum
    scored, biased, exped = counter(core, "att_scored"), counter(core, "att_biased"), counter(core, "att_exped")
    probs, turned, kept = counter(core, "att_probs"), counter(core, "att_turned"), counter(core, "att_kept")
    mixed, out = counter(core, "att_mixed"), counter(core, "att_out")
    steps, peaked = counter(core, "att_vector_step"), counter(core, "att_peaked")
    loaded = [counter(core, f"att_bias_landed_{s}") for s in range(2)]
    units = [(h, i) for h in range(len(heads)) for i in range(heads[h].tiles)]
    last_unit = {h: n for n, (h, i) in enumerate(units)}
    n_steps = 0
    widest = max(h.total for h in heads)
    with ExitStack() as scope:
        s = core.sb(scope, "att_scores", [P, 3, widest])
        pt = core.sb(scope, "att_turned_probs", [P, 2, widest // P, 512])
        peak = core.sb(scope, "att_peak", [P, 3])
        minus = core.sb(scope, "att_minus_peak", [P, 3])
        norm = core.sb(scope, "att_sum", [P, 3])
        recip = core.sb(scope, "att_recip", [P, 3])
        with core.block() as block:
            if bias_tile is not None:
                @block.sync
                def _(sp):
                    for h, head in enumerate(heads):
                        if h >= 2:
                            sp.wait_ge(biased.sem, biased.base + last_unit[h - 2] + 1)
                        sp.dma_start(bias_tile[:, h % 2, :], head.bias_load).then_inc(loaded[h % 2].sem, 16)

            @block.tensor
            def _(pe):
                def scores(n):
                    h, i = units[n]
                    head = heads[h]
                    if n >= 2:
                        pe.wait_ge(biased.sem, biased.base + n - 1)
                    at, seen = 0, head.seen(i)
                    for b, keys in enumerate(head.keys):
                        width = min(keys.shape[-1], seen - at)
                        if width <= 0:
                            break
                        last = nc.tensor.matmul(ps[:, 2 * (n % 2) + b, 0:width], head.q[:, i * P:(i + 1) * P],
                                                keys[:, 0:width], start=True, stop=True)
                        at += width
                    last.then_inc(scored.sem, 1)

                def transposes(n):
                    h, i = units[n]
                    seen = heads[h].seen(i) // P
                    pe.wait_ge(probs.sem, probs.base + n + 1)
                    if n >= 1:
                        pe.wait_ge(kept.sem, kept.base + n)
                    for kt in range(seen):
                        last = nc.tensor.transpose(ps[:, 4 + kt // 4, (kt % 4) * P:(kt % 4 + 1) * P],
                                                   s[:, n % 3, kt * P:(kt + 1) * P], core.ident[:, :])
                    last.then_inc(turned.sem, 1)

                def values(h, n):
                    head = heads[h]
                    pe.wait_ge(kept.sem, kept.base + n + 1)
                    if h >= 2:
                        pe.wait_ge(out.sem, out.base + h - 1)
                    o = head.out.base_row
                    for kt in range(head.total // P):
                        q0 = kt * P if head.causal else 0
                        last = nc.tensor.matmul(ps[o:o + HEAD, 6 + h % 2, q0:head.queries], head.values(kt),
                                                pt[:, h % 2, kt, q0:head.queries], start=kt == 0,
                                                stop=kt == head.total // P - 1)
                    last.then_inc(mixed.sem, 1)

                for n in range(len(units) + 1):
                    if n < len(units):
                        scores(n)
                    if n >= 1:
                        transposes(n - 1)
                        h, i = units[n - 1]
                        if i == heads[h].tiles - 1:
                            values(h, n - 1)

            @block.vector
            def _(dve):
                nonlocal n_steps
                chain = Chain(dve, steps, steps.base)

                def shift(n):
                    h, i = units[n]
                    head = heads[h]
                    seen = head.seen(i)
                    if bias_tile is not None and i == 0:
                        dve.wait_ge(loaded[h % 2].sem, loaded[h % 2].base + 16 * (h // 2 + 1))
                        b = bias_tile[:, h % 2, :].rearrange("p (r c) -> p r c", c=GRID_W)
                        chain(nc.vector.tensor_tensor(b, b, bias_mask, ALU.add))
                    dve.wait_ge(scored.sem, scored.base + n + 1)
                    row = s[:, n % 3, :]
                    if n >= 3:
                        dve.wait_ge(turned.sem, turned.base + n - 2)
                    at, banks, bias = 0, 2 * (n % 2), head.bias(i) if head.bias else None
                    if bias is not None:
                        last = nc.vector.scalar_tensor_tensor(row[:, 0:bias.shape[-1]], ps[:, banks, 0:bias.shape[-1]],
                                                              head.scale, bias, ALU.mult, ALU.add)
                        at, banks = bias.shape[-1], banks + 1
                    if at < seen:
                        if at:
                            chain(last)
                        last = nc.vector.tensor_scalar(row[:, at:seen], ps[:, banks, 0:seen - at], head.scale, None,
                                                       ALU.mult)
                    last.then_inc(biased.sem, 1)
                    dve.wait_ge(biased.sem, biased.base + n + 1)
                    chain(nc.vector.reduce_max(peak[:, n % 3:n % 3 + 1], row[:, 0:seen], AX.X))
                    nc.vector.tensor_scalar(minus[:, n % 3:n % 3 + 1], peak[:, n % 3:n % 3 + 1], -1.0, None,
                                            ALU.mult).then_inc(peaked.sem, 1)

                def normalise(n):
                    h, i = units[n]
                    seen = heads[h].seen(i)
                    dve.wait_ge(exped.sem, exped.base + n + 1)
                    c = slice(n % 3, n % 3 + 1)
                    chain(nc.vector.reciprocal(recip[:, c], norm[:, c]))
                    nc.vector.tensor_scalar(s[:, n % 3, 0:seen], s[:, n % 3, 0:seen], recip[:, c], None, ALU.mult)\
                        .then_inc(probs.sem, 1)

                for n in range(len(units) + 1):
                    if n < len(units):
                        shift(n)
                    if n >= 1:
                        normalise(n - 1)
                n_steps = chain.steps

            @block.scalar
            def _(eng):
                def exps(n):
                    h, i = units[n]
                    seen = heads[h].seen(i)
                    c = slice(n % 3, n % 3 + 1)
                    eng.wait_ge(peaked.sem, peaked.base + n + 1)
                    nc.scalar.activation(s[:, n % 3, 0:seen], s[:, n % 3, 0:seen], ACT.Exp, bias=minus[:, c],
                                         accum_out=norm[:, c]).then_inc(exped.sem, 1)

                def keep(n):
                    h, i = units[n]
                    seen = heads[h].seen(i) // P
                    eng.wait_ge(turned.sem, turned.base + n + 1)
                    if i == 0 and h >= 2:
                        eng.wait_ge(mixed.sem, mixed.base + h - 1)
                    for b in range(0, seen, 4):
                        m = min(4, seen - b)
                        last = nc.scalar.activation(
                            pt[:, h % 2, b:b + m, i * P:(i + 1) * P],
                            ps[:, 4 + b // 4, 0:m * P].rearrange("p (k q) -> p k q", q=P), ACT.Copy)
                    last.then_inc(kept.sem, 1)

                def finish(h):
                    head = heads[h]
                    o = head.out.base_row
                    eng.wait_ge(mixed.sem, mixed.base + h + 1)
                    nc.scalar.activation(head.out.ap, ps[o:o + HEAD, 6 + h % 2, 0:head.queries], ACT.Copy)\
                        .then_inc(out.sem, 1)

                for n in range(len(units) + 1):
                    if n < len(units):
                        exps(n)
                    if n >= 1:
                        keep(n - 1)
                        h, i = units[n - 1]
                        if i == heads[h].tiles - 1:
                            finish(h)
    nu, nh = len(units), len(heads)
    for sig in (scored, biased, peaked, exped, probs, turned, kept):
        sig.base += nu
    mixed.base += nh
    out.base += nh
    steps.base += n_steps
    if bias_tile is not None:
        for slot in range(2):
            loaded[slot].base += 16 * len(range(slot, nh, 2))


class Rows:

    def __init__(self, ap, base_row):
        self.ap, self.base_row = ap, base_row



def head_norm(core, x, rows, tiles, mean_of, gain, rotate=None, cos=None, sin=None):
    nc, ps = core.nc, core.psum
    squared, summed = counter(core, "norm_squared"), counter(core, "norm_summed")
    inverted, rooted = counter(core, "norm_inverted"), counter(core, "norm_rooted")
    scaled, turned, finished = counter(core, "norm_scaled"), counter(core, "norm_turned"), counter(core, "norm_finished")
    steps = counter(core, "norm_vector_step")
    per = 1 + (2 if rotate is not None else 0)
    with ExitStack() as scope:
        sq = core.sb(scope, "head_sq", [P, 2, SEQ])
        var = core.sb(scope, "head_var", [P, 2, SEQ])
        rstd = core.sb(scope, "head_rstd", [P, 2, SEQ])
        part = core.sb(scope, "head_part", [P, SEQ])
        with core.block() as block:
            @block.scalar
            def _(eng):
                def square(n):
                    if n >= 2:
                        eng.wait_ge(summed.sem, summed.base + n - 1)
                    nc.scalar.activation(sq[0:rows, n % 2, :], x[0:rows, n, :], ACT.Square).then_inc(squared.sem, 1)

                square(0)
                for n in range(tiles):
                    if n + 1 < tiles:
                        square(n + 1)
                    eng.wait_ge(inverted.sem, inverted.base + n + 1)
                    nc.scalar.activation(rstd[0:rows, n % 2, :], var[0:rows, n % 2, :], ACT.Sqrt).then_inc(rooted.sem, 1)

            @block.tensor
            def _(pe):
                def mean(n):
                    pe.wait_ge(squared.sem, squared.base + n + 1)
                    if n >= 2:
                        pe.wait_ge(inverted.sem, inverted.base + n - 1)
                    nc.tensor.matmul(ps[0:rows, n % 2, :], mean_of, sq[0:rows, n % 2, :], start=True, stop=True)\
                        .then_inc(summed.sem, 1)

                mean(0)
                for n in range(tiles):
                    if n + 1 < tiles:
                        mean(n + 1)
                    if rotate is not None:
                        pe.wait_ge(scaled.sem, scaled.base + n + 1)
                        if n >= 2:
                            pe.wait_ge(finished.sem, finished.base + n - 1)
                        nc.tensor.matmul(ps[0:rows, 2 + n % 2, :], rotate, x[0:rows, n, :], start=True, stop=True)\
                            .then_inc(turned.sem, 1)

            @block.vector
            def _(dve):
                chain = Chain(dve, steps, steps.base)
                for n in range(tiles):
                    dve.wait_ge(summed.sem, summed.base + n + 1)
                    v = var[0:rows, n % 2, :]
                    chain(nc.vector.tensor_scalar(v, ps[0:rows, n % 2, :], EPS, None, ALU.add))
                    nc.vector.reciprocal(v, v).then_inc(inverted.sem, 1)
                    dve.wait_ge(rooted.sem, rooted.base + n + 1)
                    nc.vector.scalar_tensor_tensor(x[0:rows, n, :], x[0:rows, n, :], gain, rstd[0:rows, n % 2, :],
                                                   ALU.mult, ALU.mult).then_inc(scaled.sem, 1)
                    if rotate is not None:
                        dve.wait_ge(turned.sem, turned.base + n + 1)
                        chain(nc.vector.tensor_tensor(part[0:rows, :], ps[0:rows, 2 + n % 2, :], sin, ALU.mult))
                        chain(nc.vector.tensor_tensor(x[0:rows, n, :], x[0:rows, n, :], cos, ALU.mult))
                        nc.vector.tensor_tensor(x[0:rows, n, :], x[0:rows, n, :], part[0:rows, :], ALU.add)\
                            .then_inc(finished.sem, 1)
                        dve.wait_ge(finished.sem, finished.base + n + 1)
    for sig in (squared, summed, inverted, rooted, scaled):
        sig.base += tiles
    if rotate is not None:
        turned.base += tiles
        finished.base += tiles
    steps.base += per * tiles


def rotation_tables(core, positions, freqs, tables):
    nc = core.nc
    landed, reduced, waved = counter(core, "positions_landed"), counter(core, "angle_reduced"), counter(core, "angle_waved")
    steps = counter(core, "rope_vector_step")
    c1 = 6.28125
    c2 = float(np.float32(np.floor((2 * np.pi - c1) * 2.0 ** 20) / 2.0 ** 20))
    c3 = float(2 * np.pi - c1 - c2)
    magic = 1.5 * 2.0 ** 23
    pi = float(np.nextafter(np.float32(np.pi), np.float32(0)))
    n_steps = 0
    with ExitStack() as scope:
        raw = core.sb(scope, "rope_positions", [P, SEQ], I32)
        pos = core.sb(scope, "rope_pos", [P, SEQ])
        ang = core.sb(scope, "rope_angle", [P, SEQ])
        turns = core.sb(scope, "rope_turns", [P, SEQ])
        red = core.sb(scope, "rope_reduced", [P, 4, SEQ])
        with core.block() as block:
            @block.sync
            def _(sp):
                sp.dma_start(raw[:, :], positions.to_broadcast([P, SEQ])).then_inc(landed.sem, 16)

            @block.vector
            def _(dve):
                nonlocal n_steps
                chain = Chain(dve, steps, steps.base)
                dve.wait_ge(landed.sem, landed.base + 16)
                chain(nc.vector.tensor_copy(pos[:, :], raw[:, :]))
                for n in range(len(tables)):
                    for j, quarter in enumerate((0.25, 0.0)):
                        r = red[:, 2 * n + j, :]
                        chain(nc.vector.tensor_scalar(ang[:, :], pos[:, :], col(freqs, n), None, ALU.mult))
                        chain(nc.vector.tensor_scalar(turns[:, :], ang[:, :], float(1 / (2 * np.pi)), quarter,
                                                      ALU.mult, ALU.add))
                        chain(nc.vector.tensor_scalar(turns[:, :], turns[:, :], magic, None, ALU.add))
                        chain(nc.vector.tensor_scalar(turns[:, :], turns[:, :], -magic, None, ALU.add))
                        src = ang[:, :]
                        for c in (c1, c2, c3):
                            chain(nc.vector.scalar_tensor_tensor(r, turns[:, :], -c, src, ALU.mult, ALU.add))
                            src = r
                        chain(nc.vector.tensor_scalar(r, r, quarter * 2 * float(np.pi), pi, ALU.add, ALU.min))
                        nc.vector.tensor_scalar(r, r, -pi, None, ALU.max).then_inc(reduced.sem, 1)
                n_steps = chain.steps

            @block.scalar
            def _(eng):
                for n, pair in enumerate(tables):
                    for j in range(2):
                        eng.wait_ge(reduced.sem, reduced.base + 2 * n + j + 1)
                        nc.scalar.activation(pair[j], red[:, 2 * n + j, :], ACT.Sin).then_inc(waved.sem, 1)
    landed.base += 16
    reduced.base += 2 * len(tables)
    waved.base += 2 * len(tables)
    steps.base += n_steps



def conv_mlp(core, weights, act, taps, bias, dst):
    nc, ps = core.nc, core.psum
    nt, ring = 2 * FT2, 4
    landed = [counter(core, f"panel_landed_{s}") for s in range(4)]
    done, first, evicted = counter(core, "panel_done"), counter(core, "panel_first_evict"), counter(core, "panel_evicted")
    conv, gated, steps = counter(core, "conv_done"), counter(core, "gate_done"), counter(core, "gemm_vector_step")
    blocks = nt // ring
    per = 2 * 2 + 2 * 2 - 1 + 1
    with ExitStack() as scope:
        w = core.sb(scope, "up_panels", [P, ring, D])
        y = core.sb(scope, "conv_out", [P, ring, SEQ])
        gate = core.sb(scope, "gate_out", [P, 2, SEQ])
        with core.block() as block:
            @block.sync
            def _(sp):
                with sp.Fori(0, blocks) as blk:
                    for u in range(ring):
                        sp.wait_ge(done.sem, done.base + blk * ring + u + 1 - ring)
                        sp.dma_start(w[:, u, :], weights[bass.ds(blk * ring + u, 1), :, :].rearrange("a p k -> p (a k)"))\
                            .then_inc(landed[u].sem, 16)

            @block.tensor
            def _(pe):
                with pe.Fori(0, blocks) as blk:
                    for u in range(ring):
                        pe.wait_ge(landed[u].sem, landed[u].base + 16 * (blk + 1))
                        pe.wait_ge(evicted.sem, evicted.base + blk * ring + u + 1 - ring)
                        for k in range(DT):
                            last = nc.tensor.matmul(ps[:, u, :], w[:, u, k * P:(k + 1) * P], act[:, k, 0:SEQ],
                                                    start=k == 0, stop=k == DT - 1)
                        last.then_inc(done.sem, 1)

            @block.scalar
            def _(eng):
                with eng.Fori(0, blocks) as blk:
                    for u in range(ring):
                        n = blk * ring + u
                        eng.wait_ge(done.sem, done.base + n + 1)
                        eng.wait_ge(gated.sem, gated.base + blk * 2 + u // 2 - 1)
                        nc.scalar.activation(y[:, u, :], ps[:, u, :], ACT.Identity, bias=col(bias, n),
                                             scale=col(taps[:, 2, :], n)).then_inc(first.sem, 1)
                        if u % 2 == 1:
                            eng.wait_ge(evicted.sem, evicted.base + n)
                            nc.scalar.activation(gate[:, u // 2, :], y[:, u - 1, :], ACT.Sigmoid).then_inc(conv.sem, 1)

            @block.vector
            def _(dve):
                with dve.Fori(0, blocks) as blk:
                    chain = Chain(dve, steps, steps.base + blk * 6)
                    for u in range(ring):
                        n = blk * ring + u
                        dve.wait_ge(first.sem, first.base + n + 1)
                        chain(nc.vector.scalar_tensor_tensor(y[:, u, 1:SEQ], ps[:, u, 0:SEQ - 1], col(taps[:, 1, :], n),
                                                             y[:, u, 1:SEQ], ALU.mult, ALU.add))
                        nc.vector.scalar_tensor_tensor(y[:, u, 2:SEQ], ps[:, u, 0:SEQ - 2], col(taps[:, 0, :], n),
                                                       y[:, u, 2:SEQ], ALU.mult, ALU.add).then_inc(evicted.sem, 1)
                        if u % 2 == 1:
                            dve.wait_ge(evicted.sem, evicted.base + n + 1)
                            dve.wait_ge(conv.sem, conv.base + blk * 2 + u // 2 + 1)
                            chain(nc.vector.tensor_tensor(gate[:, u // 2, :], gate[:, u // 2, :], y[:, u - 1, :], ALU.mult))
                            nc.vector.tensor_tensor(tile(dst, blk * 2 + u // 2), gate[:, u // 2, :], y[:, u, :],
                                                    ALU.mult).then_inc(gated.sem, 1)
                    assert chain.steps == 6
    for s in range(ring):
        landed[s].base += 16 * blocks
    done.base += nt
    first.base += nt
    evicted.base += nt
    conv.base += FT2
    gated.base += FT2
    steps.base += 6 * blocks



def neighbour_difference(core, h, segments, dst, then):
    nc = core.nc
    steps = counter(core, "mix_vector_step")
    per = 2
    with ExitStack() as scope:
        with core.block() as block:
            @block.vector
            def _(dve):
                chain = Chain(dve, steps, steps.base)
                for k in range(DT):
                    for t0, t1 in segments:
                        nc.vector.tensor_tensor(dst[:, k, t0 + 1:t1 - 1], h[:, k, t0:t1 - 2], h[:, k, t0 + 2:t1], ALU.add)
                        nc.vector.tensor_copy(dst[:, k, t0:t0 + 1], h[:, k, t0 + 1:t0 + 2])
                        last = nc.vector.tensor_copy(dst[:, k, t1 - 1:t1], h[:, k, t1 - 2:t1 - 1])
                    chain(last)
                    chain(nc.vector.scalar_tensor_tensor(dst[:, k, :], dst[:, k, :], 0.5, h[:, k, :],
                                                         ALU.mult, ALU.subtract))
                then(dve)
    steps.base += per * DT


def token_mix(core, dve, h, diff, mu, dst, tokens=T0):
    mixed = counter(core, "mix_done")
    for k in range(DT):
        core.nc.vector.scalar_tensor_tensor(dst[:, k, 0:tokens], diff[:, k, 0:tokens], col(mu, k), h[:, k, 0:tokens],
                                            ALU.mult, ALU.add).then_inc(mixed.sem, 1)
    mixed.base += DT


def wkv(core, lora_w, lora_a, up_panels, k_dram, v_dram, r_dram, g_dram, par, masks, dst):
    nc, ps = core.nc, core.psum
    chunks = T0 // CHUNK
    tiles = T0 // P
    xt = SEQ // P
    batches = tiles // 2

    def sig(name):
        return counter(core, name)

    loaded, lora, acted = sig("pair_loaded"), sig("lora_done"), sig("lora_activated")
    ps_kk, ps_inv, ps_root = sig("key_squared"), sig("key_inverted"), sig("key_rooted")
    ps_sum, normed = sig("key_summed"), sig("key_normed")
    expo, powers = sig("decay_exponent"), sig("decay_powers")
    tilde = sig("tilde_ready")
    turned, tok = sig("tilde_turned"), sig("token_major_kept")
    product = [sig(f"triangle_product_{h}") for h in range(2)]
    kept = {"V": [sig(f"triangle_kept_{h}") for h in range(2)], "S": [sig(f"factor_kept_{h}") for h in range(2)]}
    masked = [sig(f"levels_masked_{h}") for h in range(2)]
    u_done, u_kept, s_done, s_kept = sig("u_product"), sig("u_kept"), sig("state_product"), sig("state_kept")
    y_done, y_kept, zeroed = sig("y_state_product"), sig("y_state_kept"), sig("state_zeroed")
    intra, summed = sig("y_intra_product"), sig("y_summed")
    mean, centred, csq, var = sig("gn_mean"), sig("gn_centred"), sig("gn_squared"), sig("gn_var")
    ginv, groot, bonus_in, bonus = sig("gn_inverted"), sig("gn_rooted"), sig("bonus_terms"), sig("bonus_product")
    pair_done, steps = sig("pair_done"), sig("wkv_vector_step")

    def exchanges(i):
        out = [("gram", "V"), ("turn", "S")] + ([("read", "V")] if i else [])
        for n in LEVELS:
            out += [(f"z{n}", "S"), (f"w{n}", "V")] + ([(f"t{n}", "S")] if n != LEVELS[-1] else [])
        return out + [("kx", "S"), ("mkv", "V"), ("ux", "S")]

    def keeps(who, i, e=0):
        return sum(k == who for b in range(i) for _, k in exchanges(b)) + sum(k == who for _, k in exchanges(i)[:e])

    product_at = [sum(len(exchanges(b)) for b in range(i)) for i in range(batches + 1)]
    total_keeps = {who: sum(k == who for b in range(batches) for _, k in exchanges(b)) for who in "VS"}
    tile_at = [list(range(xt, tiles)) + list(range(xt)), list(range(tiles - 1, xt - 1, -1)) + list(range(xt - 1, -1, -1))]
    chunk_at = [[2 * t + (o if d == 0 else 1 - o) for t in tile_at[d] for o in range(2)] for d in range(2)]
    per_batch = chunks // batches
    first_x = CTX // CHUNK
    VSTEPS = 55

    def woven(i):
        if i == 0:
            return {}
        at = {}
        for k in range(per_batch):
            at[4 * k + 1] = ("u", (i - 1) * per_batch + k)
            at[4 * k + 3] = ("s", (i - 1) * per_batch + k)
        return at

    with ExitStack() as scope:
        def sb(name, shape):
            return core.sb(scope, name, shape)

        ups = sb("wkv_ups", [P, 2 * P])
        K, V = sb("wkv_k", [P, T0]), sb("wkv_v", [P, T0])
        R, G = sb("wkv_r", [P, SEQ]), sb("wkv_g", [P, SEQ])
        LW, A = sb("wkv_logw", [P, 2, T0]), sb("wkv_a", [P, 2, T0])
        KK, SQ, VAR = sb("wkv_kk", [P, T0]), sb("wkv_sq", [P, T0]), sb("wkv_var", [P, T0])
        INC, EXC = sb("wkv_inc", [P, 2, T0]), sb("wkv_exc", [P, 2, T0])
        PINC, PINV = sb("wkv_pinc", [P, 2, SEQ]), sb("wkv_pinv", [P, 2, T0])
        KD = sb("wkv_kd", [P, 2, T0])
        KSUM = sb("wkv_ksum", [P, SEQ])
        PC = sb("wkv_chunk_decay", [P, 2, chunks])
        TOK = sb("wkv_tok", [P, 7, T0])
        KX = INC
        UX, U = (t[:, :, :].rearrange("p d (n c) -> p d n c", c=P) for t in (LW, PINV))
        GA, GK = sb("wkv_ga", [P, 2, xt, 2, P]), sb("wkv_gk", [P, 2, xt, 2, P])
        S, SP = sb("wkv_s", [P, 2, 2, P]), sb("wkv_sp", [P, 2, P])
        YS = sb("wkv_ys", [P, 2, SEQ])
        MT, MK = sb("wkv_mt", [P, 2, 512]), sb("wkv_mk", [P, 2, 512])
        X, XT, Z = sb("wkv_x", [P, 2, 512]), sb("wkv_xt", [P, 2, 512]), sb("wkv_z", [P, 2, 512])
        LT = sb("wkv_level", [P, 2, 2, 512])
        MKV = sb("wkv_mkv", [P, 2, 4 * HEAD])
        BON = sb("wkv_bonus", [P, SEQ])

        def group(j, d):
            return slice((2 * j + d) * P, (2 * j + d + 1) * P)

        def over_tiles(ap):
            return ap.rearrange("p (j c) -> p j c", j=2)

        def mask(n):
            return masks[n].unsqueeze(1).to_broadcast([P, 2, 2 * P])

        with core.block() as block:
            @block.sync
            def _(sp):
                with sp.Fori(0, DT) as ft:
                    sp.wait_ge(pair_done.sem, pair_done.base + ft)
                    for dst_, src in ((ups, up_panels), (K, k_dram), (V, v_dram), (R, r_dram), (G, g_dram)):
                        sp.dma_start(dst_[:, :], src[bass.ds(ft, 1), :, :].rearrange("a p t -> p (a t)"))\
                            .then_inc(loaded.sem, 16)

            @block.tensor
            def _(pe):
                with pe.Fori(0, DT) as ft:
                    pe.wait_ge(loaded.sem, loaded.base + 80 * (ft + 1))
                    pe.wait_ge(pair_done.sem, pair_done.base + ft)
                    for which, src in ((0, lora_w), (1, lora_a)):
                        for d in range(2):
                            rows = slice(d * HEAD, (d + 1) * HEAD)
                            for a in range(2):
                                last = nc.tensor.matmul(ps[:, 4 * which + 2 * d + a, 0:T0 // 2],
                                                        ups[rows, which * P:(which + 1) * P],
                                                        src[rows, a * T0 // 2:(a + 1) * T0 // 2], start=True, stop=True)
                            last.then_inc(lora.sem, 1)
                    pe.wait_ge(ps_kk.sem, ps_kk.base + ft + 1)
                    pe.wait_ge(acted.sem, acted.base + 4 * ft + 4)
                    for a in range(2):
                        last = nc.tensor.matmul(ps[:, a, 0:T0 // 2], core.head_sum[:, :],
                                                SQ[:, a * T0 // 2:(a + 1) * T0 // 2], start=True, stop=True)
                    last.then_inc(ps_sum.sem, 1)
                    for n, src in enumerate((EXC[:, 0, :], EXC[:, 1, :], A[:, 0, :], A[:, 1, :], KD[:, 0, :],
                                             KD[:, 1, :], V[:, :])):
                        if n == 0:
                            pe.wait_ge(tilde.sem, tilde.base + ft + 1)
                        if n >= 4:
                            pe.wait_ge(tok.sem, tok.base + 7 * ft + n - 3)
                        for t in range(tiles):
                            last = nc.tensor.transpose(ps[:, 2 * (n % 4) + t // 3, (t % 3) * P:(t % 3 + 1) * P],
                                                       src[:, t * P:(t + 1) * P], core.ident[:, :])
                        last.then_inc(turned.sem, 1)
                    pe.wait_ge(tok.sem, tok.base + 7 * ft + 7)
                    pe.wait_ge(zeroed.sem, zeroed.base + ft + 1)

                    def products(name, h, i):
                        rows = slice(h * HEAD, (h + 1) * HEAD)
                        ba, bb = 2 * h, 2 * h + 1
                        for j in range(2):
                            for d in range(2):
                                g = group(j, d)
                                t = tile_at[d][2 * i + j]
                                at = slice(t * P, (t + 1) * P)
                                own = slice(t * P + h * HEAD, t * P + (h + 1) * HEAD)
                                v = slice((2 * j + d) * HEAD, (2 * j + d + 1) * HEAD)
                                if name == "gram":
                                    nc.tensor.matmul(ps[:, ba, g], A[rows, d, at], EXC[rows, d, at], start=True, stop=True)
                                    last = nc.tensor.matmul(ps[:, bb, g], KD[rows, d, at], EXC[rows, d, at],
                                                            start=True, stop=True)
                                elif name == "read":
                                    nc.tensor.matmul(ps[:, ba, g], A[rows, d, at], PINC[rows, d, at], start=True, stop=True)
                                    last = nc.tensor.matmul(ps[:, bb, g], KD[rows, d, at], PINC[rows, d, at],
                                                            start=True, stop=True)
                                elif name == "turn":
                                    last = nc.tensor.transpose(ps[:, ba, g], XT[:, h, g], core.ident[:, :])
                                elif name[0] == "z":
                                    last = nc.tensor.matmul(ps[:, ba, g], LT[:, h, LEVELS.index(int(name[1:])) % 2, g],
                                                            X[:, h, g], start=True, stop=True)
                                elif name == f"w{LEVELS[-1]}":
                                    last = nc.tensor.matmul(ps[:, bb, g], Z[:, h, g], XT[:, h, g], start=True, stop=True)
                                elif name[0] == "w":
                                    last = nc.tensor.matmul(ps[:, bb, g], XT[:, h, g], Z[:, h, g], start=True, stop=True)
                                elif name[0] == "t":
                                    last = nc.tensor.transpose(ps[:, ba, g], X[:, h, g], core.ident[:, :])
                                elif name == "kx":
                                    last = nc.tensor.matmul(ps[rows, ba, g], TOK[:, d, own], XT[:, h, g],
                                                            start=True, stop=True)
                                elif name == "mkv":
                                    last = nc.tensor.matmul(ps[:, bb, v], MK[:, h, g], TOK[:, 6, own], start=True, stop=True)
                                else:
                                    last = nc.tensor.matmul(ps[:, ba, v], XT[:, h, g], MKV[:, h, v], start=True, stop=True)
                        last.then_inc(product[h].sem, 1)

                    def step_u(c):
                        if c % per_batch == 0:
                            for h in range(2):
                                e = [n for n, _ in exchanges(c // per_batch)].index("kx")
                                pe.wait_ge(kept["S"][h].sem, kept["S"][h].base + total_keeps["S"] * ft
                                           + keeps("S", c // per_batch, e + 1))
                        if c:
                            pe.wait_ge(s_kept.sem, s_kept.base + (chunks - 1) * ft + c)
                        for d in range(2):
                            last = nc.tensor.matmul(ps[:, 4, d * P:(d + 1) * P], KX[:, d, c // 2 * P:(c // 2 + 1) * P],
                                                    S[:, c % 2, d, :], start=True, stop=True)
                        last.then_inc(u_done.sem, 1)
                        n = c - first_x
                        if n >= 1:
                            pe.wait_ge(y_kept.sem, y_kept.base + (chunks - first_x) * ft + n)
                        if n >= 0:
                            for d in range(2):
                                ch = chunk_at[d][c]
                                last = nc.tensor.matmul(ps[:, 7, d * CHUNK:(d + 1) * CHUNK], S[:, c % 2, d, :],
                                                        PINC[:, d, ch * CHUNK:(ch + 1) * CHUNK], start=True, stop=True)
                            last.then_inc(y_done.sem, 1)

                    def step_s(c):
                        pe.wait_ge(u_kept.sem, u_kept.base + chunks * ft + c + 1)
                        for d in range(2):
                            ch = chunk_at[d][c]
                            rows = slice(ch % 2 * HEAD, ch % 2 * HEAD + HEAD)
                            f = slice(ch // 2 * P, ch // 2 * P + P)
                            nc.tensor.matmul(ps[:, 5 + d, 0:P], TOK[rows, 2 + d, f], U[rows, d, c // 2, :],
                                             start=True, stop=False)
                            last = nc.tensor.matmul(ps[:, 5 + d, 0:P], TOK[rows, 4 + d, f], TOK[rows, 6, f],
                                                    start=False, stop=True)
                        last.then_inc(s_done.sem, 1)

                    for i in range(batches):
                        weave = woven(i)
                        for e, (name, keeper) in enumerate(exchanges(i)):
                            for h in range(2):
                                for who in "VS":
                                    n = keeps(who, i, e)
                                    if e == 0 or exchanges(i)[e - 1][1] == who or name in ("mkv", "ux"):
                                        pe.wait_ge(kept[who][h].sem, kept[who][h].base + total_keeps[who] * ft + n)
                                if name[0] == "z":
                                    pe.wait_ge(masked[h].sem, masked[h].base + len(LEVELS) * (batches * ft + i)
                                               + LEVELS.index(int(name[1:])) + 1)
                                products(name, h, i)
                            if e in weave:
                                part, c = weave[e]
                                step_u(c) if part == "u" else step_s(c)
                    for c in range(chunks - per_batch, chunks):
                        step_u(c)
                        if c < chunks - 1:
                            step_s(c)
                    pe.wait_ge(u_kept.sem, u_kept.base + chunks * (ft + 1))
                    for t in range(xt):
                        for h in range(2):
                            out = slice(h * HEAD, (h + 1) * HEAD)
                            for d in range(2):
                                n = tile_at[d].index(t)
                                nc.tensor.matmul(ps[out, 0, t * P:(t + 1) * P], U[:, d, n, out],
                                                 GA[:, h, n - CTX // P, d, :], start=d == 0, stop=False)
                                last = nc.tensor.matmul(ps[out, 0, t * P:(t + 1) * P],
                                                        TOK[:, 6, t * P + h * HEAD:t * P + (h + 1) * HEAD],
                                                        GK[:, h, n - CTX // P, d, :], start=False, stop=d == 1)
                    last.then_inc(intra.sem, 1)
                    pe.wait_ge(summed.sem, summed.base + ft + 1)
                    nc.tensor.matmul(ps[:, 1, :], core.head_mean[:, :], YS[:, 0, :], start=True, stop=True)\
                        .then_inc(mean.sem, 1)
                    pe.wait_ge(csq.sem, csq.base + ft + 1)
                    nc.tensor.matmul(ps[:, 2, :], core.head_mean[:, :], SQ[:, 0:SEQ], start=True, stop=True)\
                        .then_inc(var.sem, 1)
                    pe.wait_ge(bonus_in.sem, bonus_in.base + ft + 1)
                    nc.tensor.matmul(ps[:, 3, :], core.head_sum[:, :], BON[:, :], start=True, stop=True)\
                        .then_inc(bonus.sem, 1)

            @block.scalar
            def _(eng):
                with eng.Fori(0, DT) as ft:
                    eng.wait_ge(pair_done.sem, pair_done.base + ft)
                    for which, dst_, bias in ((0, LW, par["w0"]), (1, A, par["a0"])):
                        for d in range(2):
                            eng.wait_ge(lora.sem, lora.base + 4 * ft + 2 * which + d + 1)
                            b = 4 * which + 2 * d
                            nc.scalar.activation(halves(dst_[:, d, :]), ps[:, b:b + 2, 0:T0 // 2], ACT.Sigmoid,
                                                 bias=col(bias[d], ft)).then_inc(acted.sem, 1)
                    eng.wait_ge(normed.sem, normed.base + 2 * ft + 1)
                    nc.scalar.activation(SQ[:, :], KK[:, :], ACT.Square).then_inc(ps_kk.sem, 1)
                    eng.wait_ge(ps_inv.sem, ps_inv.base + ft + 1)
                    nc.scalar.activation(VAR[:, :], VAR[:, :], ACT.Sqrt).then_inc(ps_root.sem, 1)
                    for d in range(2):
                        eng.wait_ge(expo.sem, expo.base + 2 * ft + d + 1)
                        nc.scalar.activation(EXC[:, d, :], EXC[:, d, :], ACT.Exp)
                        nc.scalar.activation(PINC[:, d, :], INC[:, d, 0:SEQ], ACT.Exp)
                        end = CHUNK - 1 if d == 0 else 0
                        nc.scalar.activation(PC[:, d, :], INC[:, d, end::CHUNK], ACT.Exp)
                        nc.scalar.activation(PINV[:, d, :], INC[:, d, :], ACT.Exp, scale=-1.0).then_inc(powers.sem, 1)
                    for n in range(7):
                        eng.wait_ge(turned.sem, turned.base + 7 * ft + n + 1)
                        b = 2 * (n % 4)
                        nc.scalar.activation(halves(TOK[:, n, :]), ps[:, b:b + 2, 0:T0 // 2], ACT.Copy)\
                            .then_inc(tok.sem, 1)

                    def keep(name, h, i):
                        ba = 2 * h
                        if name == "kx":
                            rows = slice(h * HEAD, (h + 1) * HEAD)
                            for d in range(2):
                                last = nc.scalar.activation(
                                    over_tiles(KX[rows, d, 2 * i * P:2 * (i + 1) * P]),
                                    over_tiles(ps[rows, ba, :])[:, :, d * P:(d + 1) * P], ACT.Copy, scale=-1.0)
                        elif name == "ux":
                            own = slice(h * HEAD, (h + 1) * HEAD)
                            for d in range(2):
                                last = nc.scalar.activation(
                                    UX[:, d, 2 * i:2 * i + 2, own],
                                    over_tiles(ps[:, ba, 0:4 * HEAD])[:, :, d * HEAD:(d + 1) * HEAD], ACT.Copy, scale=-1.0)
                        else:
                            dst_ = {"z": Z, "t": XT}[name[0]] if name != "turn" else X
                            last = nc.scalar.activation(dst_[:, h, :], ps[:, ba, :], ACT.Copy)
                        last.then_inc(kept["S"][h].sem, 1)

                    def keep_y(c):
                        eng.wait_ge(y_done.sem, y_done.base + (chunks - first_x) * ft + c - first_x + 1)
                        for d in range(2):
                            ch = chunk_at[d][c]
                            last = nc.scalar.activation(YS[:, d, ch * CHUNK:(ch + 1) * CHUNK],
                                                        ps[:, 7, d * CHUNK:(d + 1) * CHUNK], ACT.Copy)
                        last.then_inc(y_kept.sem, 1)

                    for i in range(batches):
                        weave = woven(i)
                        for e, (name, keeper) in enumerate(exchanges(i)):
                            for h in range(2):
                                if keeper == "S":
                                    eng.wait_ge(product[h].sem, product[h].base + product_at[-1] * ft + product_at[i] + e + 1)
                                    keep(name, h, i)
                            if e in weave and weave[e][0] == "u" and weave[e][1] >= first_x:
                                keep_y(weave[e][1])
                    for c in range(chunks - per_batch, chunks):
                        keep_y(c)
                    eng.wait_ge(centred.sem, centred.base + ft + 1)
                    nc.scalar.activation(SQ[:, 0:SEQ], YS[:, 1, :], ACT.Square).then_inc(csq.sem, 1)
                    eng.wait_ge(ginv.sem, ginv.base + ft + 1)
                    nc.scalar.activation(VAR[:, 0:SEQ], VAR[:, 0:SEQ], ACT.Sqrt).then_inc(groot.sem, 1)

            @block.gpsimd
            def _(pool):
                with pool.Fori(0, DT) as ft:
                    for i in range(batches):
                        for l, n in enumerate(LEVELS):
                            for h in range(2):
                                if l < 2:
                                    pool.wait_ge(kept["V"][h].sem, kept["V"][h].base + total_keeps["V"] * ft
                                                 + keeps("V", i, 1))
                                else:
                                    e = [x for x, _ in exchanges(i)].index(f"z{LEVELS[l - 2]}")
                                    pool.wait_ge(product[h].sem, product[h].base + product_at[-1] * ft + product_at[i] + e + 1)
                                nc.gpsimd.tensor_tensor(over_tiles(LT[:, h, l % 2, :]), over_tiles(MT[:, h, :]), mask(n),
                                                        ALU.mult).then_inc(masked[h].sem, 1)

            @block.vector
            def _(dve):
                with dve.Fori(0, DT) as ft:
                    chain = Chain(dve, steps, steps.base + VSTEPS * ft)
                    tt, ts, stt = nc.vector.tensor_tensor, nc.vector.tensor_scalar, nc.vector.scalar_tensor_tensor
                    dve.wait_ge(loaded.sem, loaded.base + 80 * (ft + 1))
                    ts(KK[:, :], K[:, :], col(par["kk"], ft), None, ALU.mult).then_inc(normed.sem, 1)
                    nc.vector.memset(S[:, :, :, :], 0.0).then_inc(zeroed.sem, 1)
                    for d in range(2):
                        dve.wait_ge(acted.sem, acted.base + 4 * ft + d + 1)
                        chain(ts(LW[:, d, :], LW[:, d, :], -DECAY_SCALE, None, ALU.mult))
                        chain(nc.vector.tensor_tensor_scan(INC[:, d, :], masks["resets"], LW[:, d, :], 0.0,
                                                           ALU.mult, ALU.add))
                        if d == 0:
                            tt(EXC[:, d, :], INC[:, d, :], LW[:, d, :], ALU.subtract).then_inc(expo.sem, 1)
                            dve.wait_ge(expo.sem, expo.base + 2 * ft + 1)
                        else:
                            by_chunk = INC[:, d, :].rearrange("p (c t) -> p c t", t=CHUNK)
                            whole = by_chunk[:, :, CHUNK - 1:CHUNK].to_broadcast([P, chunks, CHUNK])
                            chain(tt(EXC[:, d, :].rearrange("p (c t) -> p c t", t=CHUNK), whole, by_chunk, ALU.subtract))
                            tt(INC[:, d, :], EXC[:, d, :], LW[:, d, :], ALU.add).then_inc(expo.sem, 1)
                            dve.wait_ge(expo.sem, expo.base + 2 * ft + 2)
                    dve.wait_ge(ps_sum.sem, ps_sum.base + ft + 1)
                    chain(ts(halves(VAR[:, :]), ps[:, 0:2, 0:T0 // 2], 1e-24, None, ALU.max))
                    nc.vector.reciprocal(VAR[:, :], VAR[:, :]).then_inc(ps_inv.sem, 1)
                    dve.wait_ge(ps_root.sem, ps_root.base + ft + 1)
                    tt(KK[:, :], KK[:, :], VAR[:, :], ALU.mult).then_inc(normed.sem, 1)
                    dve.wait_ge(normed.sem, normed.base + 2 * ft + 2)
                    for d in range(2):
                        dve.wait_ge(acted.sem, acted.base + 4 * ft + 3 + d)
                        chain(ts(KD[:, d, :], A[:, d, :], -1.0, col(par["ka"], ft), ALU.add, ALU.mult))
                        chain(stt(KD[:, d, :], KD[:, d, :], 1.0, K[:, :], ALU.add, ALU.mult))
                        chain(tt(A[:, d, :], A[:, d, :], KK[:, :], ALU.mult))
                    chain(tt(KSUM[:, :], KD[:, 0, 0:SEQ], KD[:, 1, 0:SEQ], ALU.add))
                    for d in range(2):
                        dve.wait_ge(powers.sem, powers.base + 2 * ft + d + 1)
                        chain(tt(KD[:, d, :], KD[:, d, :], PINV[:, d, :], ALU.mult))
                        chain(tt(A[:, d, :], A[:, d, :], PINV[:, d, :], ALU.mult))
                        chain(tt(PINC[:, d, :], PINC[:, d, :], R[:, :], ALU.mult))
                        last = tt(EXC[:, d, :], EXC[:, d, :], KK[:, :], ALU.mult)
                        if d == 0:
                            chain(last)
                    last.then_inc(tilde.sem, 1)
                    chain(tt(KSUM[:, :], KSUM[:, :], R[:, :], ALU.mult))
                    ts(BON[:, :], KSUM[:, :], col(par["rk"], ft), None, ALU.mult).then_inc(bonus_in.sem, 1)

                    def keep(name, h, i):
                        ba, bb = 2 * h, 2 * h + 1
                        if name == "gram":
                            chain(tt(over_tiles(MT[:, h, :]), over_tiles(ps[:, ba, :]), mask("strict"), ALU.mult))
                            chain(tt(over_tiles(XT[:, h, :]), over_tiles(MT[:, h, :]), mask("minus_first_t"), ALU.mult))
                            chain(tt(over_tiles(XT[:, h, :]), over_tiles(XT[:, h, :]), mask("ident"), ALU.add))
                            last = tt(over_tiles(MK[:, h, :]), over_tiles(ps[:, bb, :]), mask("strict"), ALU.mult)
                        elif name == "read":
                            n = 2 * i - CTX // P
                            for dst_, bank in ((GA, ba), (GK, bb)):
                                last = tt(dst_[:, h, n:n + 2, :, :].rearrange("p j d c -> p j (d c)"),
                                          over_tiles(ps[:, bank, :]), mask("inclusive"), ALU.mult)
                        elif name == f"w{LEVELS[-1]}":
                            last = tt(XT[:, h, :], XT[:, h, :], ps[:, bb, :], ALU.subtract)
                        elif name[0] == "w":
                            last = tt(X[:, h, :], X[:, h, :], ps[:, bb, :], ALU.subtract)
                        else:
                            last = nc.vector.tensor_copy(MKV[:, h, :], ps[:, bb, 0:4 * HEAD])
                        last.then_inc(kept["V"][h].sem, 1)

                    def step_u(c):
                        dve.wait_ge(u_done.sem, u_done.base + chunks * ft + c + 1)
                        if c % per_batch == 0:
                            for h in range(2):
                                dve.wait_ge(kept["S"][h].sem, kept["S"][h].base + total_keeps["S"] * ft
                                            + keeps("S", c // per_batch, len(exchanges(c // per_batch))))
                        for d in range(2):
                            ch = chunk_at[d][c]
                            rows = slice(ch % 2 * HEAD, ch % 2 * HEAD + HEAD)
                            last = tt(U[rows, d, c // 2, :], ps[rows, 4, d * P:(d + 1) * P], UX[rows, d, c // 2, :], ALU.add)
                        last.then_inc(u_kept.sem, 1)
                        if c < chunks - 1:
                            for d in range(2):
                                last = ts(SP[:, d, :], S[:, c % 2, d, :], PC[:, d, chunk_at[d][c]:chunk_at[d][c] + 1],
                                          None, ALU.mult)
                            chain(last)

                    def step_s(c):
                        dve.wait_ge(s_done.sem, s_done.base + (chunks - 1) * ft + c + 1)
                        for d in range(2):
                            for h in range(2):
                                own = slice(h * HEAD, (h + 1) * HEAD)
                                last = stt(S[own, 1 - c % 2, d, own], ps[own, 5 + d, own],
                                           PC[own, d, chunk_at[d][c]:chunk_at[d][c] + 1], SP[own, d, own],
                                           ALU.mult, ALU.add)
                        last.then_inc(s_kept.sem, 1)
                        dve.wait_ge(s_kept.sem, s_kept.base + (chunks - 1) * ft + c + 1)

                    for i in range(batches):
                        weave = woven(i)
                        for e, (name, keeper) in enumerate(exchanges(i)):
                            for h in range(2):
                                if keeper == "V":
                                    dve.wait_ge(product[h].sem, product[h].base + product_at[-1] * ft + product_at[i] + e + 1)
                                    keep(name, h, i)
                            if e in weave:
                                part, c = weave[e]
                                step_u(c) if part == "u" else step_s(c)
                    for c in range(chunks - per_batch, chunks):
                        step_u(c)
                        if c < chunks - 1:
                            step_s(c)
                    dve.wait_ge(intra.sem, intra.base + ft + 1)
                    dve.wait_ge(y_kept.sem, y_kept.base + (chunks - first_x) * (ft + 1))
                    chain(tt(YS[:, 0, :], YS[:, 0, :], YS[:, 1, :], ALU.add))
                    tt(YS[:, 0, :], ps[:, 0, :], YS[:, 0, :], ALU.add).then_inc(summed.sem, 1)
                    dve.wait_ge(mean.sem, mean.base + ft + 1)
                    dve.wait_ge(summed.sem, summed.base + ft + 1)
                    tt(YS[:, 1, :], YS[:, 0, :], ps[:, 1, :], ALU.subtract).then_inc(centred.sem, 1)
                    dve.wait_ge(var.sem, var.base + ft + 1)
                    chain(ts(VAR[:, 0:SEQ], ps[:, 2, :], GN_EPS, None, ALU.add))
                    nc.vector.reciprocal(VAR[:, 0:SEQ], VAR[:, 0:SEQ]).then_inc(ginv.sem, 1)
                    dve.wait_ge(groot.sem, groot.base + ft + 1)
                    dve.wait_ge(centred.sem, centred.base + ft + 1)
                    chain(stt(YS[:, 0, :], YS[:, 1, :], col(par["lng"], ft), VAR[:, 0:SEQ], ALU.mult, ALU.mult))
                    dve.wait_ge(bonus.sem, bonus.base + ft + 1)
                    chain(tt(BON[:, :], ps[:, 3, :], V[:, 0:SEQ], ALU.mult))
                    chain(stt(YS[:, 0, :], YS[:, 0, :], col(par["lnb"], ft), BON[:, :], ALU.add, ALU.add))
                    tt(tile(dst, ft), YS[:, 0, :], G[:, :], ALU.mult).then_inc(pair_done.sem, 1)
                    assert chain.steps == VSTEPS, chain.steps



COLUMNS = (
    ("ada_b0", 48), ("ada_b1", 48), ("b_ada_2", 48), ("norm_g", 2 * 4 * DT), ("ev_pool_scale", 4),
    ("rw_mu", 6 * DT), ("rw_w0", 2 * DT), ("rw_a0", 2 * DT), ("rw_kk", DT), ("rw_ka", DT), ("rw_rk", DT),
    ("rw_lng", DT), ("rw_lnb", DT), ("g_mix", DT), ("g_q_lat", 4), ("g_kv_lat", 2), ("g_q_head", 1),
    ("g_k_head", 1), ("g_dil_q", 1), ("g_dil_k", 1), ("g_ffn", DT), ("taps", 3 * 2 * FT2), ("b_conv", 2 * FT2),
)
CONSTANTS = (
    ("ident", P), ("ones", P), ("head_sum", P), ("head_mean", P), ("mla_mean", MLA_QK), ("mla_rotate", MLA_QK),
    ("dil_rotate", P), ("freqs", 2),
)
WKV_MASKS = ("strict", "inclusive", "minus_first_t", "ident") + LEVELS


def offsets(table):
    at, out = 0, {}
    for name, n in table:
        out[name] = (at, at + n)
        at += n
    return out, at


def load_all(core, pairs):
    landed = counter(core, "input_landed")
    with core.block() as block:
        @block.sync
        def _(sp):
            for dst, src in pairs:
                sp.dma_start(dst, src).then_inc(landed.sem, 16)
            sp.wait_ge(landed.sem, landed.base + 16 * len(pairs))
    landed.base += 16 * len(pairs)


def silu_rows(core, rows):
    nc = core.nc
    sigmoid, done = counter(core, "silu_sigmoid"), counter(core, "silu_done")
    with ExitStack() as scope:
        s = core.sb(scope, "silu_s", [P, len(rows), D])
        with core.block() as block:
            @block.scalar
            def _(eng):
                for n, row in enumerate(rows):
                    nc.scalar.activation(s[:, n, :], row, ACT.Sigmoid).then_inc(sigmoid.sem, 1)

            @block.vector
            def _(dve):
                for n, row in enumerate(rows):
                    dve.wait_ge(sigmoid.sem, sigmoid.base + n + 1)
                    nc.vector.tensor_tensor(row, row, s[:, n, :], ALU.mult).then_inc(done.sem, 1)
    sigmoid.base += len(rows)
    done.base += len(rows)


def gains(core, jobs):
    nc = core.nc
    done = counter(core, "gain_done")
    with core.block() as block:
        @block.vector
        def _(dve):
            for out, scale, gain, plus in jobs:
                nc.vector.scalar_tensor_tensor(out, scale, plus, gain, ALU.add, ALU.mult).then_inc(done.sem, 1)
    done.base += len(jobs)


def even_heads(core, q, k, v, queries, q0, out, bias_tile=None, bias_dram=None):
    heads = []
    ctx_tile = SEQ // P
    for h in range(8):
        rows = slice(h % 2 * HEAD, h % 2 * HEAD + HEAD)
        t = h // 2
        ctx_keys = k[rows, t, SEQ:T0]
        cols = slice(h * HEAD, (h + 1) * HEAD)
        if bias_tile is None:
            heads.append(Head(q[rows, t, q0:q0 + queries], queries, [ctx_keys],
                              lambda kt, cols=cols: v[:, ctx_tile + kt, cols],
                              Rows(out[rows, t, q0:q0 + queries], rows.start), HEAD ** -0.5))
        else:
            heads.append(Head(q[rows, t, q0:q0 + queries], queries, [k[rows, t, 0:SEQ], ctx_keys],
                              lambda kt, cols=cols: v[:, kt, cols],
                              Rows(out[rows, t, q0:q0 + queries], rows.start), HEAD ** -0.5,
                              bias=lambda i, h=h: bias_tile[:, h % 2, (6 - 2 * i) * GRID_W:(14 - 2 * i) * GRID_W],
                              bias_load=bias_dram[h, :, :]))
    return heads


def build(nc, io, stop=None):
    core = Core(nc)
    col_at, n_cols = offsets(COLUMNS)
    con_at, n_cons = offsets(CONSTANTS)
    scope = ExitStack()
    with scope:
        cols = core.sb(scope, "columns", [P, n_cols])
        cons = core.sb(scope, "constants", [P, n_cons])
        X = core.sb(scope, "residual", [P, DT, T0])
        mods = {name: core.sb(scope, f"mod_{name}", [P, N_MOD * DT]) for name in ("0x", "0c", "1x", "1c", "2x")}
        derived = core.sb(scope, "derived_gains", [P, 15, DT])

        def column(name, a=0, n=None):
            lo, hi = col_at[name]
            return cols[:, lo + a:hi if n is None else lo + a + n]

        def const(name):
            lo, hi = con_at[name]
            return cons[:, lo:hi]

        core.ident, core.ones = const("ident"), const("ones")
        core.head_sum, core.head_mean = const("head_sum"), const("head_mean")

        credit = [counter(core, n) for n in ("panel_done", "panel_evicted", "mod_tile_used", "gate_done", "pair_done",
                                           "panel_stored_0", "panel_stored_1",
                                           "triangle_kept_0", "triangle_kept_1", "factor_kept_0", "factor_kept_1")]
        with core.block() as block:
            @block.vector
            def _(dve):
                for i, s in enumerate(credit):
                    nc.vector.memset(derived[:, i, :], 0.0).then_inc(s.sem, CREDIT)
        for s in credit:
            s.base += CREDIT

        load_all(core, [(cols[:, :], io["columns"]), (cons[:, :], io["constants"]),
                        (X[:, :, 0:SEQ], io["x"].rearrange("(k p) t -> p k t", p=P)),
                        (X[:, :, SEQ:T0], io["ctx"].rearrange("(k p) t -> p k t", p=P))])

        rows_scope = ExitStack()
        rows = core.sb(rows_scope, "conditions", [P, 3, D])
        load_all(core, [(rows[:, n, :], io[name].to_broadcast([P, D]))
                        for n, name in enumerate(("c", "c_ctx", "c_2"))])
        silu_rows(core, [rows[:, n, :] for n in range(3)])
        c, cc, c2 = (rows[:, n, :] for n in range(3))
        mods0 = (column("ada_b0"), [c, cc], [mods["0x"], mods["0c"]])
        modulation(core, io["ada0"], 0, 2 * DT, *mods0)

        def mod(which, n):
            return mods[which][:, n * DT:(n + 1) * DT]

        def norm_g(layer, n):
            return column("norm_g", (4 * layer + n) * DT, DT)

        at = {}

        def derive(*jobs):
            todo = []
            for key, which, n, gain, plus in jobs:
                at[key] = derived[:, len(at), :]
                todo.append((at[key], mod(which, n), gain, plus))
            gains(core, todo)

        derive(("0x in", "0x", 1, norm_g(0, 0), 1.0), ("0c in", "0c", 1, norm_g(0, 0), 1.0))

        def both(key):
            return [(0, SEQ, at[f"0x {key}"]), (SEQ, T0, at[f"0c {key}"])]

        def evict_copy(dst):
            return lambda n, psum: nc.scalar.activation(
                halves(tile(dst, n)) if dst.shape[-1] == T0 else tile(dst, n), psum, ACT.Copy)

        def mlp(w1, w2, tokens, act, hidden_scope, out, beside=None):
            hidden = core.sb(hidden_scope, "hidden", [P, D_FF // P, tokens])

            def shaped(ap):
                return halves(ap) if tokens > 512 else ap

            gemm(core, w1, DT, D_FF // P, act, tokens,
                 act_evict=lambda n, psum: nc.scalar.activation(shaped(tile(hidden, n)), psum, ACT.Relu),
                 dve_evict=lambda n, psum, chain: nc.vector.tensor_tensor(shaped(tile(hidden, n)), psum,
                                                                          shaped(tile(hidden, n)), ALU.mult))
            gemm(core, w2, D_FF // P, DT, hidden, tokens, ring=2, bufs=2, **(beside() if beside else {}),
                 act_evict=lambda n, psum: nc.scalar.activation(shaped(tile(out, n)), psum, ACT.Copy))

        def finished(name):
            if stop != name:
                return False
            store(core, X[:, :, 0:SEQ], io["out"])
            return True

        with ExitStack() as s:
            H = core.sb(s, "h", [P, DT, T0])
            rms_stage(core, X, DT, T0, both("in"), [(0, SEQ, mod("0x", 0)), (SEQ, T0, mod("0c", 0))], H)
            with ExitStack() as s2:
                U = core.sb(s2, "u", [P, 12, T0])
                V = core.sb(s2, "v", [P, T0 // P, 512])
                CAT = core.sb(s2, "mixed", [P, DT, T0])
                with ExitStack() as s3:
                    m = Modulation(core, s3, io["ada0"], 2)
                    gemm(core, io["w_in"], DT, 12, H, T0, act_evict=evict_copy(U), bufs=2,
                         load_also=lambda sp, n, u: [m.load(sp, n * 2 + t + 2 * DT, n * 2 + t, t) for t in range(2)],
                         vector_also=lambda dve: m.vector(dve, 2 * DT, 3 * DT, *mods0))
                gemm_tokens(core, io["w_in_v"], DT, H, T0 // P, V)
                with ExitStack() as s3:
                    inv = core.sb(s3, "inverse_counts", [P, len(POOL_WINDOWS), T0])
                    load_all(core, [(inv[:, :, :], io["inv_count"].unsqueeze(0).to_broadcast([P, len(POOL_WINDOWS), T0]))])
                    pool_mixer(core, U, io["pool_w"], inv, column("ev_pool_scale"), CAT)
                with ExitStack() as s3:
                    bias = core.sb(s3, "grid_bias", [P, 2, 14 * GRID_W])
                    grid_mask = core.sb(s3, "grid_mask", [P, GRID_W])
                    load_all(core, [(grid_mask[:, :], io["grid_mask"])])
                    q, k = U[:, 4:8, :], U[:, 8:12, :]
                    attention(core, even_heads(core, q, k, V, SEQ, 0, CAT[:, 4:8, :], bias, io["bias"]), bias,
                              grid_mask[:, :].unsqueeze(1).to_broadcast([P, 14, GRID_W]))
                    attention(core, even_heads(core, q, k, V, CTX, SEQ, CAT[:, 4:8, :]))
                with ExitStack() as s3:
                    m = Modulation(core, s3, io["ada0"], 2)
                    gemm(core, io["w_out"], DT, DT, CAT, T0, act_evict=evict_copy(H), bufs=2,
                         load_also=lambda sp, n, u: m.load(sp, n + 5 * DT, n, u % 2),
                         vector_also=lambda dve: m.vector(dve, 5 * DT, DT, *mods0))
            derive(("0x mix", "0x", 2, norm_g(0, 1), 0.0), ("0c mix", "0c", 2, norm_g(0, 1), 0.0),
                   ("0x mlp", "0x", 4, norm_g(0, 2), 1.0), ("0c mlp", "0c", 4, norm_g(0, 2), 1.0),
                   ("0x out", "0x", 5, norm_g(0, 3), 0.0), ("0c out", "0c", 5, norm_g(0, 3), 0.0))
            rms_stage(core, H, DT, T0, both("mix"), residual=X)
            if finished("mix0"):
                return
            rms_stage(core, X, DT, T0, both("mlp"), [(0, SEQ, mod("0x", 3)), (SEQ, T0, mod("0c", 3))], H)
            with ExitStack() as s2:
                def beside():
                    m = Modulation(core, s2, io["ada12"], 2, junk=core.psum[:, 6:8, :].rearrange("p a t -> p (a t)"))
                    per = 2 * N_MOD * DT // DT

                    def vector(dve):
                        m.vector(dve, 0, N_MOD * DT, column("ada_b1"), [c, cc], [mods["1x"], mods["1c"]])
                        m.vector(dve, 0, N_MOD * DT, column("b_ada_2"), [c2], [mods["2x"]])

                    return {"vector_also": vector, "load_also": lambda sp, n, u: [
                        m.load(sp, n * per + t, n * per + t, t % 2) for t in range(per)]}

                mlp(io["mlp_w1_0"], io["mlp_w2_0"], T0, H, s2, H, beside)
            rms_stage(core, H, DT, T0, both("out"), residual=X)
        rows_scope.close()
        derive(("1x in", "1x", 1, norm_g(1, 0), 1.0), ("1c in", "1c", 1, norm_g(1, 0), 1.0),
               ("1x mix", "1x", 2, norm_g(1, 1), 0.0), ("1x mlp", "1x", 4, norm_g(1, 2), 1.0),
               ("1x out", "1x", 5, norm_g(1, 3), 0.0), ("2x in", "2x", 1, column("g_mix"), 1.0))
        if finished("layer0"):
            return

        names = ("k", "v", "r", "g")
        dram = {n: nc.dram_tensor(f"spilled_{n}", [DT, P, T0 if n in "kv" else SEQ], F32, kind="Internal").ap()
                for n in names}
        with ExitStack() as s0:
            LA = core.sb(s0, "lora_inputs", [P, 2, T0])
            ZT = core.sb(s0, "wkv_out", [P, DT, SEQ])
            segs = ((0, SEQ), (SEQ, T0))
            with ExitStack() as s:
                H = core.sb(s, "h", [P, DT, T0])
                M = [core.sb(s, f"mixed_tokens_{n}", [P, DT, T0]) for n in range(2)]
                DIFF = core.sb(s, "neighbour_difference", [P, DT, T0])
                rms_stage(core, X, DT, T0, [(0, SEQ, at["1x in"]), (SEQ, T0, at["1c in"])],
                          [(0, SEQ, mod("1x", 0)), (SEQ, T0, mod("1c", 0))], H)
                mu = [column("rw_mu", j * DT, DT) for j in range(6)]
                neighbour_difference(core, H, segs, DIFF, lambda dve: token_mix(core, dve, H, DIFF, mu[0], M[0]))

                def mixing(j, dst):
                    return lambda dve: token_mix(core, dve, H, DIFF, mu[j], dst)

                gemm(core, io["rw_wr"], DT, DT, M[0][:, :, 0:SEQ], SEQ, store=dram["r"], vector_also=mixing(2, M[1]))
                gemm(core, io["rw_wk"], DT, DT, M[1], T0, store=dram["k"], vector_also=mixing(3, M[0]))
                gemm(core, io["rw_wv"], DT, DT, M[0], T0, store=dram["v"], vector_also=mixing(1, M[1]))
                gemm(core, io["rw_w1"], DT, 1, M[1], T0, vector_also=mixing(4, M[0]),
                     act_evict=lambda n, psum: nc.scalar.activation(halves(LA[:, 0, :]), psum, ACT.Tanh))
                gemm(core, io["rw_a1"], DT, 1, M[0], T0, vector_also=mixing(5, M[1]),
                     act_evict=lambda n, psum: nc.scalar.activation(halves(LA[:, 1, :]), psum, ACT.Copy))
                gemm(core, io["rw_g1"], DT, 1, M[1][:, :, 0:SEQ], SEQ, act_evict=lambda n, psum: nc.scalar.activation(
                    M[0][:, 0, 0:SEQ], psum, ACT.Sigmoid))
                gemm(core, io["rw_g2"], 1, DT, M[0][:, 0:1, 0:SEQ], SEQ, store=dram["g"])
            with ExitStack() as s:
                tall = core.sb(s, "wkv_masks", [P, len(WKV_MASKS), 2 * P])
                resets = core.sb(s, "wkv_resets", [P, T0])
                load_all(core, [(tall[:, :, :], io["wkv_masks"]),
                                (resets[:, :], io["wkv_resets"].to_broadcast([P, T0]))])
                masks = {name: tall[:, i, :] for i, name in enumerate(WKV_MASKS)}
                masks["resets"] = resets[:, :]
                par = {"w0": [column("rw_w0", d * DT, DT) for d in range(2)],
                       "a0": [column("rw_a0", d * DT, DT) for d in range(2)],
                       "kk": column("rw_kk"), "ka": column("rw_ka"), "rk": column("rw_rk"),
                       "lng": column("rw_lng"), "lnb": column("rw_lnb")}
                wkv(core, LA[:, 0, :], LA[:, 1, :], io["lora_up"], dram["k"], dram["v"], dram["r"], dram["g"], par,
                    masks, ZT)
            with ExitStack() as s:
                H = core.sb(s, "h", [P, DT, SEQ])
                gemm(core, io["rw_wo"], DT, DT, ZT, SEQ, act_evict=evict_copy(H))
                if stop == "wo1":
                    store(core, H[:, :, 0:SEQ], io["out"])
                    return
                rms_stage(core, H, DT, SEQ, [(0, SEQ, at["1x mix"])], residual=X)
                if finished("mix1"):
                    return
                rms_stage(core, X, DT, SEQ, [(0, SEQ, at["1x mlp"])], [(0, SEQ, mod("1x", 3))], H)
                with ExitStack() as s2:
                    mlp(io["mlp_w1_1"], io["mlp_w2_1"], SEQ, H, s2, H)
                rms_stage(core, H, DT, SEQ, [(0, SEQ, at["1x out"])], residual=X)
        if finished("layer1"):
            return

        derive(("2x mlp", "2x", 4, column("g_ffn"), 1.0))
        with ExitStack() as s:
            H = core.sb(s, "h", [P, DT, SEQ])
            MIX = core.sb(s, "mix", [P, DT, SEQ])
            rms_stage(core, X, DT, SEQ, [(0, SEQ, at["2x in"])], [(0, SEQ, mod("2x", 0))], H)
            cs = core.sb(s, "rotation", [P, 2, 2, SEQ])
            rotation_tables(core, io["positions"], const("freqs"),
                            [(cs[:, 0, 0, :], cs[:, 0, 1, :]), (cs[:, 1, 0, :], cs[:, 1, 1, :])])
            with ExitStack() as s2:
                LAT = core.sb(s2, "latents", [P, 6, SEQ])
                QM, KM = core.sb(s2, "q_mla", [P, 8, SEQ]), core.sb(s2, "k_mla", [P, 8, SEQ])
                VM = core.sb(s2, "v_mla", [P, SEQ // P, 512])
                mask = core.sb(s2, "causal_bias", [P, 2, 512])
                load_all(core, [(mask[:, :, :], io["causal_bias"])])
                gemm(core, io["w_lat"], DT, 6, H, SEQ, act_evict=evict_copy(LAT))
                rows = slice(MLA_NOPE, MLA_QK)
                gemm(core, io["w_kpe"], DT, 1, H, SEQ, m=MLA_ROPE, m0=MLA_NOPE, act_evict=lambda n, psum:
                     nc.scalar.activation(KM[rows, :, :], psum.unsqueeze(1).to_broadcast([MLA_ROPE, 8, SEQ]), ACT.Copy))
                rms_stage(core, LAT[:, 0:4, :], 4, SEQ, [(0, SEQ, column("g_q_lat"))], dst=LAT[:, 0:4, :])
                rms_stage(core, LAT[:, 4:6, :], 2, SEQ, [(0, SEQ, column("g_kv_lat"))], dst=LAT[:, 4:6, :])
                gemm(core, io["w_q_b"], 4, 8, LAT[:, 0:4, :], SEQ, m=MLA_QK, act_evict=evict_copy(QM[0:MLA_QK, :, :]))
                gemm(core, io["w_kv_b"], 2, 8, LAT[:, 4:6, :], SEQ, m=MLA_NOPE,
                     act_evict=evict_copy(KM[0:MLA_NOPE, :, :]))
                gemm_tokens(core, io["w_kv_v"], 2, LAT[:, 4:6, :], SEQ // P, VM)
                q96 = slice(0, MLA_QK)
                for t, g in ((QM, "g_q_head"), (KM, "g_k_head")):
                    head_norm(core, t, MLA_QK, 8, const("mla_mean")[q96, :], column(g)[q96, :],
                              const("mla_rotate")[q96, :], cs[q96, 0, 0, :], cs[q96, 0, 1, :])
                attention(core, [Head(QM[0:MLA_QK, h, :], SEQ, [KM[0:MLA_QK, h, :]],
                                      lambda kt, h=h: VM[:, kt, h * HEAD:(h + 1) * HEAD],
                                      Rows(MIX[h % 2 * HEAD:h % 2 * HEAD + HEAD, h // 2, :], h % 2 * HEAD),
                                      MLA_QK ** -0.5, bias=lambda i: mask[:, 0, (3 - i) * P:512], causal=True)
                                 for h in range(8)])
                QD, KD = QM[:, 0:4, :], KM[:, 0:4, :]
                gemm(core, io["w_qd"], DT, 4, H, SEQ, act_evict=evict_copy(QD))
                gemm(core, io["w_kd"], DT, 4, H, SEQ, act_evict=evict_copy(KD))
                gemm_tokens(core, io["w_vd"], DT, H, SEQ // P, VM)
                for t, g in ((QD, "g_dil_q"), (KD, "g_dil_k")):
                    head_norm(core, t, P, 4, const("head_mean"), column(g), const("dil_rotate"),
                              cs[:, 1, 0, :], cs[:, 1, 1, :])
                attention(core, [Head(QD[h % 2 * HEAD:h % 2 * HEAD + HEAD, h // 2, :], SEQ,
                                      [KD[h % 2 * HEAD:h % 2 * HEAD + HEAD, h // 2, :]],
                                      lambda kt, h=h: VM[:, kt, h * HEAD:(h + 1) * HEAD],
                                      Rows(MIX[h % 2 * HEAD:h % 2 * HEAD + HEAD, 4 + h // 2, :], h % 2 * HEAD),
                                      HEAD ** -0.5, bias=lambda i: mask[:, 1, (3 - i) * P:512], causal=True)
                                 for h in range(8)])
            gate1, gate2 = mod("2x", 2), mod("2x", 5)
            gemm(core, io["w_o"], DT, DT, MIX, SEQ, dve_evict=lambda n, psum, chain: nc.vector.scalar_tensor_tensor(
                tile(X, n)[:, 0:SEQ], psum, col(gate1, n), tile(X, n)[:, 0:SEQ], ALU.mult, ALU.add))
            if finished("mix2"):
                return
            rms_stage(core, X, DT, SEQ, [(0, SEQ, at["2x mlp"])], [(0, SEQ, mod("2x", 3))], H)
            with ExitStack() as s2:
                G = core.sb(s2, "gated", [P, FT2, SEQ])
                taps = column("taps").rearrange("p (j n) -> p j n", j=3)
                conv_mlp(core, io["w_up"], H, taps, column("b_conv"), G)
                gemm(core, io["w_down"], FT2, DT, G, SEQ, ring=2,
                     dve_evict=lambda n, psum, chain: nc.vector.scalar_tensor_tensor(
                         tile(X, n)[:, 0:SEQ], psum, col(gate2, n), tile(X, n)[:, 0:SEQ], ALU.mult, ALU.add))
        store(core, X[:, :, 0:SEQ], io["out"])


def store(core, src, out):
    stored = counter(core, "output_stored")
    with core.block() as block:
        @block.sync
        def _(sp):
            sp.dma_start(out.rearrange("(k p) t -> p k t", p=P), src).then_inc(stored.sem, 16)
            sp.wait_ge(stored.sem, stored.base + 16)
    stored.base += 16



def panels(w, m=P):
    k, n = w.shape
    return w.reshape(k // P, P, n // m, m).transpose(2, 1, 0, 3).reshape(n // m, P, k // P * m)


def columns(v):
    return v.reshape(-1, P).T


def padded_column(v):
    out = np.zeros((P, 1), v.dtype)
    out[:len(v), 0] = v
    return out


def constants():
    f = np.float32
    out = {"ident": np.eye(P, dtype=f), "ones": np.ones((P, P), f)}
    head = np.kron(np.eye(2, dtype=f), np.ones((HEAD, HEAD), f))
    out["head_sum"], out["head_mean"] = head, head / f(HEAD)
    mean = np.zeros((P, MLA_QK), f)
    mean[:MLA_NOPE, :MLA_NOPE] = 1 / MLA_NOPE
    mean[MLA_NOPE:MLA_QK, MLA_NOPE:] = 1 / MLA_ROPE
    out["mla_mean"] = mean

    def rotate(size, start, n):
        m = np.zeros((P, n), f)
        for j in range(size // 2):
            m[start + j + size // 2, start + j] = -1
            m[start + j, start + j + size // 2] = 1
        return m

    out["mla_rotate"] = rotate(MLA_ROPE, MLA_NOPE, MLA_QK)
    out["dil_rotate"] = rotate(HEAD, 0, P) + rotate(HEAD, HEAD, P)

    def freqs(d):
        half = d // 2
        e = (f(-2.0) * np.arange(half, dtype=f)) / f(d)
        return np.tile(np.power(f(ROPE_THETA), e).astype(f), 2)

    fr = np.zeros((P, 2), f)
    fr[MLA_NOPE:MLA_QK, 0] = freqs(MLA_ROPE)
    fr[:, 1] = np.tile(freqs(HEAD), 2)
    out["freqs"] = fr
    return np.concatenate([out[n] for n, _ in CONSTANTS], axis=1)


def inverse_counts():
    out = np.zeros((len(POOL_WINDOWS), T0), np.float32)
    for g, w in enumerate(POOL_WINDOWS):
        for t0, n in ((0, SEQ), (SEQ, CTX)):
            t = np.arange(n)
            out[g, t0:t0 + n] = 1.0 / (np.clip(t + w // 2, 0, n) - np.clip(t - w // 2, 0, n))
    return out


def grid_columns():
    c = np.arange(GRID_W)
    start = np.clip(c - WIN_C // 2, 0, GRID_W - WIN_C)
    ok = (c[None, :] >= start[:, None]) & (c[None, :] < start[:, None] + WIN_C)
    return np.tile(np.where(ok, 0, NEG).astype(np.float32), (2, 1))


def grid_bias(rpb):
    c = np.arange(GRID_W)
    dc = np.clip(c[None, :] - c[:, None], -(WIN_C - 1), WIN_C - 1) + WIN_C - 1
    full = rpb[:, :, dc].transpose(0, 2, 1, 3)
    return np.concatenate([full[:, :, 1:15], full[:, :, 0:14]], axis=1).reshape(rpb.shape[0], P, 14 * GRID_W)


def causal_biases():
    q = np.arange(P)[:, None]
    k = np.arange(512)[None, :] - 3 * P
    dist = q - k
    causal = np.where(dist >= 0, 0.0, NEG)
    count = sum(((dist >= 0) & (dist % dil == 0) & (dist // dil <= window // dil)).astype(int)
                for window, dil in DIL_PATTERNS)
    dil = np.where(count > 0, np.log(np.maximum(count, 1)), NEG)
    return np.stack([causal, dil], axis=1).astype(np.float32)


def wkv_masks():
    i, j = np.arange(P)[:, None], np.arange(P)[None, :]
    same = i // CHUNK == j // CHUNK

    def level(n):
        return (i // (2 * n) == j // (2 * n)) & (i // n > j // n)

    both = {"strict": (same & (i < j), same & (i > j)), "inclusive": (same & (i <= j), same & (i >= j)),
            "minus_first_t": (-1.0 * level(1).T, -1.0 * level(1)),
            "ident": (i == j, i == j)}
    for n in LEVELS:
        both[n] = (level(n).T, level(n))
    return np.stack([np.concatenate(both[n], axis=1) for n in WKV_MASKS], axis=1).astype(np.float32)


def lay_out(i):
    f = {k: np.asarray(v) for k, v in i.items()}
    win, win2 = f["ev_w_in"][0], f["w_in_2"][0]
    taps = f["w_conv_2"][0].reshape(3, 2, FT2, P).transpose(0, 2, 1, 3).reshape(-1)
    bconv = f["b_conv_2"][0].reshape(2, FT2, P).transpose(1, 0, 2).reshape(-1)
    col = {
        "ada_b0": f["ada_b"][0], "ada_b1": f["ada_b"][1], "b_ada_2": f["b_ada_2"][0], "norm_g": f["norm_g"],
        "ev_pool_scale": f["ev_pool_scale"], "rw_mu": f["rw_mu"], "rw_w0": f["rw_w0"], "rw_a0": f["rw_a0"],
        "rw_kk": f["rw_kk"], "rw_ka": f["rw_ka"], "rw_rk": f["rw_rk"], "rw_lng": f["rw_lng"], "rw_lnb": f["rw_lnb"],
        "g_mix": f["g_mix_norm_2"], "g_q_lat": f["g_q_lat_2"], "g_kv_lat": f["g_kv_lat_2"],
        "g_q_head": np.concatenate([f["g_mla_q_nope_2"][0], f["g_mla_q_pe_2"][0]]),
        "g_k_head": np.concatenate([f["g_mla_k_nope_2"][0], f["g_mla_k_pe_2"][0]]),
        "g_dil_q": np.tile(f["g_dil_q_2"][0], 2), "g_dil_k": np.tile(f["g_dil_k_2"][0], 2), "g_ffn": f["g_ffn_norm_2"],
        "taps": taps, "b_conv": bconv,
    }
    cols = [padded_column(col[n].reshape(-1)) if col[n].size < P else columns(col[n].reshape(-1)) for n, _ in COLUMNS]
    q0 = Q_LORA + KV_LORA
    d0 = q0 + MLA_ROPE
    qb = f["w_q_b_2"][0]
    kvb = f["w_kv_b_2"][0].reshape(KV_LORA, MLA_HEADS, 2 * HEAD)
    up = f["w_up_2"][0].reshape(D, 2, FT2, P).transpose(0, 2, 1, 3).reshape(D, 2 * D_FF2)
    lora_up = np.concatenate([f["rw_w2"][0].reshape(P, DT, P), f["rw_a2"][0].reshape(P, DT, P)], axis=2).transpose(1, 0, 2)
    token_weights = lambda w: w.reshape(-1, P, 512).transpose(1, 0, 2).reshape(P, -1)
    out = {
        "x": f["x"][0].T, "ctx": f["ctx"][0].T, "c": f["c"].reshape(1, D), "c_ctx": f["c_ctx"].reshape(1, D),
        "c_2": f["c_2"].reshape(1, D), "positions": f["positions_2"].reshape(1, SEQ),
        "columns": np.concatenate(cols, axis=1), "constants": constants(),
        "ada0": f["ada_w"][0].T.reshape(48, P, D), "ada12": np.concatenate([f["ada_w"][1].T, f["w_ada_2"][0].T]).reshape(96, P, D),
        "w_in": panels(win[:, 0:1536]), "w_in_v": token_weights(win[:, 1536:]), "w_out": panels(f["ev_w_out"][0]),
        "pool_w": f["ev_pool_w"][0], "inv_count": inverse_counts(), "grid_mask": grid_columns(),
        "bias": grid_bias(f["ev_rpb"][0]),
        "mlp_w1_0": panels(f["mlp_w1"][0]), "mlp_w2_0": panels(f["mlp_w2"][0]),
        "mlp_w1_1": panels(f["mlp_w1"][1]), "mlp_w2_1": panels(f["mlp_w2"][1]),
        "rw_wr": panels(f["rw_wr"][0]), "rw_wk": panels(f["rw_wk"][0]), "rw_wv": panels(f["rw_wv"][0]),
        "rw_wo": panels(f["rw_wo"][0]),
        "rw_w1": panels(np.concatenate([f["rw_w1"][0, 0], f["rw_w1"][0, 1]], axis=1)),
        "rw_a1": panels(np.concatenate([f["rw_a1"][0, 0], f["rw_a1"][0, 1]], axis=1)),
        "rw_g1": panels(f["rw_g1"][0]), "rw_g2": panels(f["rw_g2"][0]), "lora_up": lora_up,
        "wkv_masks": wkv_masks(), "wkv_resets": (np.arange(T0) % CHUNK != 0).astype(np.float32).reshape(1, T0),
        "w_lat": panels(win2[:, 0:q0]), "w_kpe": panels(win2[:, q0:d0], MLA_ROPE),
        "w_q_b": panels(qb, MLA_QK), "w_kv_b": panels(kvb[:, :, :MLA_NOPE].reshape(KV_LORA, -1), MLA_NOPE),
        "w_kv_v": token_weights(kvb[:, :, MLA_NOPE:].reshape(KV_LORA, -1)),
        "w_qd": panels(win2[:, d0:d0 + 512]), "w_kd": panels(win2[:, d0 + 512:d0 + 1024]),
        "w_vd": token_weights(win2[:, d0 + 1024:]), "causal_bias": causal_biases(),
        "w_o": panels(f["w_o_2"][0]), "w_up": panels(up), "w_down": panels(f["w_down_2"][0]),
    }
    return {k: np.ascontiguousarray(v) for k, v in out.items()}


def kernel(**inputs):
    import concourse.bacc as bacc
    from concourse.bass_utils import run_bass_kernel_spmd

    arrays = lay_out(inputs)
    nc = bacc.Bacc("TRN2", target_bir_lowering=False, num_devices=1)
    io = {n: nc.dram_tensor(f"in_{n}", a.shape, mybir.dt.from_np(a.dtype), kind="ExternalInput").ap()
          for n, a in arrays.items()}
    io["out"] = nc.dram_tensor("out", (D, SEQ), F32, kind="ExternalOutput").ap()
    build(nc, io)
    result = run_bass_kernel_spmd(nc, [{f"in_{n}": a for n, a in arrays.items()}], core_ids=[0])
    return np.ascontiguousarray(result.results[0]["out"].T).reshape(1, SEQ, D)
```

```python
from contextlib import ExitStack

import numpy as np

import concourse.bass as bass
from concourse import mybir

F32 = mybir.dt.float32
F32R = mybir.dt.float32r
I32 = mybir.dt.int32
ALU = mybir.AluOpType
ACT = mybir.ActivationFunctionType
AX = mybir.AxisListType

P = 128
D = 1024
SEQ = 512
CTX = 256
T0 = SEQ + CTX
DT = D // P
N_MOD = 6
EPS = 1e-6
CREDIT = 16

POOL_WINDOWS = (2, 4, 8, 16)
D_FF = 4 * D
HEAD = 64
GRID_W = 64
WIN_R, WIN_C = 8, 16
ROWS = SEQ // GRID_W
NEG = -1e30

D_FF2 = 2816
FT2 = D_FF2 // P
MLA_HEADS, MLA_NOPE, MLA_ROPE = 8, 64, 32
MLA_QK = MLA_NOPE + MLA_ROPE
Q_LORA, KV_LORA = 512, 256
DIL_PATTERNS = ((128, 1), (512, 4), (2048, 16))
ROPE_THETA = 10000.0

RW_HEADS = D // HEAD
GN_EPS = 64e-5
CHUNK = 64
DECAY_SCALE = float(np.exp(-0.5))
LEVELS = tuple(2 ** i for i in range(1, CHUNK.bit_length() - 1))


class Signal:

    def __init__(self, nc, name):
        self.sem = nc.alloc_semaphore(name)
        self.base = 0


class Core:

    def __init__(self, nc):
        self.nc = nc
        self.counters = {}
        self.stages = 0
        self.psum = nc.alloc_psum_tensor("psum", [P, 8, 512], F32)

    def block(self):
        self.stages += 1
        return self.nc.Block(no_gpsimd_drain=True)

    def sb(self, scope, name, shape, dtype=F32):
        self.stages += 1
        return scope.enter_context(self.nc.sbuf_tensor(f"{name}_{self.stages}", shape, dtype))


def counter(core, name):
    if name not in core.counters:
        core.counters[name] = Signal(core.nc, name)
    return core.counters[name]


class Chain:

    def __init__(self, eng, signal, start):
        self.eng, self.counter, self.start, self.steps = eng, signal, start, 0

    def __call__(self, instruction):
        self.steps += 1
        instruction.then_inc(self.counter.sem, 1)
        self.eng.wait_ge(self.counter.sem, self.start + self.steps)


def tile(ap, n):
    if isinstance(n, int):
        return ap[:, n, :]
    return ap[:, bass.ds(n, 1), :].rearrange("p a t -> p (a t)")


def col(ap, n):
    return ap[:, n:n + 1] if isinstance(n, int) else ap[:, bass.ds(n, 1)]


def halves(ap):
    return ap.rearrange("p (a t) -> p a t", a=2)



def gemm(core, weights, kt, nt, act, tokens, act_evict=None, dve_evict=None, m=P, m0=0, kp=P, k0=0,
         dve_steps=0, ring=4, bufs=4, store=None, load_also=None, vector_also=None):
    nc = core.nc
    wide = tokens > 512
    landed = [counter(core, f"panel_landed_{s}") for s in range(4)]
    done, evicted, first = counter(core, "panel_done"), counter(core, "panel_evicted"), counter(core, "panel_first_evict")
    steps = counter(core, "gemm_vector_step")
    looped = nt % 4 == 0 and nt > 4
    landed_base = [s.base for s in landed]
    stored = [counter(core, f"panel_stored_{s}") for s in range(2)]

    def place(n):
        s = n % bufs
        if wide:
            return core.psum[m0:m0 + m, 2 * s:2 * s + 2, 0:tokens // 2]
        return core.psum[m0:m0 + m, s, 0:tokens]

    def panels(eng, ring=ring):
        if looped:
            with eng.Fori(0, nt // 4) as blk:
                for u in range(4):
                    yield blk * 4 + u, u, blk * (4 // ring) + u // ring
        else:
            for n in range(nt):
                yield n, n, n // ring

    with ExitStack() as scope:
        panel = core.sb(scope, "panels", [P, ring, kt * m])
        staged = core.sb(scope, "staged", [P, 2, tokens]) if store is not None else None
        with core.block() as block:
            @block.sync
            def _(sp):
                for n, u, turn in panels(sp):
                    sp.wait_ge(done.sem, done.base + n + 1 - ring)
                    src = weights[n, :, :] if isinstance(n, int) else \
                        weights[bass.ds(n, 1), :, :].rearrange("a p k -> p (a k)")
                    sp.dma_start(panel[k0:k0 + kp, u % ring, :], src).then_inc(landed[u % ring].sem, 16)
                    if load_also is not None:
                        load_also(sp, n, u)

            @block.tensor
            def _(pe):
                for n, u, turn in panels(pe):
                    pe.wait_ge(landed[u % ring].sem, landed_base[u % ring] + 16 * (turn + 1))
                    pe.wait_ge(evicted.sem, evicted.base + n + 1 - bufs)
                    out = place(u)
                    for k in range(kt):
                        w = panel[k0:k0 + kp, u % ring, k * m:(k + 1) * m]
                        if wide:
                            for a in range(2):
                                last = nc.tensor.matmul(out[:, a, :], w, act[:, k, a * tokens // 2:(a + 1) * tokens // 2],
                                                        start=k == 0, stop=k == kt - 1)
                        else:
                            last = nc.tensor.matmul(out, w, act[:, k, :], start=k == 0, stop=k == kt - 1)
                    last.then_inc(done.sem, 1)

            if act_evict is not None:
                @block.scalar
                def _(eng):
                    for n, u, turn in panels(eng):
                        eng.wait_ge(done.sem, done.base + n + 1)
                        act_evict(n, place(u)).then_inc(first.sem if dve_evict else evicted.sem, 1)

            if store is not None:
                @block.scalar
                def _(eng):
                    for n, u, pair in panels(eng, 2):
                        eng.wait_ge(done.sem, done.base + n + 1)
                        eng.wait_ge(stored[u % 2].sem, stored[u % 2].base + 16 * pair)
                        o = staged[:, u % 2, :]
                        nc.scalar.activation(halves(o) if wide else o, place(u), ACT.Copy).then_inc(evicted.sem, 1)
                        eng.wait_ge(evicted.sem, evicted.base + n + 1)
                        eng.dma_start(store[n, :, :] if isinstance(n, int) else
                                      store[bass.ds(n, 1), :, :].rearrange("a p t -> p (a t)"), o)\
                            .then_inc(stored[u % 2].sem, 16)
                    for slot in range(2):
                        eng.wait_ge(stored[slot].sem, stored[slot].base + 16 * (nt // 2))

            if vector_also is not None:
                @block.vector
                def _(dve):
                    vector_also(dve)

            if dve_evict is not None:
                @block.vector
                def _(dve):
                    for n, u, turn in panels(dve):
                        if act_evict is not None:
                            dve.wait_ge(first.sem, first.base + n + 1)
                        else:
                            dve.wait_ge(done.sem, done.base + n + 1)
                        chain = Chain(dve, steps, steps.base + n * dve_steps)
                        dve_evict(n, place(u), chain).then_inc(evicted.sem, 1)
                        assert chain.steps == dve_steps

    for s in range(ring):
        landed[s].base += 16 * len(range(s, nt, ring))
    if store is not None:
        for slot in range(2):
            stored[slot].base += 16 * (nt // 2)
    done.base += nt
    evicted.base += nt
    if act_evict is not None and dve_evict is not None:
        first.base += nt
    steps.base += nt * dve_steps


def gemm_tokens(core, weights, kt, act, tiles, dst):
    nc = core.nc
    landed, done, out = counter(core, "value_weights_landed"), counter(core, "panel_done"), counter(core, "panel_evicted")
    with ExitStack() as scope:
        w = core.sb(scope, "value_weights", [P, kt * 512])
        with core.block() as block:
            @block.sync
            def _(sp):
                sp.dma_start(w[:, :], weights).then_inc(landed.sem, 16)

            @block.tensor
            def _(pe):
                pe.wait_ge(landed.sem, landed.base + 16)
                for t in range(tiles):
                    pe.wait_ge(out.sem, out.base + t + 1 - 8)
                    for k in range(kt):
                        last = nc.tensor.matmul(core.psum[:, t % 8, :], act[:, k, t * P:(t + 1) * P],
                                                w[:, k * 512:(k + 1) * 512], start=k == 0, stop=k == kt - 1)
                    last.then_inc(done.sem, 1)

            @block.scalar
            def _(eng):
                for t in range(tiles):
                    eng.wait_ge(done.sem, done.base + t + 1)
                    nc.scalar.activation(dst[:, t, :], core.psum[:, t % 8, :], ACT.Copy).then_inc(out.sem, 1)
    landed.base += 16
    done.base += tiles
    out.base += tiles



class Split:

    def __init__(self, core, scope, name, shape):
        self.high = core.sb(scope, f"{name}_high", shape, F32R)
        self.low = core.sb(scope, f"{name}_low", shape, F32R)
        self.ready = None


class Phase:

    def __init__(self, weights, kc, chunks, nt, act, evict, k_first=0):
        self.weights, self.kc, self.chunks, self.nt = weights, kc, chunks, nt
        self.act, self.evict, self.k_first = act, evict, k_first
        self.jobs = nt * chunks


def gemm_split(core, phases, tokens):
    nc = core.nc
    wide = tokens > 512
    ring, parts, ahead = 4, 2, 2
    landed = [counter(core, f"panel_landed_{s}") for s in range(ring)]
    high, split = counter(core, "weights_high"), counter(core, "weights_split")
    done, out_done = counter(core, "chunk_done"), counter(core, "panel_evicted")
    bufs = min(ring // ph.chunks for ph in phases)
    size = phases[0].kc * P
    for ph in phases:
        assert ph.jobs % ring == 0 and ring % ph.chunks == 0 and ph.kc * P == size
        ph.high0, ph.split0 = high.base, split.base
        ph.landed0 = [s.base for s in landed]
        ph.done0, ph.out0 = done.base, out_done.base
        ph.ready = ph.act.ready
        for s in landed:
            s.base += 16 * (ph.jobs // ring)
        high.base += ph.jobs
        split.base += ph.jobs
        done.base += ph.jobs
        ph.evict.begin(ph.nt)

    def place(n):
        s = n % bufs
        return core.psum[:, 2 * s:2 * s + 2, 0:tokens // 2] if wide else core.psum[:, s, 0:tokens]

    with ExitStack() as scope:
        raw = core.sb(scope, "raw_weights", [P, ring, size])
        w = Split(core, scope, "weights", [P, parts, size])
        with core.block() as block:
            @block.sync
            def _(sp):
                for ph in phases:
                    with sp.Fori(0, ph.jobs // ring) as blk:
                        for u in range(ring):
                            sp.wait_ge(split.sem, ph.split0 + blk * ring + u + 1 - ring)
                            at = (ph.k_first + u % ph.chunks * ph.kc) * P
                            n = blk * (ring // ph.chunks) + u // ph.chunks
                            sp.dma_start(raw[:, u, :], ph.weights[bass.ds(n, 1), :, at:at + size]
                                         .rearrange("a p k -> p (a k)")).then_inc(landed[u].sem, 16)

            @block.tensor
            def _(pe):
                for ph in phases:
                    if ph.ready is not None:
                        pe.wait_ge(*ph.ready)
                    with pe.Fori(0, ph.jobs // ring) as blk:
                        for u in range(ring):
                            chunk, panel = u % ph.chunks, u // ph.chunks
                            pe.wait_ge(split.sem, ph.split0 + blk * ring + u + 1)
                            if chunk == 0:
                                pe.wait_ge(out_done.sem, ph.out0 + blk * (ring // ph.chunks) + panel + 1 - bufs)
                            out = place(panel)
                            for k in range(ph.kc):
                                cols, act_k = slice(k * P, (k + 1) * P), chunk * ph.kc + k
                                passes = ((w.high, ph.act.high), (w.high, ph.act.low), (w.low, ph.act.high))
                                for i, (wp, ap) in enumerate(passes):
                                    first = chunk == 0 and k == 0 and i == 0
                                    final = chunk == ph.chunks - 1 and k == ph.kc - 1 and i == len(passes) - 1
                                    for a in range(2 if wide else 1):
                                        t0, t1 = (a * tokens // 2, (a + 1) * tokens // 2) if wide else (0, tokens)
                                        last = nc.tensor.matmul(out[:, a, :] if wide else out, wp[:, u % parts, cols],
                                                                ap[:, act_k, t0:t1], start=first, stop=final)
                            last.then_inc(done.sem, 1)

            def work(eng, part, take):
                for j in range(ahead):
                    part(phases[0], j, 0, j)

                def one(at, turn, u, last_block):
                    ph, v = phases[at], u + ahead
                    if v < ring or not last_block:
                        part(ph, turn * ring + v, turn + v // ring, v % ring)
                    elif at + 1 < len(phases):
                        part(phases[at + 1], v - ring, 0, v - ring)
                    if u % ph.chunks == ph.chunks - 1:
                        n = turn * (ring // ph.chunks) + u // ph.chunks
                        take(ph, n, turn, u, place(u // ph.chunks), ph.done0 + turn * ring + u + 1)

                for at, ph in enumerate(phases):
                    n_blocks = ph.jobs // ring
                    with eng.Fori(0, n_blocks - 1) as blk:
                        for u in range(ring):
                            one(at, blk, u, False)
                    for u in range(ring):
                        one(at, n_blocks - 1, u, True)

            @block.scalar
            def _(eng):
                def part(ph, j, turn, u):
                    eng.wait_ge(landed[u].sem, ph.landed0[u] + 16 * (turn + 1))
                    eng.wait_ge(done.sem, ph.done0 + j + 1 - parts)
                    nc.scalar.activation(w.high[:, u % parts, :], raw[:, u, :], ACT.Copy).then_inc(high.sem, 1)

                work(eng, part, lambda ph, n, turn, u, psum, count:
                     ph.evict.scalar(eng, n, turn, u, psum, done.sem, count))

            @block.vector
            def _(eng):
                def part(ph, j, turn, u):
                    eng.wait_ge(high.sem, ph.high0 + j + 1)
                    nc.vector.tensor_tensor(w.low[:, u % parts, :], raw[:, u, :], w.high[:, u % parts, :].bitcast(F32),
                                            ALU.subtract).then_inc(split.sem, 1)

                work(eng, part, lambda ph, n, turn, u, psum, count:
                     ph.evict.vector(eng, n, turn, u, psum, done.sem, count))


class Eviction:

    def __init__(self, core):
        self.core, self.out = core, counter(core, "panel_evicted")

    def scalar(self, eng, n, turn, u, psum, done, count):
        pass

    def vector(self, eng, n, turn, u, psum, done, count):
        pass

    def begin(self, nt):
        self.out0 = self.out.base
        self.out.base += nt


class ScalarEviction(Eviction):

    def __init__(self, core, op):
        super().__init__(core)
        self.op = op

    def scalar(self, eng, n, turn, u, psum, done, count):
        eng.wait_ge(done, count)
        self.op(n, psum).then_inc(self.out.sem, 1)


class VectorEviction(Eviction):

    def __init__(self, core, op):
        super().__init__(core)
        self.op = op

    def vector(self, eng, n, turn, u, psum, done, count):
        eng.wait_ge(done, count)
        self.op(n, psum).then_inc(self.out.sem, 1)


class SquaredRelu(Eviction):

    def __init__(self, core, dst, tokens, product):
        super().__init__(core)
        self.dst, self.tokens, self.product = dst, tokens, product
        self.rounded, self.kept = counter(core, "hidden_high"), counter(core, "hidden_low")
        self.relu = counter(core, "hidden_relu")

    def scalar(self, eng, n, turn, u, psum, done, count):
        nc, product = self.core.nc, self.product[:, :]
        eng.wait_ge(done, count)
        eng.wait_ge(self.kept.sem, self.kept0 + n)
        nc.scalar.activation(halves(product) if self.tokens > 512 else product, psum, ACT.Relu)\
            .then_inc(self.relu.sem, 1)
        eng.wait_ge(self.out.sem, self.out0 + n + 1)
        nc.scalar.activation(tile(self.dst.high, n), product, ACT.Copy).then_inc(self.rounded.sem, 1)

    def vector(self, eng, n, turn, u, psum, done, count):
        nc, product = self.core.nc, self.product[:, :]
        shaped = halves(product) if self.tokens > 512 else product
        eng.wait_ge(self.relu.sem, self.relu0 + n + 1)
        nc.vector.tensor_tensor(shaped, psum, shaped, ALU.mult).then_inc(self.out.sem, 1)
        eng.wait_ge(self.rounded.sem, self.rounded0 + n + 1)
        nc.vector.tensor_tensor(tile(self.dst.low, n), product, tile(self.dst.high, n).bitcast(F32), ALU.subtract)\
            .then_inc(self.kept.sem, 1)

    def begin(self, nt):
        super().begin(nt)
        self.rounded0, self.kept0, self.relu0 = self.rounded.base, self.kept.base, self.relu.base
        for s in (self.rounded, self.kept, self.relu):
            s.base += nt
        self.dst.ready = (self.kept.sem, self.kept.base)



def rms_stage(core, src, kt, tokens, scales, shifts=None, dst=None, residual=None, eps=EPS):
    nc = core.nc
    squared, summed = counter(core, "norm_squared"), counter(core, "norm_summed")
    inverted, rooted = counter(core, "norm_inverted"), counter(core, "norm_rooted")
    scaled, finished = counter(core, "norm_scaled"), counter(core, "norm_finished")
    steps = counter(core, "norm_vector_step")
    split = isinstance(dst, Split)
    high = counter(core, "norm_high")
    nb = 2 if tokens > 512 else 1
    width = tokens // nb
    with ExitStack() as scope:
        sq = core.sb(scope, "norm_sq", [P, 2, tokens])
        var = core.sb(scope, "norm_var", [P, tokens])
        inv = core.sb(scope, "norm_inv", [P, tokens])
        rstd = core.sb(scope, "norm_rstd", [P, tokens])
        tmp = core.sb(scope, "norm_tmp", [P, 2, tokens])
        total = core.psum[:, 0:nb, 0:width]

        def by_bank(ap):
            return ap.rearrange("p (a t) -> p a t", a=nb)

        with core.block() as block:
            @block.scalar
            def _(eng):
                for k in range(kt):
                    if k >= 2:
                        eng.wait_ge(summed.sem, summed.base + k - 1)
                    nc.scalar.activation(sq[:, k % 2, :], src[:, k, 0:tokens], ACT.Square).then_inc(squared.sem, 1)
                eng.wait_ge(inverted.sem, inverted.base + 1)
                nc.scalar.activation(rstd[:, :], inv[:, :], ACT.Sqrt).then_inc(rooted.sem, 1)
                if shifts is not None:
                    for k in range(kt):
                        eng.wait_ge(scaled.sem, scaled.base + k + 1)
                        for t0, t1, c in shifts:
                            last = nc.scalar.activation((dst.high if split else dst)[:, k, t0:t1], tmp[:, k % 2, t0:t1], ACT.Identity,
                                                        bias=col(c, k))
                        last.then_inc((high if split else finished).sem, 1)

            @block.tensor
            def _(pe):
                for k in range(kt):
                    pe.wait_ge(squared.sem, squared.base + k + 1)
                    for a in range(nb):
                        last = nc.tensor.matmul(total[:, a, :], core.ones[:, :], sq[:, k % 2, a * width:(a + 1) * width],
                                                start=k == 0, stop=k == kt - 1)
                    last.then_inc(summed.sem, 1)

            @block.vector
            def _(dve):
                chain = Chain(dve, steps, steps.base)
                dve.wait_ge(summed.sem, summed.base + kt)
                chain(nc.vector.tensor_scalar(by_bank(var[:, :]), total, 1.0 / (kt * P), eps, ALU.mult, ALU.add))
                nc.vector.reciprocal(inv[:, :], var[:, :]).then_inc(inverted.sem, 1)
                dve.wait_ge(rooted.sem, rooted.base + 1)

                def low(k):
                    dve.wait_ge(high.sem, high.base + k + 1)
                    for t0, t1, c in shifts:
                        last = nc.vector.scalar_tensor_tensor(dst.low[:, k, t0:t1], tmp[:, k % 2, t0:t1], col(c, k),
                                                              dst.high[:, k, t0:t1].bitcast(F32), ALU.add, ALU.subtract)
                    last.then_inc(finished.sem, 1)

                for k in range(kt):
                    if k >= 2 and (shifts is not None or residual is not None):
                        dve.wait_ge(finished.sem, finished.base + k - 1)
                    for t0, t1, c in scales:
                        o = dst[:, k, t0:t1] if shifts is None and residual is None else tmp[:, k % 2, t0:t1]
                        last = nc.vector.scalar_tensor_tensor(o, src[:, k, t0:t1], col(c, k), rstd[:, t0:t1],
                                                              ALU.mult, ALU.mult)
                    last.then_inc(scaled.sem, 1)
                    if split and k >= 1:
                        low(k - 1)
                if split:
                    low(kt - 1)

            if residual is not None:
                @block.gpsimd
                def _(pool):
                    for k in range(kt):
                        pool.wait_ge(scaled.sem, scaled.base + k + 1)
                        nc.gpsimd.tensor_tensor(residual[:, k, 0:tokens], residual[:, k, 0:tokens], tmp[:, k % 2, :],
                                                ALU.add).then_inc(finished.sem, 1)
                    pool.wait_ge(finished.sem, finished.base + kt)
    squared.base += kt
    summed.base += kt
    inverted.base += 1
    rooted.base += 1
    steps.base += 1
    scaled.base += kt
    if shifts is not None or residual is not None:
        finished.base += kt
    if split:
        high.base += kt



class Modulation:

    def __init__(self, core, scope, weights, ring, junk=None):
        self.core, self.weights, self.ring = core, weights, ring
        self.w = core.sb(scope, "mod_weights", [P, ring, D])
        self.junk = core.sb(scope, "mod_products", [P, D])[:, :] if junk is None else junk
        self.part = core.sb(scope, "mod_part", [P, 2, ring])
        self.landed = [counter(core, f"mod_landed_{s}") for s in range(ring)]
        self.used, self.steps = counter(core, "mod_tile_used"), counter(core, "mod_vector_step")
        self.used_base = self.used.base

    def load(self, sp, tile_, at, slot):
        sp.wait_ge(self.used.sem, self.used_base + at + 1 - self.ring)
        sp.dma_start(self.w[:, slot, :], self.weights[bass.ds(tile_, 1), :, :].rearrange("a p k -> p (a k)"))\
            .then_inc(self.landed[slot].sem, 16)

    def vector(self, dve, first, count, biases, vectors, mods):
        nc, ring, nv = self.core.nc, self.ring, len(vectors)
        per = (nv - 1) * ring + nv
        used, landed, steps = self.used, self.landed, self.steps
        with dve.Fori(0, count // ring) as blk:
            chain = Chain(dve, steps, steps.base + blk * per)
            for u in range(ring):
                dve.wait_ge(landed[u].sem, landed[u].base + 16 * (blk + 1))
                for v in range(nv):
                    ins = nc.vector.tensor_tensor_reduce(
                        out=self.junk, in0=self.w[:, u, :], in1=vectors[v], scale=1.0, scalar=0.0,
                        op0=ALU.mult, op1=ALU.add, accum_out=self.part[:, v, u:u + 1])
                    if v == nv - 1:
                        ins.then_inc(used.sem, 1)
                        dve.wait_ge(used.sem, used.base + blk * ring + u + 1)
                    else:
                        chain(ins)
            for v in range(nv):
                at = bass.ds(blk * ring + first, ring)
                chain(nc.vector.tensor_tensor(mods[v][:, at], self.part[:, v, :], biases[:, at], ALU.add))
            assert chain.steps == per
        for s in range(ring):
            landed[s].base += 16 * (count // ring)
        used.base += count
        steps.base += per * (count // ring)


def modulation(core, weights, first, count, biases, vectors, mods):
    ring = 4
    with ExitStack() as scope:
        m = Modulation(core, scope, weights, ring)
        with core.block() as block:
            @block.sync
            def _(sp):
                with sp.Fori(0, count // ring) as blk:
                    for u in range(ring):
                        m.load(sp, blk * ring + u + first, blk * ring + u, u)

            @block.vector
            def _(dve):
                m.vector(dve, first, count, biases, vectors, mods)



def pool_mixer(core, u, pool_weights, inv_count, scale_cols, dst):
    nc = core.nc
    pad = POOL_WINDOWS[-1] // 2
    x0, c0 = pad, pad + SEQ + pad
    total = c0 + CTX + pad
    groups = len(POOL_WINDOWS)
    landed, done, ready, out = (counter(core, "pool_weights_landed"), counter(core, "panel_done"),
                                counter(core, "pool_ready"), counter(core, "pool_out"))
    zeroed, steps = counter(core, "pool_zeroed"), counter(core, "pool_vector_step")
    n_steps = 0
    with ExitStack() as scope:
        w = core.sb(scope, "pool_w", [P, groups, P])
        padded = core.sb(scope, "pool_padded", [P, total])
        sums = core.sb(scope, "pool_sums", [P, 2, total])
        mean = core.sb(scope, "pool_mean", [P, T0])
        diff = core.sb(scope, "pool_diff", [P, groups, T0])
        with core.block() as block:
            @block.sync
            def _(sp):
                sp.dma_start(w[:, :, :], pool_weights.rearrange("g p k -> p g k")).then_inc(landed.sem, 16)

            @block.gpsimd
            def _(pool):
                nc.gpsimd.memset(padded[:, :], 0.0).then_inc(zeroed.sem, 1)

            @block.vector
            def _(dve):
                nonlocal n_steps
                chain = Chain(dve, steps, steps.base)
                dve.wait_ge(zeroed.sem, zeroed.base + 1)
                for g, window in enumerate(POOL_WINDOWS):
                    chain(nc.vector.tensor_copy(padded[:, x0:x0 + SEQ], u[:, g, 0:SEQ]))
                    chain(nc.vector.tensor_copy(padded[:, c0:c0 + CTX], u[:, g, SEQ:T0]))
                    have, src, slot = 1, padded[:, :], 0
                    while have < window:
                        n = total - 2 * have + 1
                        chain(nc.vector.tensor_tensor(sums[:, slot, 0:n], src[:, 0:n], src[:, have:have + n], ALU.add))
                        src, slot, have = sums[:, slot, :], 1 - slot, 2 * have
                    for t0, t1, at in ((0, SEQ, x0), (SEQ, T0, c0)):
                        lo = at - window // 2
                        chain(nc.vector.tensor_tensor(mean[:, t0:t1], src[:, lo:lo + t1 - t0], inv_count[:, g, t0:t1],
                                                      ALU.mult))
                    nc.vector.tensor_tensor(diff[:, g, :], mean[:, :], u[:, g, :], ALU.subtract).then_inc(ready.sem, 1)
                    dve.wait_ge(ready.sem, ready.base + g + 1)
                n_steps = chain.steps

            @block.tensor
            def _(pe):
                pe.wait_ge(landed.sem, landed.base + 16)
                for g in range(groups):
                    pe.wait_ge(ready.sem, ready.base + g + 1)
                    for a in range(2):
                        last = nc.tensor.matmul(core.psum[:, 2 * g + a, 0:T0 // 2], w[:, g, :],
                                                diff[:, g, a * T0 // 2:(a + 1) * T0 // 2], start=True, stop=True)
                    last.then_inc(done.sem, 1)

            @block.scalar
            def _(eng):
                for g in range(groups):
                    eng.wait_ge(done.sem, done.base + g + 1)
                    nc.scalar.activation(halves(dst[:, g, :]), core.psum[:, 2 * g:2 * g + 2, 0:T0 // 2], ACT.Identity,
                                         scale=col(scale_cols, g)).then_inc(out.sem, 1)
    landed.base += 16
    zeroed.base += 1
    ready.base += groups
    done.base += groups
    out.base += groups
    steps.base += n_steps



class Head:

    def __init__(self, q, queries, keys, values, out, scale, bias=None, causal=False, bias_load=None):
        self.q, self.queries, self.keys, self.values, self.out = q, queries, keys, values, out
        self.scale, self.bias, self.causal, self.bias_load = scale, bias, causal, bias_load
        self.tiles = queries // P
        self.total = sum(k.shape[-1] for k in keys)

    def seen(self, i):
        return (i + 1) * P if self.causal else self.total


def attention(core, heads, bias_tile=None, bias_mask=None):
    nc = core.nc
    ps = core.psum
    scored, biased, exped = counter(core, "att_scored"), counter(core, "att_biased"), counter(core, "att_exped")
    probs, turned, kept = counter(core, "att_probs"), counter(core, "att_turned"), counter(core, "att_kept")
    mixed, out = counter(core, "att_mixed"), counter(core, "att_out")
    steps, peaked = counter(core, "att_vector_step"), counter(core, "att_peaked")
    loaded = [counter(core, f"att_bias_landed_{s}") for s in range(2)]
    units = [(h, i) for h in range(len(heads)) for i in range(heads[h].tiles)]
    last_unit = {h: n for n, (h, i) in enumerate(units)}
    n_steps = 0
    widest = max(h.total for h in heads)
    with ExitStack() as scope:
        s = core.sb(scope, "att_scores", [P, 3, widest])
        pt = core.sb(scope, "att_turned_probs", [P, 2, widest // P, 512])
        peak = core.sb(scope, "att_peak", [P, 3])
        minus = core.sb(scope, "att_minus_peak", [P, 3])
        norm = core.sb(scope, "att_sum", [P, 3])
        recip = core.sb(scope, "att_recip", [P, 3])
        with core.block() as block:
            if bias_tile is not None:
                @block.sync
                def _(sp):
                    for h, head in enumerate(heads):
                        if h >= 2:
                            sp.wait_ge(biased.sem, biased.base + last_unit[h - 2] + 1)
                        sp.dma_start(bias_tile[:, h % 2, :], head.bias_load).then_inc(loaded[h % 2].sem, 16)

            @block.tensor
            def _(pe):
                def scores(n):
                    h, i = units[n]
                    head = heads[h]
                    if n >= 2:
                        pe.wait_ge(biased.sem, biased.base + n - 1)
                    at, seen = 0, head.seen(i)
                    for b, keys in enumerate(head.keys):
                        width = min(keys.shape[-1], seen - at)
                        if width <= 0:
                            break
                        last = nc.tensor.matmul(ps[:, 2 * (n % 2) + b, 0:width], head.q[:, i * P:(i + 1) * P],
                                                keys[:, 0:width], start=True, stop=True)
                        at += width
                    last.then_inc(scored.sem, 1)

                def transposes(n):
                    h, i = units[n]
                    seen = heads[h].seen(i) // P
                    pe.wait_ge(probs.sem, probs.base + n + 1)
                    if n >= 1:
                        pe.wait_ge(kept.sem, kept.base + n)
                    for kt in range(seen):
                        last = nc.tensor.transpose(ps[:, 4 + kt // 4, (kt % 4) * P:(kt % 4 + 1) * P],
                                                   s[:, n % 3, kt * P:(kt + 1) * P], core.ident[:, :])
                    last.then_inc(turned.sem, 1)

                def values(h, n):
                    head = heads[h]
                    pe.wait_ge(kept.sem, kept.base + n + 1)
                    if h >= 2:
                        pe.wait_ge(out.sem, out.base + h - 1)
                    o = head.out.base_row
                    for kt in range(head.total // P):
                        q0 = kt * P if head.causal else 0
                        last = nc.tensor.matmul(ps[o:o + HEAD, 6 + h % 2, q0:head.queries], head.values(kt),
                                                pt[:, h % 2, kt, q0:head.queries], start=kt == 0,
                                                stop=kt == head.total // P - 1)
                    last.then_inc(mixed.sem, 1)

                for n in range(len(units) + 2):
                    if n < len(units):
                        scores(n)
                    if n >= 2:
                        transposes(n - 2)
                        h, i = units[n - 2]
                        if i == heads[h].tiles - 1:
                            values(h, n - 2)

            @block.vector
            def _(dve):
                nonlocal n_steps
                chain = Chain(dve, steps, steps.base)

                def shift(n):
                    h, i = units[n]
                    head = heads[h]
                    seen = head.seen(i)
                    if bias_tile is not None and i == 0:
                        dve.wait_ge(loaded[h % 2].sem, loaded[h % 2].base + 16 * (h // 2 + 1))
                        b = bias_tile[:, h % 2, :].rearrange("p (r c) -> p r c", c=GRID_W)
                        chain(nc.vector.tensor_tensor(b, b, bias_mask, ALU.add))
                    dve.wait_ge(scored.sem, scored.base + n + 1)
                    row = s[:, n % 3, :]
                    if n >= 3:
                        dve.wait_ge(turned.sem, turned.base + n - 2)
                    at, banks, bias = 0, 2 * (n % 2), head.bias(i) if head.bias else None
                    if bias is not None:
                        last = nc.vector.scalar_tensor_tensor(row[:, 0:bias.shape[-1]], ps[:, banks, 0:bias.shape[-1]],
                                                              head.scale, bias, ALU.mult, ALU.add)
                        at, banks = bias.shape[-1], banks + 1
                    if at < seen:
                        if at:
                            chain(last)
                        last = nc.vector.tensor_scalar(row[:, at:seen], ps[:, banks, 0:seen - at], head.scale, None,
                                                       ALU.mult)
                    last.then_inc(biased.sem, 1)
                    dve.wait_ge(biased.sem, biased.base + n + 1)
                    chain(nc.vector.reduce_max(peak[:, n % 3:n % 3 + 1], row[:, 0:seen], AX.X))
                    nc.vector.tensor_scalar(minus[:, n % 3:n % 3 + 1], peak[:, n % 3:n % 3 + 1], -1.0, None,
                                            ALU.mult).then_inc(peaked.sem, 1)

                def normalise(n):
                    h, i = units[n]
                    seen = heads[h].seen(i)
                    dve.wait_ge(exped.sem, exped.base + n + 1)
                    c = slice(n % 3, n % 3 + 1)
                    chain(nc.vector.reciprocal(recip[:, c], norm[:, c]))
                    nc.vector.tensor_scalar(s[:, n % 3, 0:seen], s[:, n % 3, 0:seen], recip[:, c], None, ALU.mult)\
                        .then_inc(probs.sem, 1)

                for n in range(len(units) + 1):
                    if n < len(units):
                        shift(n)
                    if n >= 1:
                        normalise(n - 1)
                n_steps = chain.steps

            @block.scalar
            def _(eng):
                def exps(n):
                    h, i = units[n]
                    seen = heads[h].seen(i)
                    c = slice(n % 3, n % 3 + 1)
                    eng.wait_ge(peaked.sem, peaked.base + n + 1)
                    nc.scalar.activation(s[:, n % 3, 0:seen], s[:, n % 3, 0:seen], ACT.Exp, bias=minus[:, c],
                                         accum_out=norm[:, c]).then_inc(exped.sem, 1)

                def keep(n):
                    h, i = units[n]
                    seen = heads[h].seen(i) // P
                    eng.wait_ge(turned.sem, turned.base + n + 1)
                    if i == 0 and h >= 2:
                        eng.wait_ge(mixed.sem, mixed.base + h - 1)
                    for b in range(0, seen, 4):
                        m = min(4, seen - b)
                        last = nc.scalar.activation(
                            pt[:, h % 2, b:b + m, i * P:(i + 1) * P],
                            ps[:, 4 + b // 4, 0:m * P].rearrange("p (k q) -> p k q", q=P), ACT.Copy)
                    last.then_inc(kept.sem, 1)

                def finish(h):
                    head = heads[h]
                    o = head.out.base_row
                    eng.wait_ge(mixed.sem, mixed.base + h + 1)
                    nc.scalar.activation(head.out.ap, ps[o:o + HEAD, 6 + h % 2, 0:head.queries], ACT.Copy)\
                        .then_inc(out.sem, 1)

                for n in range(len(units) + 2):
                    if n < len(units):
                        exps(n)
                    if n >= 2:
                        keep(n - 2)
                        h, i = units[n - 2]
                        if i == heads[h].tiles - 1:
                            finish(h)
    nu, nh = len(units), len(heads)
    for sig in (scored, biased, peaked, exped, probs, turned, kept):
        sig.base += nu
    mixed.base += nh
    out.base += nh
    steps.base += n_steps
    if bias_tile is not None:
        for slot in range(2):
            loaded[slot].base += 16 * len(range(slot, nh, 2))


class Rows:

    def __init__(self, ap, base_row):
        self.ap, self.base_row = ap, base_row



def head_norm(core, x, rows, tiles, mean_of, gain, rotate=None, cos=None, sin=None):
    nc, ps = core.nc, core.psum
    squared, summed = counter(core, "norm_squared"), counter(core, "norm_summed")
    inverted, rooted = counter(core, "norm_inverted"), counter(core, "norm_rooted")
    scaled, turned, finished = counter(core, "norm_scaled"), counter(core, "norm_turned"), counter(core, "norm_finished")
    steps = counter(core, "norm_vector_step")
    per = 1 + (2 if rotate is not None else 0)
    with ExitStack() as scope:
        sq = core.sb(scope, "head_sq", [P, 2, SEQ])
        var = core.sb(scope, "head_var", [P, 2, SEQ])
        rstd = core.sb(scope, "head_rstd", [P, 2, SEQ])
        part = core.sb(scope, "head_part", [P, SEQ])
        with core.block() as block:
            @block.scalar
            def _(eng):
                def square(n):
                    if n >= 2:
                        eng.wait_ge(summed.sem, summed.base + n - 1)
                    nc.scalar.activation(sq[0:rows, n % 2, :], x[0:rows, n, :], ACT.Square).then_inc(squared.sem, 1)

                square(0)
                for n in range(tiles):
                    if n + 1 < tiles:
                        square(n + 1)
                    eng.wait_ge(inverted.sem, inverted.base + n + 1)
                    nc.scalar.activation(rstd[0:rows, n % 2, :], var[0:rows, n % 2, :], ACT.Sqrt).then_inc(rooted.sem, 1)

            @block.tensor
            def _(pe):
                def mean(n):
                    pe.wait_ge(squared.sem, squared.base + n + 1)
                    if n >= 2:
                        pe.wait_ge(inverted.sem, inverted.base + n - 1)
                    nc.tensor.matmul(ps[0:rows, n % 2, :], mean_of, sq[0:rows, n % 2, :], start=True, stop=True)\
                        .then_inc(summed.sem, 1)

                mean(0)
                for n in range(tiles):
                    if n + 1 < tiles:
                        mean(n + 1)
                    if rotate is not None:
                        pe.wait_ge(scaled.sem, scaled.base + n + 1)
                        if n >= 2:
                            pe.wait_ge(finished.sem, finished.base + n - 1)
                        nc.tensor.matmul(ps[0:rows, 2 + n % 2, :], rotate, x[0:rows, n, :], start=True, stop=True)\
                            .then_inc(turned.sem, 1)

            @block.vector
            def _(dve):
                chain = Chain(dve, steps, steps.base)
                for n in range(tiles):
                    dve.wait_ge(summed.sem, summed.base + n + 1)
                    v = var[0:rows, n % 2, :]
                    chain(nc.vector.tensor_scalar(v, ps[0:rows, n % 2, :], EPS, None, ALU.add))
                    nc.vector.reciprocal(v, v).then_inc(inverted.sem, 1)
                    dve.wait_ge(rooted.sem, rooted.base + n + 1)
                    nc.vector.scalar_tensor_tensor(x[0:rows, n, :], x[0:rows, n, :], gain, rstd[0:rows, n % 2, :],
                                                   ALU.mult, ALU.mult).then_inc(scaled.sem, 1)
                    if rotate is not None:
                        dve.wait_ge(turned.sem, turned.base + n + 1)
                        chain(nc.vector.tensor_tensor(part[0:rows, :], ps[0:rows, 2 + n % 2, :], sin, ALU.mult))
                        chain(nc.vector.tensor_tensor(x[0:rows, n, :], x[0:rows, n, :], cos, ALU.mult))
                        nc.vector.tensor_tensor(x[0:rows, n, :], x[0:rows, n, :], part[0:rows, :], ALU.add)\
                            .then_inc(finished.sem, 1)
                        dve.wait_ge(finished.sem, finished.base + n + 1)
    for sig in (squared, summed, inverted, rooted, scaled):
        sig.base += tiles
    if rotate is not None:
        turned.base += tiles
        finished.base += tiles
    steps.base += per * tiles


def rotation_tables(core, positions, freqs, tables):
    nc = core.nc
    landed, reduced, waved = counter(core, "positions_landed"), counter(core, "angle_reduced"), counter(core, "angle_waved")
    steps = counter(core, "rope_vector_step")
    c1 = 6.28125
    c2 = float(np.float32(np.floor((2 * np.pi - c1) * 2.0 ** 20) / 2.0 ** 20))
    c3 = float(2 * np.pi - c1 - c2)
    magic = 1.5 * 2.0 ** 23
    pi = float(np.nextafter(np.float32(np.pi), np.float32(0)))
    n_steps = 0
    with ExitStack() as scope:
        raw = core.sb(scope, "rope_positions", [P, SEQ], I32)
        pos = core.sb(scope, "rope_pos", [P, SEQ])
        ang = core.sb(scope, "rope_angle", [P, SEQ])
        turns = core.sb(scope, "rope_turns", [P, SEQ])
        red = core.sb(scope, "rope_reduced", [P, 4, SEQ])
        with core.block() as block:
            @block.sync
            def _(sp):
                sp.dma_start(raw[:, :], positions.to_broadcast([P, SEQ])).then_inc(landed.sem, 16)

            @block.vector
            def _(dve):
                nonlocal n_steps
                chain = Chain(dve, steps, steps.base)
                dve.wait_ge(landed.sem, landed.base + 16)
                chain(nc.vector.tensor_copy(pos[:, :], raw[:, :]))
                for n in range(len(tables)):
                    for j, quarter in enumerate((0.25, 0.0)):
                        r = red[:, 2 * n + j, :]
                        chain(nc.vector.tensor_scalar(ang[:, :], pos[:, :], col(freqs, n), None, ALU.mult))
                        chain(nc.vector.tensor_scalar(turns[:, :], ang[:, :], float(1 / (2 * np.pi)), quarter,
                                                      ALU.mult, ALU.add))
                        chain(nc.vector.tensor_scalar(turns[:, :], turns[:, :], magic, None, ALU.add))
                        chain(nc.vector.tensor_scalar(turns[:, :], turns[:, :], -magic, None, ALU.add))
                        src = ang[:, :]
                        for c in (c1, c2, c3):
                            chain(nc.vector.scalar_tensor_tensor(r, turns[:, :], -c, src, ALU.mult, ALU.add))
                            src = r
                        chain(nc.vector.tensor_scalar(r, r, quarter * 2 * float(np.pi), pi, ALU.add, ALU.min))
                        nc.vector.tensor_scalar(r, r, -pi, None, ALU.max).then_inc(reduced.sem, 1)
                n_steps = chain.steps

            @block.scalar
            def _(eng):
                for n, pair in enumerate(tables):
                    for j in range(2):
                        eng.wait_ge(reduced.sem, reduced.base + 2 * n + j + 1)
                        nc.scalar.activation(pair[j], red[:, 2 * n + j, :], ACT.Sin).then_inc(waved.sem, 1)
    landed.base += 16
    reduced.base += 2 * len(tables)
    waved.base += 2 * len(tables)
    steps.base += n_steps



class ConvolvedGate(Eviction):
    RING = 4

    def __init__(self, core, scope, taps, bias, dst):
        super().__init__(core)
        self.taps, self.bias, self.dst = taps, bias, dst
        self.y = core.sb(scope, "conv_out", [P, self.RING, SEQ])
        self.gate = core.sb(scope, "gate_out", [P, 2, SEQ])
        self.first, self.conv, self.gated = (counter(core, "panel_first_evict"), counter(core, "conv_done"),
                                             counter(core, "gate_done"))
        self.multiplied, self.rounded = counter(core, "gate_multiplied"), counter(core, "gate_high")
        self.steps = counter(core, "gemm_vector_step")

    def begin(self, nt):
        super().begin(nt)
        self.first0, self.conv0, self.gated0 = self.first.base, self.conv.base, self.gated.base
        self.multiplied0, self.rounded0, self.steps0 = self.multiplied.base, self.rounded.base, self.steps.base
        self.first.base += nt
        for s in (self.conv, self.gated, self.multiplied, self.rounded):
            s.base += nt // 2
        self.steps.base += 6 * (nt // self.RING)

    def scalar(self, eng, n, turn, u, psum, done, count):
        nc, y, pair = self.core.nc, self.y, turn * 2 + u // 2
        eng.wait_ge(done, count)
        eng.wait_ge(self.gated.sem, self.gated0 + pair - 1)
        nc.scalar.activation(y[:, u, :], psum, ACT.Identity, bias=col(self.bias, n),
                             scale=col(self.taps[:, 2, :], n)).then_inc(self.first.sem, 1)
        if u % 2 == 1:
            gate = self.gate[:, u // 2, :]
            eng.wait_ge(self.out.sem, self.out0 + n)
            nc.scalar.activation(gate, y[:, u - 1, :], ACT.Sigmoid).then_inc(self.conv.sem, 1)
            eng.wait_ge(self.multiplied.sem, self.multiplied0 + pair + 1)
            nc.scalar.activation(tile(self.dst.high, pair), gate, ACT.Copy).then_inc(self.rounded.sem, 1)

    def vector(self, eng, n, turn, u, psum, done, count):
        nc, y, pair = self.core.nc, self.y, turn * 2 + u // 2
        chain = Chain(eng, self.steps, self.steps0 + turn * 6 + u // 2 * 3 + u % 2)
        eng.wait_ge(self.first.sem, self.first0 + n + 1)
        chain(nc.vector.scalar_tensor_tensor(y[:, u, 1:SEQ], psum[:, 0:SEQ - 1], col(self.taps[:, 1, :], n),
                                             y[:, u, 1:SEQ], ALU.mult, ALU.add))
        nc.vector.scalar_tensor_tensor(y[:, u, 2:SEQ], psum[:, 0:SEQ - 2], col(self.taps[:, 0, :], n),
                                       y[:, u, 2:SEQ], ALU.mult, ALU.add).then_inc(self.out.sem, 1)
        if u % 2 == 1:
            gate = self.gate[:, u // 2, :]
            eng.wait_ge(self.out.sem, self.out0 + n + 1)
            eng.wait_ge(self.conv.sem, self.conv0 + pair + 1)
            chain(nc.vector.tensor_tensor(gate, gate, y[:, u - 1, :], ALU.mult))
            nc.vector.tensor_tensor(gate, gate, y[:, u, :], ALU.mult).then_inc(self.multiplied.sem, 1)
            eng.wait_ge(self.rounded.sem, self.rounded0 + pair + 1)
            nc.vector.tensor_tensor(tile(self.dst.low, pair), gate, tile(self.dst.high, pair).bitcast(F32),
                                    ALU.subtract).then_inc(self.gated.sem, 1)



def neighbour_difference(core, h, segments, dst, then):
    nc = core.nc
    steps = counter(core, "mix_vector_step")
    per = 2
    with ExitStack() as scope:
        with core.block() as block:
            @block.vector
            def _(dve):
                chain = Chain(dve, steps, steps.base)
                for k in range(DT):
                    for t0, t1 in segments:
                        nc.vector.tensor_tensor(dst[:, k, t0 + 1:t1 - 1], h[:, k, t0:t1 - 2], h[:, k, t0 + 2:t1], ALU.add)
                        nc.vector.tensor_copy(dst[:, k, t0:t0 + 1], h[:, k, t0 + 1:t0 + 2])
                        last = nc.vector.tensor_copy(dst[:, k, t1 - 1:t1], h[:, k, t1 - 2:t1 - 1])
                    chain(last)
                    chain(nc.vector.scalar_tensor_tensor(dst[:, k, :], dst[:, k, :], 0.5, h[:, k, :],
                                                         ALU.mult, ALU.subtract))
                then(dve)
    steps.base += per * DT


def token_mix(core, dve, h, diff, mu, dst, tokens=T0):
    mixed = counter(core, "mix_done")
    for k in range(DT):
        core.nc.vector.scalar_tensor_tensor(dst[:, k, 0:tokens], diff[:, k, 0:tokens], col(mu, k), h[:, k, 0:tokens],
                                            ALU.mult, ALU.add).then_inc(mixed.sem, 1)
    mixed.base += DT


def wkv(core, lora_w, lora_a, up_panels, k_dram, v_dram, r_dram, g_dram, par, masks, dst):
    nc, ps = core.nc, core.psum
    chunks = T0 // CHUNK
    tiles = T0 // P
    xt = SEQ // P
    batches = tiles // 2

    def sig(name):
        return counter(core, name)

    loaded, lora, acted = sig("pair_loaded"), sig("lora_done"), sig("lora_activated")
    ps_kk, ps_inv, ps_root = sig("key_squared"), sig("key_inverted"), sig("key_rooted")
    ps_sum, normed = sig("key_summed"), sig("key_normed")
    expo, powers = sig("decay_exponent"), sig("decay_powers")
    tilde = sig("tilde_ready")
    turned, tok = sig("tilde_turned"), sig("token_major_kept")
    product = [sig(f"triangle_product_{h}") for h in range(2)]
    kept = {"V": [sig(f"triangle_kept_{h}") for h in range(2)], "S": [sig(f"factor_kept_{h}") for h in range(2)]}
    masked = [sig(f"levels_masked_{h}") for h in range(2)]
    u_done, u_kept, s_done, s_kept = sig("u_product"), sig("u_kept"), sig("state_product"), sig("state_kept")
    y_done, y_kept, zeroed = sig("y_state_product"), sig("y_state_kept"), sig("state_zeroed")
    intra, summed = sig("y_intra_product"), sig("y_summed")
    mean, centred, csq, var = sig("gn_mean"), sig("gn_centred"), sig("gn_squared"), sig("gn_var")
    ginv, groot, bonus_in, bonus = sig("gn_inverted"), sig("gn_rooted"), sig("bonus_terms"), sig("bonus_product")
    pair_done, steps = sig("pair_done"), sig("wkv_vector_step")

    def exchanges(i):
        out = [("gram", "V"), ("turn", "S")] + ([("read", "V")] if i else [])
        for n in LEVELS:
            out += [(f"z{n}", "S"), (f"w{n}", "V")] + ([(f"t{n}", "S")] if n != LEVELS[-1] else [])
        return out + [("kx", "S"), ("mkv", "V"), ("ux", "S")]

    def keeps(who, i, e=0):
        return sum(k == who for b in range(i) for _, k in exchanges(b)) + sum(k == who for _, k in exchanges(i)[:e])

    product_at = [sum(len(exchanges(b)) for b in range(i)) for i in range(batches + 1)]
    total_keeps = {who: sum(k == who for b in range(batches) for _, k in exchanges(b)) for who in "VS"}
    tile_at = [list(range(xt, tiles)) + list(range(xt)), list(range(tiles - 1, xt - 1, -1)) + list(range(xt - 1, -1, -1))]
    chunk_at = [[2 * t + (o if d == 0 else 1 - o) for t in tile_at[d] for o in range(2)] for d in range(2)]
    per_batch = chunks // batches
    first_x = CTX // CHUNK
    VSTEPS = 55

    def woven(i):
        if i == 0:
            return {}
        at = {}
        for k in range(per_batch):
            at[4 * k + 1] = ("u", (i - 1) * per_batch + k)
            at[4 * k + 3] = ("s", (i - 1) * per_batch + k)
        return at

    with ExitStack() as scope:
        def sb(name, shape):
            return core.sb(scope, name, shape)

        ups = sb("wkv_ups", [P, 2 * P])
        K, V = sb("wkv_k", [P, T0]), sb("wkv_v", [P, T0])
        R, G = sb("wkv_r", [P, SEQ]), sb("wkv_g", [P, SEQ])
        LW, A = sb("wkv_logw", [P, 2, T0]), sb("wkv_a", [P, 2, T0])
        KK, SQ, VAR = sb("wkv_kk", [P, T0]), sb("wkv_sq", [P, T0]), sb("wkv_var", [P, T0])
        INC, EXC = sb("wkv_inc", [P, 2, T0]), sb("wkv_exc", [P, 2, T0])
        PINC, PINV = sb("wkv_pinc", [P, 2, SEQ]), sb("wkv_pinv", [P, 2, T0])
        KD = sb("wkv_kd", [P, 2, T0])
        KSUM = sb("wkv_ksum", [P, SEQ])
        PC = sb("wkv_chunk_decay", [P, 2, chunks])
        TOK = sb("wkv_tok", [P, 7, T0])
        KX = INC
        UX, U = (t[:, :, :].rearrange("p d (n c) -> p d n c", c=P) for t in (LW, PINV))
        GA, GK = sb("wkv_ga", [P, 2, xt, 2, P]), sb("wkv_gk", [P, 2, xt, 2, P])
        S, SP = sb("wkv_s", [P, 2, 2, P]), sb("wkv_sp", [P, 2, P])
        YS = sb("wkv_ys", [P, 2, SEQ])
        MT, MK = sb("wkv_mt", [P, 2, 512]), sb("wkv_mk", [P, 2, 512])
        X, XT, Z = sb("wkv_x", [P, 2, 512]), sb("wkv_xt", [P, 2, 512]), sb("wkv_z", [P, 2, 512])
        LT = sb("wkv_level", [P, 2, 2, 512])
        MKV = sb("wkv_mkv", [P, 2, 4 * HEAD])
        BON = sb("wkv_bonus", [P, SEQ])

        def group(j, d):
            return slice((2 * j + d) * P, (2 * j + d + 1) * P)

        def over_tiles(ap):
            return ap.rearrange("p (j c) -> p j c", j=2)

        def mask(n):
            return masks[n].unsqueeze(1).to_broadcast([P, 2, 2 * P])

        with core.block() as block:
            @block.sync
            def _(sp):
                with sp.Fori(0, DT) as ft:
                    sp.wait_ge(pair_done.sem, pair_done.base + ft)
                    for dst_, src in ((ups, up_panels), (K, k_dram), (V, v_dram), (R, r_dram), (G, g_dram)):
                        sp.dma_start(dst_[:, :], src[bass.ds(ft, 1), :, :].rearrange("a p t -> p (a t)"))\
                            .then_inc(loaded.sem, 16)

            @block.tensor
            def _(pe):
                with pe.Fori(0, DT) as ft:
                    pe.wait_ge(loaded.sem, loaded.base + 80 * (ft + 1))
                    pe.wait_ge(pair_done.sem, pair_done.base + ft)
                    for which, src in ((0, lora_w), (1, lora_a)):
                        for d in range(2):
                            rows = slice(d * HEAD, (d + 1) * HEAD)
                            for a in range(2):
                                last = nc.tensor.matmul(ps[:, 4 * which + 2 * d + a, 0:T0 // 2],
                                                        ups[rows, which * P:(which + 1) * P],
                                                        src[rows, a * T0 // 2:(a + 1) * T0 // 2], start=True, stop=True)
                            last.then_inc(lora.sem, 1)
                    pe.wait_ge(ps_kk.sem, ps_kk.base + ft + 1)
                    pe.wait_ge(acted.sem, acted.base + 4 * ft + 4)
                    for a in range(2):
                        last = nc.tensor.matmul(ps[:, a, 0:T0 // 2], core.head_sum[:, :],
                                                SQ[:, a * T0 // 2:(a + 1) * T0 // 2], start=True, stop=True)
                    last.then_inc(ps_sum.sem, 1)
                    for n, src in enumerate((EXC[:, 0, :], EXC[:, 1, :], A[:, 0, :], A[:, 1, :], KD[:, 0, :],
                                             KD[:, 1, :], V[:, :])):
                        if n == 0:
                            pe.wait_ge(tilde.sem, tilde.base + ft + 1)
                        if n >= 4:
                            pe.wait_ge(tok.sem, tok.base + 7 * ft + n - 3)
                        for t in range(tiles):
                            last = nc.tensor.transpose(ps[:, 2 * (n % 4) + t // 3, (t % 3) * P:(t % 3 + 1) * P],
                                                       src[:, t * P:(t + 1) * P], core.ident[:, :])
                        last.then_inc(turned.sem, 1)
                    pe.wait_ge(tok.sem, tok.base + 7 * ft + 7)
                    pe.wait_ge(zeroed.sem, zeroed.base + ft + 1)

                    def products(name, h, i):
                        rows = slice(h * HEAD, (h + 1) * HEAD)
                        ba, bb = 2 * h, 2 * h + 1
                        for j in range(2):
                            for d in range(2):
                                g = group(j, d)
                                t = tile_at[d][2 * i + j]
                                at = slice(t * P, (t + 1) * P)
                                own = slice(t * P + h * HEAD, t * P + (h + 1) * HEAD)
                                v = slice((2 * j + d) * HEAD, (2 * j + d + 1) * HEAD)
                                if name == "gram":
                                    nc.tensor.matmul(ps[:, ba, g], A[rows, d, at], EXC[rows, d, at], start=True, stop=True)
                                    last = nc.tensor.matmul(ps[:, bb, g], KD[rows, d, at], EXC[rows, d, at],
                                                            start=True, stop=True)
                                elif name == "read":
                                    nc.tensor.matmul(ps[:, ba, g], A[rows, d, at], PINC[rows, d, at], start=True, stop=True)
                                    last = nc.tensor.matmul(ps[:, bb, g], KD[rows, d, at], PINC[rows, d, at],
                                                            start=True, stop=True)
                                elif name == "turn":
                                    last = nc.tensor.transpose(ps[:, ba, g], XT[:, h, g], core.ident[:, :])
                                elif name[0] == "z":
                                    last = nc.tensor.matmul(ps[:, ba, g], LT[:, h, LEVELS.index(int(name[1:])) % 2, g],
                                                            X[:, h, g], start=True, stop=True)
                                elif name == f"w{LEVELS[-1]}":
                                    last = nc.tensor.matmul(ps[:, bb, g], Z[:, h, g], XT[:, h, g], start=True, stop=True)
                                elif name[0] == "w":
                                    last = nc.tensor.matmul(ps[:, bb, g], XT[:, h, g], Z[:, h, g], start=True, stop=True)
                                elif name[0] == "t":
                                    last = nc.tensor.transpose(ps[:, ba, g], X[:, h, g], core.ident[:, :])
                                elif name == "kx":
                                    last = nc.tensor.matmul(ps[rows, ba, g], TOK[:, d, own], XT[:, h, g],
                                                            start=True, stop=True)
                                elif name == "mkv":
                                    last = nc.tensor.matmul(ps[:, bb, v], MK[:, h, g], TOK[:, 6, own], start=True, stop=True)
                                else:
                                    last = nc.tensor.matmul(ps[:, ba, v], XT[:, h, g], MKV[:, h, v], start=True, stop=True)
                        last.then_inc(product[h].sem, 1)

                    def step_u(c):
                        if c % per_batch == 0:
                            for h in range(2):
                                e = [n for n, _ in exchanges(c // per_batch)].index("kx")
                                pe.wait_ge(kept["S"][h].sem, kept["S"][h].base + total_keeps["S"] * ft
                                           + keeps("S", c // per_batch, e + 1))
                        if c:
                            pe.wait_ge(s_kept.sem, s_kept.base + (chunks - 1) * ft + c)
                        for d in range(2):
                            last = nc.tensor.matmul(ps[:, 4, d * P:(d + 1) * P], KX[:, d, c // 2 * P:(c // 2 + 1) * P],
                                                    S[:, c % 2, d, :], start=True, stop=True)
                        last.then_inc(u_done.sem, 1)
                        n = c - first_x
                        if n >= 1:
                            pe.wait_ge(y_kept.sem, y_kept.base + (chunks - first_x) * ft + n)
                        if n >= 0:
                            for d in range(2):
                                ch = chunk_at[d][c]
                                last = nc.tensor.matmul(ps[:, 7, d * CHUNK:(d + 1) * CHUNK], S[:, c % 2, d, :],
                                                        PINC[:, d, ch * CHUNK:(ch + 1) * CHUNK], start=True, stop=True)
                            last.then_inc(y_done.sem, 1)

                    def step_s(c):
                        pe.wait_ge(u_kept.sem, u_kept.base + chunks * ft + c + 1)
                        for d in range(2):
                            ch = chunk_at[d][c]
                            rows = slice(ch % 2 * HEAD, ch % 2 * HEAD + HEAD)
                            f = slice(ch // 2 * P, ch // 2 * P + P)
                            nc.tensor.matmul(ps[:, 5 + d, 0:P], TOK[rows, 2 + d, f], U[rows, d, c // 2, :],
                                             start=True, stop=False)
                            last = nc.tensor.matmul(ps[:, 5 + d, 0:P], TOK[rows, 4 + d, f], TOK[rows, 6, f],
                                                    start=False, stop=True)
                        last.then_inc(s_done.sem, 1)

                    for i in range(batches):
                        weave = woven(i)
                        for e, (name, keeper) in enumerate(exchanges(i)):
                            for h in range(2):
                                for who in "VS":
                                    n = keeps(who, i, e)
                                    if e == 0 or exchanges(i)[e - 1][1] == who or name in ("mkv", "ux"):
                                        pe.wait_ge(kept[who][h].sem, kept[who][h].base + total_keeps[who] * ft + n)
                                if name[0] == "z":
                                    pe.wait_ge(masked[h].sem, masked[h].base + len(LEVELS) * (batches * ft + i)
                                               + LEVELS.index(int(name[1:])) + 1)
                                products(name, h, i)
                            if e in weave:
                                part, c = weave[e]
                                step_u(c) if part == "u" else step_s(c)
                    for c in range(chunks - per_batch, chunks):
                        step_u(c)
                        if c < chunks - 1:
                            step_s(c)
                    pe.wait_ge(u_kept.sem, u_kept.base + chunks * (ft + 1))
                    for t in range(xt):
                        for h in range(2):
                            out = slice(h * HEAD, (h + 1) * HEAD)
                            for d in range(2):
                                n = tile_at[d].index(t)
                                nc.tensor.matmul(ps[out, 0, t * P:(t + 1) * P], U[:, d, n, out],
                                                 GA[:, h, n - CTX // P, d, :], start=d == 0, stop=False)
                                last = nc.tensor.matmul(ps[out, 0, t * P:(t + 1) * P],
                                                        TOK[:, 6, t * P + h * HEAD:t * P + (h + 1) * HEAD],
                                                        GK[:, h, n - CTX // P, d, :], start=False, stop=d == 1)
                    last.then_inc(intra.sem, 1)
                    pe.wait_ge(summed.sem, summed.base + ft + 1)
                    nc.tensor.matmul(ps[:, 1, :], core.head_mean[:, :], YS[:, 0, :], start=True, stop=True)\
                        .then_inc(mean.sem, 1)
                    pe.wait_ge(csq.sem, csq.base + ft + 1)
                    nc.tensor.matmul(ps[:, 2, :], core.head_mean[:, :], SQ[:, 0:SEQ], start=True, stop=True)\
                        .then_inc(var.sem, 1)
                    pe.wait_ge(bonus_in.sem, bonus_in.base + ft + 1)
                    nc.tensor.matmul(ps[:, 3, :], core.head_sum[:, :], BON[:, :], start=True, stop=True)\
                        .then_inc(bonus.sem, 1)

            @block.scalar
            def _(eng):
                with eng.Fori(0, DT) as ft:
                    eng.wait_ge(pair_done.sem, pair_done.base + ft)
                    for which, dst_, bias in ((0, LW, par["w0"]), (1, A, par["a0"])):
                        for d in range(2):
                            eng.wait_ge(lora.sem, lora.base + 4 * ft + 2 * which + d + 1)
                            b = 4 * which + 2 * d
                            nc.scalar.activation(halves(dst_[:, d, :]), ps[:, b:b + 2, 0:T0 // 2], ACT.Sigmoid,
                                                 bias=col(bias[d], ft)).then_inc(acted.sem, 1)
                    eng.wait_ge(normed.sem, normed.base + 2 * ft + 1)
                    nc.scalar.activation(SQ[:, :], KK[:, :], ACT.Square).then_inc(ps_kk.sem, 1)
                    eng.wait_ge(ps_inv.sem, ps_inv.base + ft + 1)
                    nc.scalar.activation(VAR[:, :], VAR[:, :], ACT.Sqrt).then_inc(ps_root.sem, 1)
                    for d in range(2):
                        eng.wait_ge(expo.sem, expo.base + 2 * ft + d + 1)
                        nc.scalar.activation(EXC[:, d, :], EXC[:, d, :], ACT.Exp)
                        nc.scalar.activation(PINC[:, d, :], INC[:, d, 0:SEQ], ACT.Exp)
                        end = CHUNK - 1 if d == 0 else 0
                        nc.scalar.activation(PC[:, d, :], INC[:, d, end::CHUNK], ACT.Exp)
                        nc.scalar.activation(PINV[:, d, :], INC[:, d, :], ACT.Exp, scale=-1.0).then_inc(powers.sem, 1)
                    for n in range(7):
                        eng.wait_ge(turned.sem, turned.base + 7 * ft + n + 1)
                        b = 2 * (n % 4)
                        nc.scalar.activation(halves(TOK[:, n, :]), ps[:, b:b + 2, 0:T0 // 2], ACT.Copy)\
                            .then_inc(tok.sem, 1)

                    def keep(name, h, i):
                        ba = 2 * h
                        if name == "kx":
                            rows = slice(h * HEAD, (h + 1) * HEAD)
                            for d in range(2):
                                last = nc.scalar.activation(
                                    over_tiles(KX[rows, d, 2 * i * P:2 * (i + 1) * P]),
                                    over_tiles(ps[rows, ba, :])[:, :, d * P:(d + 1) * P], ACT.Copy, scale=-1.0)
                        elif name == "ux":
                            own = slice(h * HEAD, (h + 1) * HEAD)
                            for d in range(2):
                                last = nc.scalar.activation(
                                    UX[:, d, 2 * i:2 * i + 2, own],
                                    over_tiles(ps[:, ba, 0:4 * HEAD])[:, :, d * HEAD:(d + 1) * HEAD], ACT.Copy, scale=-1.0)
                        else:
                            dst_ = {"z": Z, "t": XT}[name[0]] if name != "turn" else X
                            last = nc.scalar.activation(dst_[:, h, :], ps[:, ba, :], ACT.Copy)
                        last.then_inc(kept["S"][h].sem, 1)

                    def keep_y(c):
                        eng.wait_ge(y_done.sem, y_done.base + (chunks - first_x) * ft + c - first_x + 1)
                        for d in range(2):
                            ch = chunk_at[d][c]
                            last = nc.scalar.activation(YS[:, d, ch * CHUNK:(ch + 1) * CHUNK],
                                                        ps[:, 7, d * CHUNK:(d + 1) * CHUNK], ACT.Copy)
                        last.then_inc(y_kept.sem, 1)

                    for i in range(batches):
                        weave = woven(i)
                        for e, (name, keeper) in enumerate(exchanges(i)):
                            for h in range(2):
                                if keeper == "S":
                                    eng.wait_ge(product[h].sem, product[h].base + product_at[-1] * ft + product_at[i] + e + 1)
                                    keep(name, h, i)
                            if e in weave and weave[e][0] == "u" and weave[e][1] >= first_x:
                                keep_y(weave[e][1])
                    for c in range(chunks - per_batch, chunks):
                        keep_y(c)
                    eng.wait_ge(centred.sem, centred.base + ft + 1)
                    nc.scalar.activation(SQ[:, 0:SEQ], YS[:, 1, :], ACT.Square).then_inc(csq.sem, 1)
                    eng.wait_ge(ginv.sem, ginv.base + ft + 1)
                    nc.scalar.activation(VAR[:, 0:SEQ], VAR[:, 0:SEQ], ACT.Sqrt).then_inc(groot.sem, 1)

            @block.gpsimd
            def _(pool):
                with pool.Fori(0, DT) as ft:
                    for i in range(batches):
                        for l, n in enumerate(LEVELS):
                            for h in range(2):
                                if l < 2:
                                    pool.wait_ge(kept["V"][h].sem, kept["V"][h].base + total_keeps["V"] * ft
                                                 + keeps("V", i, 1))
                                else:
                                    e = [x for x, _ in exchanges(i)].index(f"z{LEVELS[l - 2]}")
                                    pool.wait_ge(product[h].sem, product[h].base + product_at[-1] * ft + product_at[i] + e + 1)
                                nc.gpsimd.tensor_tensor(over_tiles(LT[:, h, l % 2, :]), over_tiles(MT[:, h, :]), mask(n),
                                                        ALU.mult).then_inc(masked[h].sem, 1)

            @block.vector
            def _(dve):
                with dve.Fori(0, DT) as ft:
                    chain = Chain(dve, steps, steps.base + VSTEPS * ft)
                    tt, ts, stt = nc.vector.tensor_tensor, nc.vector.tensor_scalar, nc.vector.scalar_tensor_tensor
                    dve.wait_ge(loaded.sem, loaded.base + 80 * (ft + 1))
                    ts(KK[:, :], K[:, :], col(par["kk"], ft), None, ALU.mult).then_inc(normed.sem, 1)
                    nc.vector.memset(S[:, :, :, :], 0.0).then_inc(zeroed.sem, 1)
                    for d in range(2):
                        dve.wait_ge(acted.sem, acted.base + 4 * ft + d + 1)
                        chain(ts(LW[:, d, :], LW[:, d, :], -DECAY_SCALE, None, ALU.mult))
                        chain(nc.vector.tensor_tensor_scan(INC[:, d, :], masks["resets"], LW[:, d, :], 0.0,
                                                           ALU.mult, ALU.add))
                        if d == 0:
                            tt(EXC[:, d, :], INC[:, d, :], LW[:, d, :], ALU.subtract).then_inc(expo.sem, 1)
                            dve.wait_ge(expo.sem, expo.base + 2 * ft + 1)
                        else:
                            by_chunk = INC[:, d, :].rearrange("p (c t) -> p c t", t=CHUNK)
                            whole = by_chunk[:, :, CHUNK - 1:CHUNK].to_broadcast([P, chunks, CHUNK])
                            chain(tt(EXC[:, d, :].rearrange("p (c t) -> p c t", t=CHUNK), whole, by_chunk, ALU.subtract))
                            tt(INC[:, d, :], EXC[:, d, :], LW[:, d, :], ALU.add).then_inc(expo.sem, 1)
                            dve.wait_ge(expo.sem, expo.base + 2 * ft + 2)
                    dve.wait_ge(ps_sum.sem, ps_sum.base + ft + 1)
                    chain(ts(halves(VAR[:, :]), ps[:, 0:2, 0:T0 // 2], 1e-24, None, ALU.max))
                    nc.vector.reciprocal(VAR[:, :], VAR[:, :]).then_inc(ps_inv.sem, 1)
                    dve.wait_ge(ps_root.sem, ps_root.base + ft + 1)
                    tt(KK[:, :], KK[:, :], VAR[:, :], ALU.mult).then_inc(normed.sem, 1)
                    dve.wait_ge(normed.sem, normed.base + 2 * ft + 2)
                    for d in range(2):
                        dve.wait_ge(acted.sem, acted.base + 4 * ft + 3 + d)
                        chain(ts(KD[:, d, :], A[:, d, :], -1.0, col(par["ka"], ft), ALU.add, ALU.mult))
                        chain(stt(KD[:, d, :], KD[:, d, :], 1.0, K[:, :], ALU.add, ALU.mult))
                        chain(tt(A[:, d, :], A[:, d, :], KK[:, :], ALU.mult))
                    chain(tt(KSUM[:, :], KD[:, 0, 0:SEQ], KD[:, 1, 0:SEQ], ALU.add))
                    for d in range(2):
                        dve.wait_ge(powers.sem, powers.base + 2 * ft + d + 1)
                        chain(tt(KD[:, d, :], KD[:, d, :], PINV[:, d, :], ALU.mult))
                        chain(tt(A[:, d, :], A[:, d, :], PINV[:, d, :], ALU.mult))
                        chain(tt(PINC[:, d, :], PINC[:, d, :], R[:, :], ALU.mult))
                        last = tt(EXC[:, d, :], EXC[:, d, :], KK[:, :], ALU.mult)
                        if d == 0:
                            chain(last)
                    last.then_inc(tilde.sem, 1)
                    chain(tt(KSUM[:, :], KSUM[:, :], R[:, :], ALU.mult))
                    ts(BON[:, :], KSUM[:, :], col(par["rk"], ft), None, ALU.mult).then_inc(bonus_in.sem, 1)

                    def keep(name, h, i):
                        ba, bb = 2 * h, 2 * h + 1
                        if name == "gram":
                            chain(tt(over_tiles(MT[:, h, :]), over_tiles(ps[:, ba, :]), mask("strict"), ALU.mult))
                            chain(tt(over_tiles(XT[:, h, :]), over_tiles(MT[:, h, :]), mask("minus_first_t"), ALU.mult))
                            chain(tt(over_tiles(XT[:, h, :]), over_tiles(XT[:, h, :]), mask("ident"), ALU.add))
                            last = tt(over_tiles(MK[:, h, :]), over_tiles(ps[:, bb, :]), mask("strict"), ALU.mult)
                        elif name == "read":
                            n = 2 * i - CTX // P
                            for dst_, bank in ((GA, ba), (GK, bb)):
                                last = tt(dst_[:, h, n:n + 2, :, :].rearrange("p j d c -> p j (d c)"),
                                          over_tiles(ps[:, bank, :]), mask("inclusive"), ALU.mult)
                        elif name == f"w{LEVELS[-1]}":
                            last = tt(XT[:, h, :], XT[:, h, :], ps[:, bb, :], ALU.subtract)
                        elif name[0] == "w":
                            last = tt(X[:, h, :], X[:, h, :], ps[:, bb, :], ALU.subtract)
                        else:
                            last = nc.vector.tensor_copy(MKV[:, h, :], ps[:, bb, 0:4 * HEAD])
                        last.then_inc(kept["V"][h].sem, 1)

                    def step_u(c):
                        dve.wait_ge(u_done.sem, u_done.base + chunks * ft + c + 1)
                        if c % per_batch == 0:
                            for h in range(2):
                                dve.wait_ge(kept["S"][h].sem, kept["S"][h].base + total_keeps["S"] * ft
                                            + keeps("S", c // per_batch, len(exchanges(c // per_batch))))
                        for d in range(2):
                            ch = chunk_at[d][c]
                            rows = slice(ch % 2 * HEAD, ch % 2 * HEAD + HEAD)
                            last = tt(U[rows, d, c // 2, :], ps[rows, 4, d * P:(d + 1) * P], UX[rows, d, c // 2, :], ALU.add)
                        last.then_inc(u_kept.sem, 1)
                        if c < chunks - 1:
                            for d in range(2):
                                last = ts(SP[:, d, :], S[:, c % 2, d, :], PC[:, d, chunk_at[d][c]:chunk_at[d][c] + 1],
                                          None, ALU.mult)
                            chain(last)

                    def step_s(c):
                        dve.wait_ge(s_done.sem, s_done.base + (chunks - 1) * ft + c + 1)
                        for d in range(2):
                            for h in range(2):
                                own = slice(h * HEAD, (h + 1) * HEAD)
                                last = stt(S[own, 1 - c % 2, d, own], ps[own, 5 + d, own],
                                           PC[own, d, chunk_at[d][c]:chunk_at[d][c] + 1], SP[own, d, own],
                                           ALU.mult, ALU.add)
                        last.then_inc(s_kept.sem, 1)
                        dve.wait_ge(s_kept.sem, s_kept.base + (chunks - 1) * ft + c + 1)

                    for i in range(batches):
                        weave = woven(i)
                        for e, (name, keeper) in enumerate(exchanges(i)):
                            for h in range(2):
                                if keeper == "V":
                                    dve.wait_ge(product[h].sem, product[h].base + product_at[-1] * ft + product_at[i] + e + 1)
                                    keep(name, h, i)
                            if e in weave:
                                part, c = weave[e]
                                step_u(c) if part == "u" else step_s(c)
                    for c in range(chunks - per_batch, chunks):
                        step_u(c)
                        if c < chunks - 1:
                            step_s(c)
                    dve.wait_ge(intra.sem, intra.base + ft + 1)
                    dve.wait_ge(y_kept.sem, y_kept.base + (chunks - first_x) * (ft + 1))
                    chain(tt(YS[:, 0, :], YS[:, 0, :], YS[:, 1, :], ALU.add))
                    tt(YS[:, 0, :], ps[:, 0, :], YS[:, 0, :], ALU.add).then_inc(summed.sem, 1)
                    dve.wait_ge(mean.sem, mean.base + ft + 1)
                    dve.wait_ge(summed.sem, summed.base + ft + 1)
                    tt(YS[:, 1, :], YS[:, 0, :], ps[:, 1, :], ALU.subtract).then_inc(centred.sem, 1)
                    dve.wait_ge(var.sem, var.base + ft + 1)
                    chain(ts(VAR[:, 0:SEQ], ps[:, 2, :], GN_EPS, None, ALU.add))
                    nc.vector.reciprocal(VAR[:, 0:SEQ], VAR[:, 0:SEQ]).then_inc(ginv.sem, 1)
                    dve.wait_ge(groot.sem, groot.base + ft + 1)
                    dve.wait_ge(centred.sem, centred.base + ft + 1)
                    chain(stt(YS[:, 0, :], YS[:, 1, :], col(par["lng"], ft), VAR[:, 0:SEQ], ALU.mult, ALU.mult))
                    dve.wait_ge(bonus.sem, bonus.base + ft + 1)
                    chain(tt(BON[:, :], ps[:, 3, :], V[:, 0:SEQ], ALU.mult))
                    chain(stt(YS[:, 0, :], YS[:, 0, :], col(par["lnb"], ft), BON[:, :], ALU.add, ALU.add))
                    tt(tile(dst, ft), YS[:, 0, :], G[:, :], ALU.mult).then_inc(pair_done.sem, 1)
                    assert chain.steps == VSTEPS, chain.steps



COLUMNS = (
    ("ada_b0", 48), ("ada_b1", 48), ("b_ada_2", 48), ("norm_g", 2 * 4 * DT), ("ev_pool_scale", 4),
    ("rw_mu", 6 * DT), ("rw_w0", 2 * DT), ("rw_a0", 2 * DT), ("rw_kk", DT), ("rw_ka", DT), ("rw_rk", DT),
    ("rw_lng", DT), ("rw_lnb", DT), ("g_mix", DT), ("g_q_lat", 4), ("g_kv_lat", 2), ("g_q_head", 1),
    ("g_k_head", 1), ("g_dil_q", 1), ("g_dil_k", 1), ("g_ffn", DT), ("taps", 3 * 2 * FT2), ("b_conv", 2 * FT2),
)
CONSTANTS = (
    ("ident", P), ("ones", P), ("head_sum", P), ("head_mean", P), ("mla_mean", MLA_QK), ("mla_rotate", MLA_QK),
    ("dil_rotate", P), ("freqs", 2),
)
WKV_MASKS = ("strict", "inclusive", "minus_first_t", "ident") + LEVELS


def offsets(table):
    at, out = 0, {}
    for name, n in table:
        out[name] = (at, at + n)
        at += n
    return out, at


def load_all(core, pairs):
    landed = counter(core, "input_landed")
    with core.block() as block:
        @block.sync
        def _(sp):
            for dst, src in pairs:
                sp.dma_start(dst, src).then_inc(landed.sem, 16)
            sp.wait_ge(landed.sem, landed.base + 16 * len(pairs))
    landed.base += 16 * len(pairs)


def silu_rows(core, rows):
    nc = core.nc
    sigmoid, done = counter(core, "silu_sigmoid"), counter(core, "silu_done")
    with ExitStack() as scope:
        s = core.sb(scope, "silu_s", [P, len(rows), D])
        with core.block() as block:
            @block.scalar
            def _(eng):
                for n, row in enumerate(rows):
                    nc.scalar.activation(s[:, n, :], row, ACT.Sigmoid).then_inc(sigmoid.sem, 1)

            @block.vector
            def _(dve):
                for n, row in enumerate(rows):
                    dve.wait_ge(sigmoid.sem, sigmoid.base + n + 1)
                    nc.vector.tensor_tensor(row, row, s[:, n, :], ALU.mult).then_inc(done.sem, 1)
    sigmoid.base += len(rows)
    done.base += len(rows)


def gains(core, jobs):
    nc = core.nc
    done = counter(core, "gain_done")
    with core.block() as block:
        @block.vector
        def _(dve):
            for out, scale, gain, plus in jobs:
                nc.vector.scalar_tensor_tensor(out, scale, plus, gain, ALU.add, ALU.mult).then_inc(done.sem, 1)
    done.base += len(jobs)


def even_heads(core, q, k, v, queries, q0, out, bias_tile=None, bias_dram=None):
    heads = []
    ctx_tile = SEQ // P
    for h in range(8):
        rows = slice(h % 2 * HEAD, h % 2 * HEAD + HEAD)
        t = h // 2
        ctx_keys = k[rows, t, SEQ:T0]
        cols = slice(h * HEAD, (h + 1) * HEAD)
        if bias_tile is None:
            heads.append(Head(q[rows, t, q0:q0 + queries], queries, [ctx_keys],
                              lambda kt, cols=cols: v[:, ctx_tile + kt, cols],
                              Rows(out[rows, t, q0:q0 + queries], rows.start), HEAD ** -0.5))
        else:
            heads.append(Head(q[rows, t, q0:q0 + queries], queries, [k[rows, t, 0:SEQ], ctx_keys],
                              lambda kt, cols=cols: v[:, kt, cols],
                              Rows(out[rows, t, q0:q0 + queries], rows.start), HEAD ** -0.5,
                              bias=lambda i, h=h: bias_tile[:, h % 2, (6 - 2 * i) * GRID_W:(14 - 2 * i) * GRID_W],
                              bias_load=bias_dram[h, :, :]))
    return heads


def build(nc, io, stop=None):
    core = Core(nc)
    col_at, n_cols = offsets(COLUMNS)
    con_at, n_cons = offsets(CONSTANTS)
    scope = ExitStack()
    with scope:
        cols = core.sb(scope, "columns", [P, n_cols])
        cons = core.sb(scope, "constants", [P, n_cons])
        X = core.sb(scope, "residual", [P, DT, T0])
        mods = {name: core.sb(scope, f"mod_{name}", [P, N_MOD * DT]) for name in ("0x", "0c", "1x", "1c", "2x")}
        derived = core.sb(scope, "derived_gains", [P, 15, DT])

        def column(name, a=0, n=None):
            lo, hi = col_at[name]
            return cols[:, lo + a:hi if n is None else lo + a + n]

        def const(name):
            lo, hi = con_at[name]
            return cons[:, lo:hi]

        core.ident, core.ones = const("ident"), const("ones")
        core.head_sum, core.head_mean = const("head_sum"), const("head_mean")

        credit = [counter(core, n) for n in ("panel_done", "panel_evicted", "mod_tile_used", "gate_done", "pair_done",
                                           "weights_split", "chunk_done", "hidden_low",
                                           "panel_stored_0", "panel_stored_1",
                                           "triangle_kept_0", "triangle_kept_1", "factor_kept_0", "factor_kept_1")]
        with core.block() as block:
            @block.vector
            def _(dve):
                for i, s in enumerate(credit):
                    nc.vector.memset(derived[:, i, :], 0.0).then_inc(s.sem, CREDIT)
        for s in credit:
            s.base += CREDIT

        load_all(core, [(cols[:, :], io["columns"]), (cons[:, :], io["constants"]),
                        (X[:, :, 0:SEQ], io["x"].rearrange("(k p) t -> p k t", p=P)),
                        (X[:, :, SEQ:T0], io["ctx"].rearrange("(k p) t -> p k t", p=P))])

        rows_scope = ExitStack()
        rows = core.sb(rows_scope, "conditions", [P, 2, D])
        load_all(core, [(rows[:, n, :], io[name].to_broadcast([P, D]))
                        for n, name in enumerate(("c", "c_ctx"))])
        silu_rows(core, [rows[:, n, :] for n in range(2)])
        c, cc = rows[:, 0, :], rows[:, 1, :]
        mods0 = (column("ada_b0"), [c, cc], [mods["0x"], mods["0c"]])
        mods1 = (column("ada_b1"), [c, cc], [mods["1x"], mods["1c"]])
        modulation(core, io["ada01"], 0, 2 * DT, *mods0)

        def mod(which, n):
            return mods[which][:, n * DT:(n + 1) * DT]

        def norm_g(layer, n):
            return column("norm_g", (4 * layer + n) * DT, DT)

        at = {}

        def derive(*jobs):
            todo = []
            for key, which, n, gain, plus in jobs:
                at[key] = derived[:, len(at), :]
                todo.append((at[key], mod(which, n), gain, plus))
            gains(core, todo)

        derive(("0x in", "0x", 1, norm_g(0, 0), 1.0), ("0c in", "0c", 1, norm_g(0, 0), 1.0))

        def both(key):
            return [(0, SEQ, at[f"0x {key}"]), (SEQ, T0, at[f"0c {key}"])]

        def evict_copy(dst):
            return lambda n, psum: nc.scalar.activation(
                halves(tile(dst, n)) if dst.shape[-1] == T0 else tile(dst, n), psum, ACT.Copy)

        def mlp(w1, w2, tokens, act, out, group, chunks):
            with ExitStack() as s3:
                hidden = Split(core, s3, "hidden", [P, group, tokens])

                def add(n, psum):
                    o = halves(tile(out, n)) if tokens > 512 else tile(out, n)
                    return nc.vector.tensor_tensor(o, psum, o, ALU.add)

                squared = core.sb(s3, "squared", [P, tokens])
                phases = []
                for g in range(D_FF // P // group):
                    phases += [Phase(w1[g * group:(g + 1) * group, :, :], DT, 1, group, act,
                                     SquaredRelu(core, hidden, tokens, squared)),
                               Phase(w2, group // chunks, chunks, DT, hidden,
                                     ScalarEviction(core, evict_copy(out)) if g == 0 else VectorEviction(core, add),
                                     k_first=g * group)]
                gemm_split(core, phases, tokens)

        def finished(name):
            if stop != name:
                return False
            store(core, X[:, :, 0:SEQ], io["out"])
            return True

        with ExitStack() as s:
            H = core.sb(s, "h", [P, DT, T0])
            rms_stage(core, X, DT, T0, both("in"), [(0, SEQ, mod("0x", 0)), (SEQ, T0, mod("0c", 0))], H)
            with ExitStack() as s2:
                U = core.sb(s2, "u", [P, 12, T0])
                V = core.sb(s2, "v", [P, T0 // P, 512])
                CAT = core.sb(s2, "mixed", [P, DT, T0])
                with ExitStack() as s3:
                    m = Modulation(core, s3, io["ada01"], 2)

                    def vector(dve):
                        m.vector(dve, 2 * DT, 3 * DT, *mods0)
                        m.vector(dve, 0, 3 * DT, *mods1)

                    gemm(core, io["w_in"], DT, 12, H, T0, act_evict=evict_copy(U), bufs=2, vector_also=vector,
                         load_also=lambda sp, n, u: [m.load(sp, n * 4 + t + 2 * DT, n * 4 + t, t % 2) for t in range(4)])
                gemm_tokens(core, io["w_in_v"], DT, H, T0 // P, V)
                with ExitStack() as s3:
                    inv = core.sb(s3, "inverse_counts", [P, len(POOL_WINDOWS), T0])
                    load_all(core, [(inv[:, :, :], io["inv_count"].unsqueeze(0).to_broadcast([P, len(POOL_WINDOWS), T0]))])
                    pool_mixer(core, U, io["pool_w"], inv, column("ev_pool_scale"), CAT)
                with ExitStack() as s3:
                    bias = core.sb(s3, "grid_bias", [P, 2, 14 * GRID_W])
                    grid_mask = core.sb(s3, "grid_mask", [P, GRID_W])
                    load_all(core, [(grid_mask[:, :], io["grid_mask"])])
                    q, k = U[:, 4:8, :], U[:, 8:12, :]
                    attention(core, even_heads(core, q, k, V, SEQ, 0, CAT[:, 4:8, :], bias, io["bias"]), bias,
                              grid_mask[:, :].unsqueeze(1).to_broadcast([P, 14, GRID_W]))
                    attention(core, even_heads(core, q, k, V, CTX, SEQ, CAT[:, 4:8, :]))
                with ExitStack() as s3:
                    m = Modulation(core, s3, io["ada01"], 2)

                    def vector(dve):
                        m.vector(dve, 5 * DT, DT, *mods0)
                        m.vector(dve, 3 * DT, 3 * DT, *mods1)

                    gemm(core, io["w_out"], DT, DT, CAT, T0, act_evict=evict_copy(H), bufs=2, vector_also=vector,
                         load_also=lambda sp, n, u: [m.load(sp, n * 4 + t + 8 * DT, n * 4 + t, t % 2) for t in range(4)])
            derive(("0x mix", "0x", 2, norm_g(0, 1), 0.0), ("0c mix", "0c", 2, norm_g(0, 1), 0.0),
                   ("0x mlp", "0x", 4, norm_g(0, 2), 1.0), ("0c mlp", "0c", 4, norm_g(0, 2), 1.0),
                   ("0x out", "0x", 5, norm_g(0, 3), 0.0), ("0c out", "0c", 5, norm_g(0, 3), 0.0))
            rms_stage(core, H, DT, T0, both("mix"), residual=X)
            if finished("mix0"):
                return
            with ExitStack() as s2:
                A = Split(core, s2, "mlp_in", [P, DT, T0])
                rms_stage(core, X, DT, T0, both("mlp"), [(0, SEQ, mod("0x", 3)), (SEQ, T0, mod("0c", 3))], A)
                mlp(io["mlp_w1_0"], io["mlp_w2_0"], T0, A, H, DT, 1)
            rms_stage(core, H, DT, T0, both("out"), residual=X)
        rows_scope.close()
        derive(("1x in", "1x", 1, norm_g(1, 0), 1.0), ("1c in", "1c", 1, norm_g(1, 0), 1.0),
               ("1x mix", "1x", 2, norm_g(1, 1), 0.0), ("1x mlp", "1x", 4, norm_g(1, 2), 1.0),
               ("1x out", "1x", 5, norm_g(1, 3), 0.0))
        if finished("layer0"):
            return

        names = ("k", "v", "r", "g")
        dram = {n: nc.dram_tensor(f"spilled_{n}", [DT, P, T0 if n in "kv" else SEQ], F32, kind="Internal").ap()
                for n in names}
        with ExitStack() as s0:
            LA = core.sb(s0, "lora_inputs", [P, 2, T0])
            ZT = core.sb(s0, "wkv_out", [P, DT, SEQ])
            segs = ((0, SEQ), (SEQ, T0))
            with ExitStack() as s:
                H = core.sb(s, "h", [P, DT, T0])
                M = [core.sb(s, f"mixed_tokens_{n}", [P, DT, T0]) for n in range(2)]
                DIFF = core.sb(s, "neighbour_difference", [P, DT, T0])
                rms_stage(core, X, DT, T0, [(0, SEQ, at["1x in"]), (SEQ, T0, at["1c in"])],
                          [(0, SEQ, mod("1x", 0)), (SEQ, T0, mod("1c", 0))], H)
                mu = [column("rw_mu", j * DT, DT) for j in range(6)]
                neighbour_difference(core, H, segs, DIFF, lambda dve: token_mix(core, dve, H, DIFF, mu[0], M[0]))

                row = core.sb(s, "condition", [P, 1, D])
                load_all(core, [(row[:, 0, :], io["c_2"].to_broadcast([P, D]))])
                silu_rows(core, [row[:, 0, :]])

                def mixing(j, dst):
                    return lambda dve: token_mix(core, dve, H, DIFF, mu[j], dst)

                def mixed_product(name, src, j, dst, first):
                    with ExitStack() as s2:
                        m = Modulation(core, s2, io["ada2"], 2)

                        def vector(dve):
                            token_mix(core, dve, H, DIFF, mu[j], dst)
                            m.vector(dve, first, 2 * DT, column("b_ada_2"), [row[:, 0, :]], [mods["2x"]])

                        gemm(core, io[f"rw_w{name}"], DT, DT, src, src.shape[-1], store=dram[name], vector_also=vector,
                             load_also=lambda sp, n, u: [m.load(sp, n * 2 + t + first, n * 2 + t, t) for t in range(2)])

                mixed_product("r", M[0][:, :, 0:SEQ], 2, M[1], 0)
                mixed_product("k", M[1], 3, M[0], 2 * DT)
                mixed_product("v", M[0], 1, M[1], 4 * DT)
                gemm(core, io["rw_w1"], DT, 1, M[1], T0, vector_also=mixing(4, M[0]),
                     act_evict=lambda n, psum: nc.scalar.activation(halves(LA[:, 0, :]), psum, ACT.Tanh))
                gemm(core, io["rw_a1"], DT, 1, M[0], T0, vector_also=mixing(5, M[1]),
                     act_evict=lambda n, psum: nc.scalar.activation(halves(LA[:, 1, :]), psum, ACT.Copy))
                gemm(core, io["rw_g1"], DT, 1, M[1][:, :, 0:SEQ], SEQ, act_evict=lambda n, psum: nc.scalar.activation(
                    M[0][:, 0, 0:SEQ], psum, ACT.Sigmoid))
                gemm(core, io["rw_g2"], 1, DT, M[0][:, 0:1, 0:SEQ], SEQ, store=dram["g"])
            with ExitStack() as s:
                tall = core.sb(s, "wkv_masks", [P, len(WKV_MASKS), 2 * P])
                resets = core.sb(s, "wkv_resets", [P, T0])
                load_all(core, [(tall[:, :, :], io["wkv_masks"]),
                                (resets[:, :], io["wkv_resets"].to_broadcast([P, T0]))])
                masks = {name: tall[:, i, :] for i, name in enumerate(WKV_MASKS)}
                masks["resets"] = resets[:, :]
                par = {"w0": [column("rw_w0", d * DT, DT) for d in range(2)],
                       "a0": [column("rw_a0", d * DT, DT) for d in range(2)],
                       "kk": column("rw_kk"), "ka": column("rw_ka"), "rk": column("rw_rk"),
                       "lng": column("rw_lng"), "lnb": column("rw_lnb")}
                wkv(core, LA[:, 0, :], LA[:, 1, :], io["lora_up"], dram["k"], dram["v"], dram["r"], dram["g"], par,
                    masks, ZT)
            with ExitStack() as s:
                H = core.sb(s, "h", [P, DT, SEQ])
                gemm(core, io["rw_wo"], DT, DT, ZT, SEQ, act_evict=evict_copy(H))
                if stop == "wo1":
                    store(core, H[:, :, 0:SEQ], io["out"])
                    return
                rms_stage(core, H, DT, SEQ, [(0, SEQ, at["1x mix"])], residual=X)
                if finished("mix1"):
                    return
                with ExitStack() as s2:
                    A = Split(core, s2, "mlp_in", [P, DT, SEQ])
                    rms_stage(core, X, DT, SEQ, [(0, SEQ, at["1x mlp"])], [(0, SEQ, mod("1x", 3))], A)
                    mlp(io["mlp_w1_1"], io["mlp_w2_1"], SEQ, A, H, 2 * DT, 2)
                rms_stage(core, H, DT, SEQ, [(0, SEQ, at["1x out"])], residual=X)
        if finished("layer1"):
            return

        derive(("2x in", "2x", 1, column("g_mix"), 1.0), ("2x mlp", "2x", 4, column("g_ffn"), 1.0))
        with ExitStack() as s:
            H = core.sb(s, "h", [P, DT, SEQ])
            MIX = core.sb(s, "mix", [P, DT, SEQ])
            rms_stage(core, X, DT, SEQ, [(0, SEQ, at["2x in"])], [(0, SEQ, mod("2x", 0))], H)
            cs = core.sb(s, "rotation", [P, 2, 2, SEQ])
            rotation_tables(core, io["positions"], const("freqs"),
                            [(cs[:, 0, 0, :], cs[:, 0, 1, :]), (cs[:, 1, 0, :], cs[:, 1, 1, :])])
            with ExitStack() as s2:
                LAT = core.sb(s2, "latents", [P, 6, SEQ])
                QM, KM = core.sb(s2, "q_mla", [P, 8, SEQ]), core.sb(s2, "k_mla", [P, 8, SEQ])
                VM = core.sb(s2, "v_mla", [P, SEQ // P, 512])
                mask = core.sb(s2, "causal_bias", [P, 2, 512])
                load_all(core, [(mask[:, :, :], io["causal_bias"])])
                gemm(core, io["w_lat"], DT, 6, H, SEQ, act_evict=evict_copy(LAT))
                rows = slice(MLA_NOPE, MLA_QK)
                gemm(core, io["w_kpe"], DT, 1, H, SEQ, m=MLA_ROPE, m0=MLA_NOPE, act_evict=lambda n, psum:
                     nc.scalar.activation(KM[rows, :, :], psum.unsqueeze(1).to_broadcast([MLA_ROPE, 8, SEQ]), ACT.Copy))
                rms_stage(core, LAT[:, 0:4, :], 4, SEQ, [(0, SEQ, column("g_q_lat"))], dst=LAT[:, 0:4, :])
                rms_stage(core, LAT[:, 4:6, :], 2, SEQ, [(0, SEQ, column("g_kv_lat"))], dst=LAT[:, 4:6, :])
                gemm(core, io["w_q_b"], 4, 8, LAT[:, 0:4, :], SEQ, m=MLA_QK, act_evict=evict_copy(QM[0:MLA_QK, :, :]))
                gemm(core, io["w_kv_b"], 2, 8, LAT[:, 4:6, :], SEQ, m=MLA_NOPE,
                     act_evict=evict_copy(KM[0:MLA_NOPE, :, :]))
                gemm_tokens(core, io["w_kv_v"], 2, LAT[:, 4:6, :], SEQ // P, VM)
                q96 = slice(0, MLA_QK)
                for t, g in ((QM, "g_q_head"), (KM, "g_k_head")):
                    head_norm(core, t, MLA_QK, 8, const("mla_mean")[q96, :], column(g)[q96, :],
                              const("mla_rotate")[q96, :], cs[q96, 0, 0, :], cs[q96, 0, 1, :])
                attention(core, [Head(QM[0:MLA_QK, h, :], SEQ, [KM[0:MLA_QK, h, :]],
                                      lambda kt, h=h: VM[:, kt, h * HEAD:(h + 1) * HEAD],
                                      Rows(MIX[h % 2 * HEAD:h % 2 * HEAD + HEAD, h // 2, :], h % 2 * HEAD),
                                      MLA_QK ** -0.5, bias=lambda i: mask[:, 0, (3 - i) * P:512], causal=True)
                                 for h in range(8)])
                QD, KD = QM[:, 0:4, :], KM[:, 0:4, :]
                gemm(core, io["w_qd"], DT, 4, H, SEQ, act_evict=evict_copy(QD))
                gemm(core, io["w_kd"], DT, 4, H, SEQ, act_evict=evict_copy(KD))
                gemm_tokens(core, io["w_vd"], DT, H, SEQ // P, VM)
                for t, g in ((QD, "g_dil_q"), (KD, "g_dil_k")):
                    head_norm(core, t, P, 4, const("head_mean"), column(g), const("dil_rotate"),
                              cs[:, 1, 0, :], cs[:, 1, 1, :])
                attention(core, [Head(QD[h % 2 * HEAD:h % 2 * HEAD + HEAD, h // 2, :], SEQ,
                                      [KD[h % 2 * HEAD:h % 2 * HEAD + HEAD, h // 2, :]],
                                      lambda kt, h=h: VM[:, kt, h * HEAD:(h + 1) * HEAD],
                                      Rows(MIX[h % 2 * HEAD:h % 2 * HEAD + HEAD, 4 + h // 2, :], h % 2 * HEAD),
                                      HEAD ** -0.5, bias=lambda i: mask[:, 1, (3 - i) * P:512], causal=True)
                                 for h in range(8)])
            gate1, gate2 = mod("2x", 2), mod("2x", 5)
            gemm(core, io["w_o"], DT, DT, MIX, SEQ, dve_evict=lambda n, psum, chain: nc.vector.scalar_tensor_tensor(
                tile(X, n)[:, 0:SEQ], psum, col(gate1, n), tile(X, n)[:, 0:SEQ], ALU.mult, ALU.add))
            if finished("mix2"):
                return
        with ExitStack() as s:
            G = Split(core, s, "gated", [P, FT2, SEQ])
            with ExitStack() as s2:
                A = Split(core, s2, "mlp_in", [P, DT, SEQ])
                rms_stage(core, X, DT, SEQ, [(0, SEQ, at["2x mlp"])], [(0, SEQ, mod("2x", 3))], A)
                taps = column("taps").rearrange("p (j n) -> p j n", j=3)
                gemm_split(core, [Phase(io["w_up"], DT, 1, 2 * FT2, A,
                                        ConvolvedGate(core, s2, taps, column("b_conv"), G))], SEQ)
            gemm_split(core, [Phase(io["w_down"], FT2 // 2, 2, DT, G, VectorEviction(
                core, lambda n, psum: nc.vector.scalar_tensor_tensor(
                    tile(X, n)[:, 0:SEQ], psum, col(gate2, n), tile(X, n)[:, 0:SEQ], ALU.mult, ALU.add)))], SEQ)
        store(core, X[:, :, 0:SEQ], io["out"])


def store(core, src, out):
    stored = counter(core, "output_stored")
    with core.block() as block:
        @block.sync
        def _(sp):
            sp.dma_start(out.rearrange("(k p) t -> p k t", p=P), src).then_inc(stored.sem, 16)
            sp.wait_ge(stored.sem, stored.base + 16)
    stored.base += 16



def panels(w, m=P):
    k, n = w.shape
    return w.reshape(k // P, P, n // m, m).transpose(2, 1, 0, 3).reshape(n // m, P, k // P * m)


def columns(v):
    return v.reshape(-1, P).T


def padded_column(v):
    out = np.zeros((P, 1), v.dtype)
    out[:len(v), 0] = v
    return out


def constants():
    f = np.float32
    out = {"ident": np.eye(P, dtype=f), "ones": np.ones((P, P), f)}
    head = np.kron(np.eye(2, dtype=f), np.ones((HEAD, HEAD), f))
    out["head_sum"], out["head_mean"] = head, head / f(HEAD)
    mean = np.zeros((P, MLA_QK), f)
    mean[:MLA_NOPE, :MLA_NOPE] = 1 / MLA_NOPE
    mean[MLA_NOPE:MLA_QK, MLA_NOPE:] = 1 / MLA_ROPE
    out["mla_mean"] = mean

    def rotate(size, start, n):
        m = np.zeros((P, n), f)
        for j in range(size // 2):
            m[start + j + size // 2, start + j] = -1
            m[start + j, start + j + size // 2] = 1
        return m

    out["mla_rotate"] = rotate(MLA_ROPE, MLA_NOPE, MLA_QK)
    out["dil_rotate"] = rotate(HEAD, 0, P) + rotate(HEAD, HEAD, P)

    def freqs(d):
        half = d // 2
        e = (f(-2.0) * np.arange(half, dtype=f)) / f(d)
        return np.tile(np.power(f(ROPE_THETA), e).astype(f), 2)

    fr = np.zeros((P, 2), f)
    fr[MLA_NOPE:MLA_QK, 0] = freqs(MLA_ROPE)
    fr[:, 1] = np.tile(freqs(HEAD), 2)
    out["freqs"] = fr
    return np.concatenate([out[n] for n, _ in CONSTANTS], axis=1)


def inverse_counts():
    out = np.zeros((len(POOL_WINDOWS), T0), np.float32)
    for g, w in enumerate(POOL_WINDOWS):
        for t0, n in ((0, SEQ), (SEQ, CTX)):
            t = np.arange(n)
            out[g, t0:t0 + n] = 1.0 / (np.clip(t + w // 2, 0, n) - np.clip(t - w // 2, 0, n))
    return out


def grid_columns():
    c = np.arange(GRID_W)
    start = np.clip(c - WIN_C // 2, 0, GRID_W - WIN_C)
    ok = (c[None, :] >= start[:, None]) & (c[None, :] < start[:, None] + WIN_C)
    return np.tile(np.where(ok, 0, NEG).astype(np.float32), (2, 1))


def grid_bias(rpb):
    c = np.arange(GRID_W)
    dc = np.clip(c[None, :] - c[:, None], -(WIN_C - 1), WIN_C - 1) + WIN_C - 1
    full = rpb[:, :, dc].transpose(0, 2, 1, 3)
    return np.concatenate([full[:, :, 1:15], full[:, :, 0:14]], axis=1).reshape(rpb.shape[0], P, 14 * GRID_W)


def causal_biases():
    q = np.arange(P)[:, None]
    k = np.arange(512)[None, :] - 3 * P
    dist = q - k
    causal = np.where(dist >= 0, 0.0, NEG)
    count = sum(((dist >= 0) & (dist % dil == 0) & (dist // dil <= window // dil)).astype(int)
                for window, dil in DIL_PATTERNS)
    dil = np.where(count > 0, np.log(np.maximum(count, 1)), NEG)
    return np.stack([causal, dil], axis=1).astype(np.float32)


def wkv_masks():
    i, j = np.arange(P)[:, None], np.arange(P)[None, :]
    same = i // CHUNK == j // CHUNK

    def level(n):
        return (i // (2 * n) == j // (2 * n)) & (i // n > j // n)

    both = {"strict": (same & (i < j), same & (i > j)), "inclusive": (same & (i <= j), same & (i >= j)),
            "minus_first_t": (-1.0 * level(1).T, -1.0 * level(1)),
            "ident": (i == j, i == j)}
    for n in LEVELS:
        both[n] = (level(n).T, level(n))
    return np.stack([np.concatenate(both[n], axis=1) for n in WKV_MASKS], axis=1).astype(np.float32)


def lay_out(i):
    f = {k: np.asarray(v) for k, v in i.items()}
    win, win2 = f["ev_w_in"][0], f["w_in_2"][0]
    taps = f["w_conv_2"][0].reshape(3, 2, FT2, P).transpose(0, 2, 1, 3).reshape(-1)
    bconv = f["b_conv_2"][0].reshape(2, FT2, P).transpose(1, 0, 2).reshape(-1)
    col = {
        "ada_b0": f["ada_b"][0], "ada_b1": f["ada_b"][1], "b_ada_2": f["b_ada_2"][0], "norm_g": f["norm_g"],
        "ev_pool_scale": f["ev_pool_scale"], "rw_mu": f["rw_mu"], "rw_w0": f["rw_w0"], "rw_a0": f["rw_a0"],
        "rw_kk": f["rw_kk"], "rw_ka": f["rw_ka"], "rw_rk": f["rw_rk"], "rw_lng": f["rw_lng"], "rw_lnb": f["rw_lnb"],
        "g_mix": f["g_mix_norm_2"], "g_q_lat": f["g_q_lat_2"], "g_kv_lat": f["g_kv_lat_2"],
        "g_q_head": np.concatenate([f["g_mla_q_nope_2"][0], f["g_mla_q_pe_2"][0]]),
        "g_k_head": np.concatenate([f["g_mla_k_nope_2"][0], f["g_mla_k_pe_2"][0]]),
        "g_dil_q": np.tile(f["g_dil_q_2"][0], 2), "g_dil_k": np.tile(f["g_dil_k_2"][0], 2), "g_ffn": f["g_ffn_norm_2"],
        "taps": taps, "b_conv": bconv,
    }
    cols = [padded_column(col[n].reshape(-1)) if col[n].size < P else columns(col[n].reshape(-1)) for n, _ in COLUMNS]
    q0 = Q_LORA + KV_LORA
    d0 = q0 + MLA_ROPE
    qb = f["w_q_b_2"][0]
    kvb = f["w_kv_b_2"][0].reshape(KV_LORA, MLA_HEADS, 2 * HEAD)
    up = f["w_up_2"][0].reshape(D, 2, FT2, P).transpose(0, 2, 1, 3).reshape(D, 2 * D_FF2)
    lora_up = np.concatenate([f["rw_w2"][0].reshape(P, DT, P), f["rw_a2"][0].reshape(P, DT, P)], axis=2).transpose(1, 0, 2)
    token_weights = lambda w: w.reshape(-1, P, 512).transpose(1, 0, 2).reshape(P, -1)
    out = {
        "x": f["x"][0].T, "ctx": f["ctx"][0].T, "c": f["c"].reshape(1, D), "c_ctx": f["c_ctx"].reshape(1, D),
        "c_2": f["c_2"].reshape(1, D), "positions": f["positions_2"].reshape(1, SEQ),
        "columns": np.concatenate(cols, axis=1), "constants": constants(),
        "ada01": np.concatenate([f["ada_w"][0].T[:5 * D], f["ada_w"][1].T[:3 * D], f["ada_w"][0].T[5 * D:],
                                 f["ada_w"][1].T[3 * D:]]).reshape(96, P, D),
        "ada2": f["w_ada_2"][0].T.reshape(48, P, D),
        "w_in": panels(win[:, 0:1536]), "w_in_v": token_weights(win[:, 1536:]), "w_out": panels(f["ev_w_out"][0]),
        "pool_w": f["ev_pool_w"][0], "inv_count": inverse_counts(), "grid_mask": grid_columns(),
        "bias": grid_bias(f["ev_rpb"][0]),
        "mlp_w1_0": panels(f["mlp_w1"][0]), "mlp_w2_0": panels(f["mlp_w2"][0]),
        "mlp_w1_1": panels(f["mlp_w1"][1]), "mlp_w2_1": panels(f["mlp_w2"][1]),
        "rw_wr": panels(f["rw_wr"][0]), "rw_wk": panels(f["rw_wk"][0]), "rw_wv": panels(f["rw_wv"][0]),
        "rw_wo": panels(f["rw_wo"][0]),
        "rw_w1": panels(np.concatenate([f["rw_w1"][0, 0], f["rw_w1"][0, 1]], axis=1)),
        "rw_a1": panels(np.concatenate([f["rw_a1"][0, 0], f["rw_a1"][0, 1]], axis=1)),
        "rw_g1": panels(f["rw_g1"][0]), "rw_g2": panels(f["rw_g2"][0]), "lora_up": lora_up,
        "wkv_masks": wkv_masks(), "wkv_resets": (np.arange(T0) % CHUNK != 0).astype(np.float32).reshape(1, T0),
        "w_lat": panels(win2[:, 0:q0]), "w_kpe": panels(win2[:, q0:d0], MLA_ROPE),
        "w_q_b": panels(qb, MLA_QK), "w_kv_b": panels(kvb[:, :, :MLA_NOPE].reshape(KV_LORA, -1), MLA_NOPE),
        "w_kv_v": token_weights(kvb[:, :, MLA_NOPE:].reshape(KV_LORA, -1)),
        "w_qd": panels(win2[:, d0:d0 + 512]), "w_kd": panels(win2[:, d0 + 512:d0 + 1024]),
        "w_vd": token_weights(win2[:, d0 + 1024:]), "causal_bias": causal_biases(),
        "w_o": panels(f["w_o_2"][0]), "w_up": panels(up), "w_down": panels(f["w_down_2"][0]),
    }
    return {k: np.ascontiguousarray(v) for k, v in out.items()}


def kernel(**inputs):
    import concourse.bacc as bacc
    from concourse.bass_utils import run_bass_kernel_spmd

    arrays = lay_out(inputs)
    nc = bacc.Bacc("TRN2", target_bir_lowering=False, num_devices=1)
    io = {n: nc.dram_tensor(f"in_{n}", a.shape, mybir.dt.from_np(a.dtype), kind="ExternalInput").ap()
          for n, a in arrays.items()}
    io["out"] = nc.dram_tensor("out", (D, SEQ), F32, kind="ExternalOutput").ap()
    build(nc, io)
    result = run_bass_kernel_spmd(nc, [{f"in_{n}": a for n, a in arrays.items()}], core_ids=[0])
    return np.ascontiguousarray(result.results[0]["out"].T).reshape(1, SEQ, D)
```
